# Optimizing a Trainium2 kernel written in Bass

```python
import jax, jax.numpy as jnp
from jax import lax
import numpy as np

D_MODEL = 2048
BATCH = 1
SEQ = 1024
DEPTH = 2

CHUNK = 64
N_A_LAYERS = DEPTH // 2
N_B_LAYERS = DEPTH - N_A_LAYERS
RMS_EPS = 1e-6

GLA_HEADS = 4
GLA_DK = (D_MODEL // 2) // GLA_HEADS
GLA_DV = D_MODEL // GLA_HEADS
GLA_QK_W = GLA_HEADS * GLA_DK
GLA_V_W = GLA_HEADS * GLA_DV
GLA_GATE_RANK = 16
GLA_TAU = 16.0
GLA_IN_W = 2 * GLA_QK_W + 2 * GLA_V_W + GLA_GATE_RANK

SWA_Q_HEADS = 32
SWA_KV_HEADS = 4
SWA_GROUP = SWA_Q_HEADS // SWA_KV_HEADS
SWA_HEAD_DIM = D_MODEL // SWA_Q_HEADS
SWA_W = SWA_Q_HEADS * SWA_HEAD_DIM
WINDOW = 128
WINDOW_CHUNKS = WINDOW // CHUNK
NEG_INF = -1e30

kernel_name = "yoco_gla_swa_sink_hybrid"

def _rms_norm(x, gain):
    xf = x.astype(jnp.float32)
    y = xf * lax.rsqrt(jnp.mean(xf * xf, axis=-1, keepdims=True) + RMS_EPS)
    return (y * gain.astype(jnp.float32)).astype(x.dtype)

def _to_chunk_heads(t, n_heads, dh):
    b, s, _ = t.shape
    return t.reshape(b, s // CHUNK, CHUNK, n_heads, dh).transpose(1, 0, 3, 2, 4)

def _gla_layer(x, norm_g, w_in, w_alpha_up, b_alpha, out_norm_g, w_out):
    b, s, _ = x.shape
    f32 = jnp.float32
    h = _rms_norm(x, norm_g)
    proj = jnp.einsum('bsd,de->bse', h, w_in)
    q, k, v, g, a_low = jnp.split(
        proj, [GLA_QK_W, 2 * GLA_QK_W, 2 * GLA_QK_W + GLA_V_W, 2 * GLA_QK_W + 2 * GLA_V_W], axis=-1)
    log_alpha = jax.nn.log_sigmoid(
        (jnp.einsum('bsr,re->bse', a_low, w_alpha_up) + b_alpha).astype(f32)) / GLA_TAU
    q = _to_chunk_heads(q.astype(f32), GLA_HEADS, GLA_DK) * (GLA_DK ** -0.5)
    k = _to_chunk_heads(k.astype(f32), GLA_HEADS, GLA_DK)
    v = _to_chunk_heads(v.astype(f32), GLA_HEADS, GLA_DV)
    la = _to_chunk_heads(log_alpha, GLA_HEADS, GLA_DK)
    cum = jnp.cumsum(la, axis=3)
    total = cum[:, :, :, -1:, :]
    k_dec = k * jnp.exp(total - cum)
    chunk_decay = jnp.exp(total[:, :, :, 0, :])

    def step(state, inp):
        qc, kc, vc, dc = inp
        state = dc[..., None] * state + jnp.einsum('bhck,bhcv->bhkv', kc, vc)
        return state, jnp.einsum('bhck,bhkv->bhcv', qc, state)

    init = jnp.zeros((b, GLA_HEADS, GLA_DK, GLA_DV), f32)
    _, o = lax.scan(step, init, (q, k_dec, v, chunk_decay))
    o = o.transpose(1, 0, 3, 2, 4).reshape(b, s, GLA_HEADS, GLA_DV)
    o = _rms_norm(o, out_norm_g).reshape(b, s, GLA_V_W)
    o = o * jax.nn.silu(g.astype(f32))
    return x + jnp.einsum('bse,ed->bsd', o.astype(x.dtype), w_out)

def _shared_kv(x, kv_norm_g, w_kv, k_norm_g):
    b, s, _ = x.shape
    n = s // CHUNK
    h = _rms_norm(x, kv_norm_g)
    kv = jnp.einsum('bsd,de->bse', h, w_kv)
    k, v = jnp.split(kv, 2, axis=-1)
    k = _rms_norm(k.reshape(b, s, SWA_KV_HEADS, SWA_HEAD_DIM), k_norm_g).astype(jnp.float32)
    v = v.reshape(b, s, SWA_KV_HEADS, SWA_HEAD_DIM).astype(jnp.float32)
    kc = k.reshape(b, n, CHUNK, SWA_KV_HEADS, SWA_HEAD_DIM)
    vc = v.reshape(b, n, CHUNK, SWA_KV_HEADS, SWA_HEAD_DIM)
    pad = lambda t, w: jnp.pad(t, ((0, 0), (w, 0), (0, 0), (0, 0), (0, 0)))[:, :n]
    offs = list(range(WINDOW_CHUNKS - 1, -1, -1))
    k_win = jnp.concatenate([pad(kc, w) for w in offs], axis=2)
    v_win = jnp.concatenate([pad(vc, w) for w in offs], axis=2)
    key_off = jnp.repeat(jnp.arange(WINDOW_CHUNKS - 1, -1, -1), CHUNK)
    valid = jnp.arange(n)[:, None] >= key_off[None, :]
    return k_win, v_win, valid

def _swa_layer(x, norm_g, w_in, q_norm_g, sinks, w_out, k_win, v_win, valid):
    b, s, _ = x.shape
    n = s // CHUNK
    f32 = jnp.float32
    h = _rms_norm(x, norm_g)
    proj = jnp.einsum('bsd,de->bse', h, w_in)
    q, g = jnp.split(proj, [SWA_W], axis=-1)
    q = _rms_norm(q.reshape(b, s, SWA_Q_HEADS, SWA_HEAD_DIM), q_norm_g).astype(f32)
    q = q.reshape(b, n, CHUNK, SWA_KV_HEADS, SWA_GROUP, SWA_HEAD_DIM)
    scores = jnp.einsum('bnckgd,bnwkd->bnkgcw', q, k_win) * (SWA_HEAD_DIM ** -0.5)
    scores = jnp.where(valid[None, :, None, None, None, :], scores, NEG_INF)
    sink = sinks.astype(f32).reshape(SWA_KV_HEADS, SWA_GROUP)[None, None, :, :, None, None]
    m = jnp.maximum(jnp.max(scores, axis=-1, keepdims=True), sink)
    e = jnp.exp(scores - m)
    probs = e / (jnp.sum(e, axis=-1, keepdims=True) + jnp.exp(sink - m))
    o = jnp.einsum('bnkgcw,bnwkd->bnckgd', probs, v_win).reshape(b, s, SWA_W)
    o = o * jax.nn.silu(g.astype(f32))
    return x + jnp.einsum('bse,ed->bsd', o.astype(x.dtype), w_out)

def setup_inputs(seed: int = 0) -> dict:
    key = jax.random.key(seed)
    ks = jax.random.split(key, 16)
    nrm = lambda k, shape, scale: jax.random.normal(k, shape, jnp.float32) * scale
    gain = lambda k, shape: 1.0 + 0.05 * jax.random.normal(k, shape, jnp.float32)
    return {
        "x": nrm(ks[0], (BATCH, SEQ, D_MODEL), 1.0),
        "a_norm": gain(ks[1], (N_A_LAYERS, D_MODEL)),
        "a_w_in": nrm(ks[2], (N_A_LAYERS, D_MODEL, GLA_IN_W), D_MODEL ** -0.5),
        "a_w_alpha_up": nrm(ks[3], (N_A_LAYERS, GLA_GATE_RANK, GLA_QK_W), GLA_GATE_RANK ** -0.5),
        "a_b_alpha": nrm(ks[4], (N_A_LAYERS, GLA_QK_W), 0.1),
        "a_out_norm": gain(ks[5], (N_A_LAYERS, GLA_DV)),
        "a_w_out": nrm(ks[6], (N_A_LAYERS, GLA_V_W, D_MODEL), GLA_V_W ** -0.5),
        "kv_norm": gain(ks[7], (D_MODEL,)),
        "w_kv": nrm(ks[8], (D_MODEL, 2 * SWA_KV_HEADS * SWA_HEAD_DIM), D_MODEL ** -0.5),
        "k_norm": gain(ks[9], (SWA_HEAD_DIM,)),
        "b_norm": gain(ks[10], (N_B_LAYERS, D_MODEL)),
        "b_w_in": nrm(ks[11], (N_B_LAYERS, D_MODEL, 2 * SWA_W), D_MODEL ** -0.5),
        "b_q_norm": gain(ks[12], (N_B_LAYERS, SWA_HEAD_DIM)),
        "b_sinks": nrm(ks[13], (N_B_LAYERS, SWA_Q_HEADS), 0.5),
        "b_w_out": nrm(ks[14], (N_B_LAYERS, SWA_W, D_MODEL), SWA_W ** -0.5),
    }

def reference(x, a_norm, a_w_in, a_w_alpha_up, a_b_alpha, a_out_norm, a_w_out,
              kv_norm, w_kv, k_norm, b_norm, b_w_in, b_q_norm, b_sinks, b_w_out):
    h = x
    k_win = v_win = valid = None
    for layer in range(DEPTH):
        if layer < N_A_LAYERS:
            h = _gla_layer(h, a_norm[layer], a_w_in[layer], a_w_alpha_up[layer],
                           a_b_alpha[layer], a_out_norm[layer], a_w_out[layer])
        else:
            if layer == N_A_LAYERS:
                k_win, v_win, valid = _shared_kv(h, kv_norm, w_kv, k_norm)
            j = layer - N_A_LAYERS
            h = _swa_layer(h, b_norm[j], b_w_in[j], b_q_norm[j], b_sinks[j], b_w_out[j],
                           k_win, v_win, valid)
    return h


_drawn_inputs = setup_inputs


def setup_inputs(seed=0):
    import zlib

    import numpy as np

    out = dict(_drawn_inputs(seed))
    spreads = {}
    factors = {'kv_norm': 8.0, 'k_norm': 8.0, 'b_norm': 8.0, 'b_q_norm': 8.0, 'b_sinks': 8.0}
    for name, (base, spread) in spreads.items():
        noise = np.random.default_rng([zlib.crc32(name.encode()), seed]).standard_normal(out[name].shape)
        drawn = base * np.exp(spread * noise) if base else spread * noise
        out[name] = __import__('jax').numpy.asarray(drawn.astype(out[name].dtype))
    for name, factor in factors.items():
        out[name] = (out[name] * factor).astype(out[name].dtype)
    return out
```

```python
import concourse.bass as bass
from concourse import mybir
from contextlib import ExitStack

F32 = mybir.dt.float32
F32R = mybir.dt.float32r
ALU = mybir.AluOpType
ACT = mybir.ActivationFunctionType
AX = mybir.AxisListType


def trunk_kernel(nc, x, a_norm, a_w_in, a_w_alpha_up, a_b_alpha, a_out_norm, a_w_out,
                 kv_norm, w_kv, k_norm, b_norm, b_w_in, b_q_norm, b_sinks, b_w_out, out):
    P = 128
    SEQ, D = x.shape[1], x.shape[2]
    KT = D // P
    ST = SEQ // P
    HALF = 512
    NH = SEQ // HALF
    UK, BC = 4, 256
    NU = KT // UK
    CT = BC // P
    CHUNK = 64
    GH, DK, DV = 4, 256, 512
    RANK = a_w_alpha_up.shape[1]
    TAU = 16.0
    HD = 64
    KVH = 4
    QCT = 4
    EPS = 1e-6
    NQ, NK_, NV_, NG_ = GH * DK // BC, GH * DK // BC, GH * DV // BC, GH * DV // BC
    KA0 = NQ
    VA0 = KA0 + NK_
    GA0 = VA0 + NV_
    OA0 = GA0 + NG_
    KV0 = OA0 + D // BC
    QB0 = KV0 + 2
    GB0 = QB0 + D // BC
    OB0 = GB0 + D // BC
    END = OB0 + D // BC

    def scratch(name, shape):
        return nc.dram_tensor(name, shape, F32).ap()

    xT_s = scratch("xT_s", [D, SEQ])
    qa_s = scratch("qa_s", [GH * DK, SEQ])
    ka_s = scratch("ka_s", [SEQ, GH * DK])
    va_s = scratch("va_s", [SEQ, GH * DV])
    ga_s = scratch("ga_s", [GH * DV, SEQ])
    x1_s = scratch("x1_s", [D, SEQ])
    kb_s = scratch("kb_s", [KVH * HD, SEQ])
    vb_s = scratch("vb_s", [SEQ, KVH * HD])
    qb_s = scratch("qb_s", [D, SEQ])
    gb_s = scratch("gb_s", [D, SEQ])

    x2d, out2d = x[0], out[0]

    ctx = ExitStack()
    with ctx:
        def sb(name, shape, dt=F32):
            return ctx.enter_context(nc.sbuf_tensor(name, shape, dt))

        def sem(name):
            return ctx.enter_context(nc.semaphore(name))

        XH = sb("XH", [P, KT, SEQ], F32R)
        XL = sb("XL", [P, KT, SEQ], F32R)
        WRAW = sb("WRAW", [P, NU, UK, BC])
        WHI = sb("WHI", [P, 2, UK, BC], F32R)
        WLO = sb("WLO", [P, 2, UK, BC], F32R)
        RSTD = sb("RSTD", [P, SEQ])
        WORK = sb("WORK", [P, 10240])
        ident = sb("ident", [P, P])
        pair = sb("pair", [P, P])
        ones = sb("ones", [P, P])
        NR = 3 * KT + DV // P + GH * DK // P + 2
        vrows = sb("vrows", [NR, P])
        vcols = sb("vcols", [P, NR])
        g_a, g_kv, g_b = (vcols[:, i * KT:(i + 1) * KT] for i in range(3))
        g_o = vcols[:, 3 * KT:3 * KT + DV // P]
        b_al = vcols[:, 3 * KT + DV // P:NR - 2]
        srow = sb("srow", [1, KVH * 8])
        kgain = sb("kgain", [P, 1])
        sinks = sb("sinks", [P, KVH, 4])
        dc = sb("dc", [P, GH * DK // P, SEQ // CHUNK])
        wa = WRAW[:, 3, 0, :].rearrange("p (k r) -> p k r", r=RANK)
        ssq = sb("ssq", [P, ST])
        eps_t = sb("eps_t", [P, 1])
        st1 = sb("st1", [P, 8])
        st2 = sb("st2", [P, 16])

        PS = ctx.enter_context(nc.psum_tensor("PS", [P, 8, 512], F32))

        xin = WORK[:, 0:4 * D].rearrange("p (n d) -> p n d", n=4)
        xraw = WORK[:, 8192:10240].rearrange("p (n k s) -> p n k s", n=4, k=4)
        stageT = WORK[:, 0:2048].rearrange("p (i s) -> p i s", i=CT)
        stageN = WORK[:, 2048:4096].rearrange("p (s c) -> p s c", s=ST)
        reload_ = WORK[:, 2048:4096].rearrange("p (i s) -> p i s", i=CT)
        bufA = WORK[:, 4096:6144].rearrange("p (i s) -> p i s", i=CT)
        bufB = WORK[:, 6144:8192].rearrange("p (i s) -> p i s", i=CT)
        alow = WORK[0:64, 8192:9216]
        wup = WORK[0:64, 9216:9216 + BC]
        sqsum = WORK[:, 8192:9216]
        state = WORK[:, 0:4096].rearrange("p (h i v) -> p h i v", h=GH, i=2)
        gq = WORK[:, 4096:5120].rearrange("p (h i s) -> p h i s", h=GH, i=2)
        gk = WORK[:, 5120:6144].rearrange("p (h k) -> p h k", h=GH)
        gv = WORK[:, 6144:8192].rearrange("p (h v) -> p h v", h=GH)
        gg = WORK[:, 8192:9216].rearrange("p (n i s) -> p n i s", n=2, i=4)
        onrm = WORK[:, 9216:9728]
        ogate = WORK[:, 9728:10240]
        sq_ = WORK[:, 0:2048].rearrange("p (h c i s) -> p h c i s", h=KVH, c=2, i=QCT)
        sg_ = WORK[:, 2048:4096].rearrange("p (h i s) -> p h i s", h=KVH, i=QCT)
        sk_ = WORK[:, 4096:4096 + KVH * 192].rearrange("p (h s) -> p h s", h=KVH)
        sv_ = WORK[:, 4864:4864 + KVH * 2 * HD].rearrange("p (h c d) -> p h c d", h=KVH, c=2)
        ex_ = WORK[:, 5376:5376 + 2 * 516].rearrange("p (n k) -> p n k", n=2)
        pr_ = WORK[:, 6408:6408 + 1024].rearrange("p (n g k) -> p n g k", n=2, g=4)
        pt_ = WORK[:, 7432:7432 + 1024].rearrange("p (n r k) -> p n r k", n=2, r=2)
        so_ = WORK[:, 8456:8456 + 512].rearrange("p (n i s) -> p n i s", n=2, i=QCT)

        v_pe = sem("v_pe")
        v_ok = sem("v_ok")
        consts_in = sem("consts_in")
        zeroed = sem("zeroed")
        x_in = [sem(f"x_in{i}") for i in range(4)]
        x_tr = sem("x_tr")
        x_hi = sem("x_hi")
        x_cp = sem("x_cp")
        x_lo = sem("x_lo")
        x_sq = sem("x_sq")
        x_st = [sem(f"x_st{i}") for i in range(4)]
        ss_pe = sem("ss_pe")
        ms_rt = sem("ms_rt")
        rstd_ok = sem("rstd_ok")
        wa_sc = sem("wa_sc")
        wa_hi = sem("wa_hi")
        wa_lo = sem("wa_lo")
        al_pe = sem("al_pe")
        al_ok = sem("al_ok")
        w_in = [sem(f"w_in{i}") for i in range(NU)]
        w_hi = sem("w_hi")
        w_lo = sem("w_lo")
        unit_used = sem("unit_used")
        acc_ready = sem("acc_ready")
        acc_free = sem("acc_free")
        out_ready = sem("out_ready")
        stored = sem("stored")
        silu_in = sem("silu_in")
        t_ready = sem("t_ready")
        t_free = sem("t_free")
        sq_done = sem("sq_done")
        n_ready = sem("n_ready")
        n_root = sem("n_root")
        n_dve = sem("n_dve")
        up_in = sem("up_in")
        l_ready = sem("l_ready")
        l_abs = sem("l_abs")
        l_log = sem("l_log")
        l_dve = sem("l_dve")
        l_cum = sem("l_cum")
        l_exp = sem("l_exp")
        l_ok = sem("l_ok")
        res_in = sem("res_in")
        sum_ok = sem("sum_ok")
        rel_in = sem("rel_in")
        r_hi = sem("r_hi")
        r_lo = sem("r_lo")
        s_zero = sem("s_zero")
        qkv_in = [sem(f"qkv_in{i}") for i in range(GH)]
        gg_in = [sem(f"gg_in{i}") for i in range(2)]
        kv_pe = sem("kv_pe")
        st_up = sem("st_up")
        o_pe = sem("o_pe")
        o_ss = sem("o_ss")
        o_rt = sem("o_rt")
        o_rc = sem("o_rc")
        o_nm = sem("o_nm")
        o_tr = sem("o_tr")
        o_gt = sem("o_gt")
        o_hi = sem("o_hi")
        o_lo = sem("o_lo")
        att_in = [sem(f"att_in{i}") for i in range(KVH)]
        s_pe = sem("s_pe")
        s_mx0 = sem("s_mx0")
        s_sub = sem("s_sub")
        s_exp = sem("s_exp")
        s_sm = sem("s_sm")
        s_pr = sem("s_pr")
        s_tr = sem("s_tr")
        s_cp = sem("s_cp")
        s_pv = sem("s_pv")
        s_gt = sem("s_gt")
        s_hi = sem("s_hi")
        s_lo = sem("s_lo")

        NCONST = 11

        block = ctx.enter_context(nc.Block())

        def weights(w, b, u):
            return w[u * UK * P:(u + 1) * UK * P, bass.ds(b * BC, BC)].rearrange("(k p) c -> p k c", p=P)

        wa_in_w, wa_out_w, wb_in_w, wb_out_w = a_w_in[0], a_w_out[0], b_w_in[0], b_w_out[0]

        @block.sync
        def _(sp):
            def load_w(w, nb, b, first=False):
                for u in range(NU):
                    load_unit(w, nb, b, u, first)

            def load_unit(w, nb, b, u, first=False):
                if not first:
                    sp.wait_ge(w_lo, (nb - 1) * NU + u + 1)
                sp.dma_start(WRAW[:, u], weights(w, b, u)).then_inc(w_in[u], 16)

            def store_T(dst, nb, b):
                sp.wait_ge(out_ready, nb + 1)
                sp.dma_start(dst[bass.ds(b * BC, BC), :].rearrange("(i p) s -> p i s", p=P),
                             stageT).then_inc(stored, 16)

            def store_N(dst, nb, b):
                sp.wait_ge(out_ready, nb + 1)
                sp.dma_start(dst[:, bass.ds(b * BC, BC)].rearrange("(s p) c -> p s c", p=P),
                             stageN).then_inc(stored, 16)

            def store_x(i):
                t, q = i // 4, i % 4
                sp.wait_ge(x_cp, i + 1)
                sp.dma_start(xT_s[q * 4 * P:(q + 1) * 4 * P, t * P:(t + 1) * P].rearrange("(k p) s -> p k s", p=P),
                             xraw[:, i % 4]).then_inc(x_st[i % 4], 16)

            for t in range(4):
                sp.dma_start(xin[:, t], x2d[t * P:(t + 1) * P, :]).then_inc(x_in[t], 16)
            at = 0
            for v in (a_norm[0], kv_norm, b_norm[0], a_out_norm[0], a_b_alpha[0]):
                n = v.shape[0] // P
                sp.dma_start(vrows[at:at + n, :], v.rearrange("(k p) -> k p", p=P)).then_inc(consts_in, 16)
                at += n
            for v in (k_norm, b_q_norm[0]):
                for half in range(2):
                    sp.dma_start(vrows[at:at + 1, half * HD:(half + 1) * HD],
                                 v.rearrange("(o p) -> o p", o=1)).then_inc(consts_in, 16)
                at += 1
            sp.dma_start(srow[:, :], b_sinks).then_inc(consts_in, 16)
            sp.dma_start(wa[:, :, :], wa_in_w[:, OA0 * BC:].rearrange("(k p) r -> p k r", p=P)
                         ).then_inc(consts_in, 16)
            for u in range(3):
                load_unit(wa_in_w, 0, 0, u, first=True)
            for t in range(4, ST):
                sp.wait_ge(x_sq, t - 3)
                sp.dma_start(xin[:, t % 4], x2d[t * P:(t + 1) * P, :]).then_inc(x_in[t % 4], 16)
                for i in range(4 * (t - 4), 4 * (t - 3)):
                    store_x(i)
                if t == 6:
                    sp.wait_ge(wa_lo, 1)
                    load_unit(wa_in_w, 0, 0, 3, first=True)
            for i in range(4 * (ST - 4), 4 * ST):
                store_x(i)

            with sp.Fori(1, KA0) as nb:
                load_w(wa_in_w, nb, nb)
                store_T(qa_s, nb - 1, nb - 1)
            for nb in range(KA0, VA0):
                load_w(wa_in_w, nb, nb)
                if nb > KA0:
                    sp.wait_ge(l_ready, 2 * (nb - KA0))
                else:
                    sp.wait_ge(al_ok, 2)
                for r in range(2):
                    sp.dma_start(wup[32 * r:32 * r + RANK, :],
                                 a_w_alpha_up[0][:, (nb - KA0) * DK:(nb - KA0 + 1) * DK]).then_inc(up_in, 16)
                if nb == KA0:
                    store_T(qa_s, nb - 1, nb - 1)
                else:
                    store_N(ka_s, nb - 1, nb - 1 - KA0)
            load_w(wa_in_w, VA0, VA0)
            store_N(ka_s, VA0 - 1, VA0 - 1 - KA0)
            with sp.Fori(VA0 + 1, GA0 + 1) as nb:
                load_w(wa_in_w, nb, nb)
                store_N(va_s, nb - 1, nb - (1 + VA0))
            with sp.Fori(GA0 + 1, OA0) as nb:
                load_w(wa_in_w, nb, nb)
                store_T(ga_s, nb - 1, nb - (1 + GA0))
            load_w(wa_out_w, OA0, 0)
            store_T(ga_s, OA0 - 1, NG_ - 1)

            sp.wait_ge(stored, 16 * OA0)

            def load_head(t, h, first):
                if not first:
                    sp.wait_ge(o_pe, 8 * (t - 1) + 2 * h + 2)
                else:
                    sp.wait_ge(s_zero, 1)
                sp.dma_start(gq[:, h], qa_s[h * DK:(h + 1) * DK, bass.ds(t * P, P)]
                             .rearrange("(i p) s -> p i s", p=P)).then_inc(qkv_in[h], 16)
                sp.dma_start(gk[:, h], ka_s[bass.ds(t * P, P), h * DK:(h + 1) * DK]).then_inc(qkv_in[h], 16)
                sp.dma_start(gv[:, h], va_s[bass.ds(t * P, P), h * DV:(h + 1) * DV]).then_inc(qkv_in[h], 16)
                if not (first and h < 2):
                    sp.wait_ge(o_gt, 4 * t + h - 1)
                sp.dma_start(gg[:, h % 2], ga_s[h * DV:(h + 1) * DV, bass.ds(t * P, P)]
                             .rearrange("(i p) s -> p i s", p=P)).then_inc(gg_in[h % 2], 16)

            for h in range(GH):
                load_head(0, h, True)
            with sp.Fori(1, ST) as t:
                for h in range(GH):
                    load_head(t, h, False)

            def load_res(src, nb, b, first, work_free=None):
                if first:
                    sp.wait_ge(*work_free)
                else:
                    sp.wait_ge(acc_free, (nb + 1) * 4)
                sp.dma_start(bufA, src[bass.ds(b * BC, BC), :].rearrange("(i p) s -> p i s", p=P)
                             ).then_inc(res_in, 16)

            load_res(xT_s, OA0, 0, True, (o_lo, 4 * ST))
            with sp.Fori(OA0 + 1, KV0) as nb:
                load_w(wa_out_w, nb, nb - OA0)
                load_res(xT_s, nb, nb - OA0, False)
                store_T(x1_s, nb - 1, nb - (1 + OA0))
            sp.wait_ge(stored, 16 * (KV0 - 1))
            for pr in range(7):
                if pr > 0:
                    sp.wait_ge(r_lo, pr)
                sp.dma_start(reload_, x1_s[pr * BC:(pr + 1) * BC, :].rearrange("(i p) s -> p i s", p=P)
                             ).then_inc(rel_in, 16)
                if pr % 2 == 0:
                    load_unit(w_kv, KV0, 0, pr // 2)
            store_T(x1_s, KV0 - 1, 7)
            load_w(w_kv, KV0 + 1, 1)
            store_T(kb_s, KV0, 0)
            load_w(wb_in_w, QB0, 0)
            store_N(vb_s, KV0 + 1, 0)
            with sp.Fori(QB0 + 1, GB0 + 1) as nb:
                load_w(wb_in_w, nb, nb - QB0)
                store_T(qb_s, nb - 1, nb - (1 + QB0))
            with sp.Fori(GB0 + 1, OB0) as nb:
                load_w(wb_in_w, nb, nb - QB0)
                store_T(gb_s, nb - 1, nb - (1 + GB0))
            load_w(wb_out_w, OB0, 0)
            store_T(gb_s, OB0 - 1, D // BC - 1)

            sp.wait_ge(stored, 16 * OB0)
            sp.wait_ge(s_zero, 2)

            def load_att(t, h, first):
                if not first:
                    sp.wait_ge(s_gt, 8 * (t - 1) + 2 * h + 2)
                for c in range(2):
                    sp.dma_start(sq_[:, h, c], qb_s[h * 512:(h + 1) * 512, bass.ds(t * P + c * CHUNK, CHUNK)]
                                 .rearrange("(i p) s -> p i s", p=P)).then_inc(att_in[h], 16)
                sp.dma_start(sg_[:, h], gb_s[h * 512:(h + 1) * 512, bass.ds(t * P, P)]
                             .rearrange("(i p) s -> p i s", p=P)).then_inc(att_in[h], 16)
                for half in range(2):
                    rows = slice(half * HD, (half + 1) * HD)
                    if first:
                        sp.dma_start(sk_[rows, h, 64:192], kb_s[h * HD:(h + 1) * HD, 0:128]
                                     ).then_inc(att_in[h], 16)
                    else:
                        sp.dma_start(sk_[rows, h, :], kb_s[h * HD:(h + 1) * HD, bass.ds(t * P - 64, 192)]
                                     ).then_inc(att_in[h], 16)
                for c in range(2):
                    if first and c == 0:
                        sp.dma_start(sv_[64:128, h, c], vb_s[0:64, h * HD:(h + 1) * HD]).then_inc(att_in[h], 16)
                    else:
                        sp.dma_start(sv_[:, h, c], vb_s[bass.ds(t * P - 64 + 64 * c, P), h * HD:(h + 1) * HD]
                                     ).then_inc(att_in[h], 16)

            for h in range(KVH):
                load_att(0, h, True)
            with sp.Fori(1, ST) as t:
                for h in range(KVH):
                    load_att(t, h, False)

            load_res(x1_s, OB0, 0, True, (s_lo, 8 * ST))
            with sp.Fori(OB0 + 1, END) as nb:
                load_w(wb_out_w, nb, nb - OB0)
                load_res(x1_s, nb, nb - OB0, False)
                store_N(out2d, nb - 1, nb - (1 + OB0))
            store_N(out2d, END - 1, D // BC - 1)
            sp.wait_ge(stored, 16 * END)

        @block.gpsimd
        def _(pool):
            nc.gpsimd.memset(ident[:, :], 0.0).then_inc(zeroed, 1)
            nc.gpsimd.memset(ones[:, :], 1.0).then_inc(zeroed, 1)
            nc.gpsimd.memset(pair[:, :], 1.0).then_inc(zeroed, 1)
            nc.gpsimd.memset(eps_t[:, :], EPS).then_inc(zeroed, 1)
            pool.wait_ge(zeroed, 4)
            nc.gpsimd.affine_select(out=ident[:, :], in_=ident[:, :], compare_op=ALU.not_equal, fill=1.0, base=0,
                                    pattern=[[-1, P]], channel_multiplier=1).then_inc(zeroed, 1)
            nc.gpsimd.affine_select(out=pair[:, 64:128], in_=pair[:, 64:128], compare_op=ALU.is_ge, fill=0.0,
                                    base=-64, pattern=[[0, 64]], channel_multiplier=1).then_inc(zeroed, 1)
            nc.gpsimd.affine_select(out=pair[:, 0:64], in_=pair[:, 0:64], compare_op=ALU.is_ge, fill=0.0,
                                    base=63, pattern=[[0, 64]], channel_multiplier=-1).then_inc(zeroed, 1)
            for i in range(4 * ST):
                t, q = i // 4, i % 4
                pool.wait_ge(x_cp, i + 1)
                dst = (slice(None), slice(4 * q, 4 * q + 4), slice(t * P, (t + 1) * P))
                nc.gpsimd.tensor_tensor(XL[dst], xraw[:, i % 4], XH[dst].bitcast(F32), ALU.subtract
                                        ).then_inc(x_lo, 1)
            pool.wait_ge(o_lo, 4 * ST)
            nc.gpsimd.memset(sqsum, 0.0).then_inc(sum_ok, 1)
            with pool.Fori(OA0, KV0) as nb:
                for i in range(CT):
                    if i == 0:
                        pool.wait_ge(sq_done, nb - OA0 + 1)
                    pool.wait_ge(sum_ok, (nb - OA0) * 2 + i + 1)
                    nc.gpsimd.tensor_tensor(sqsum, sqsum, bufB[:, i], ALU.add).then_inc(sum_ok, 1)
            def normalise(n, i):
                e = ex_[:, i % 2, 0:512].rearrange("p (g k) -> p g k", g=4)
                pool.wait_ge(s_sm, 3 * n + 3)
                if not isinstance(n, int) or n >= 2:
                    pool.wait_ge(s_tr, n - 1)
                nc.gpsimd.tensor_tensor(pr_[:, i % 2], e,
                                        st2[:, 8 + 4 * (i % 2):12 + 4 * (i % 2)].unsqueeze(2).to_broadcast([P, 4, P]),
                                        ALU.mult).then_inc(s_pr, 1)

            for i in range(8):
                normalise(i, i)
            with pool.Fori(1, ST) as t:
                for i in range(8):
                    normalise(8 * t + i, i)

        @block.scalar
        def _(act):
            def split_hi(nb, u, gain):
                act.wait_ge(w_in[u], 16 * (nb + 1))
                if isinstance(nb, int) and nb == 0 and u < 2:
                    pass
                elif u == 1:
                    act.wait_ge(acc_ready, 4 * nb)
                elif u >= 2:
                    act.wait_ge(unit_used, 3 * nb + u - 1)
                else:
                    act.wait_ge(unit_used, 3 * nb)
                if gain is None:
                    nc.scalar.copy(WHI[:, u % 2], WRAW[:, u]).then_inc(w_hi, 1)
                    return
                for k in range(UK):
                    g = gain[:, (u * UK + k) % gain.shape[1]:(u * UK + k) % gain.shape[1] + 1]
                    last = nc.scalar.activation(WHI[:, u % 2, k], WRAW[:, u, k], ACT.Copy, scale=g)
                last.then_inc(w_hi, 1)

            def splits(nb, gain, *us):
                for u in us:
                    split_hi(nb, u, gain)

            def copy_T(nb, tb):
                for g in range(4):
                    act.wait_ge(t_ready, 4 * tb + g + 1)
                    last = nc.scalar.copy(stageN[:, 2 * g:2 * g + 2, :],
                                          PS[:, 4 + g, :].rearrange("p (s c) -> p s c", s=2))
                    if g < 3:
                        last.then_inc(t_free, 1)
                last.then_inc(out_ready, 1)

            def square(nb, k):
                act.wait_ge(acc_free, 4 * nb + 8)
                nc.scalar.activation(bufB, stageT, ACT.Square).then_inc(sq_done, 1)

            def roots(nb, k):
                for j in range(4):
                    act.wait_ge(n_ready, 4 * k + j + 1)
                    last = nc.scalar.activation(bufA[:, j // 2, (j % 2) * HALF:(j % 2 + 1) * HALF], PS[:, 4 + j, :],
                                                ACT.Sqrt, scale=1.0 / HD, bias=eps_t[:, 0:1])
                last.then_inc(n_root, 1)

            def silu(nb, k):
                act.wait_ge(acc_free, 4 * nb + 8)
                nc.scalar.activation(stageT, stageT, ACT.Silu).then_inc(out_ready, 1)

            act.wait_ge(zeroed, 7)
            for t in range(ST):
                for q in range(4):
                    i = 4 * t + q
                    act.wait_ge(x_tr, i + 1)
                    nc.scalar.copy(XH[:, 4 * q:4 * q + 4, t * P:(t + 1) * P],
                                   PS[:, 4 + i % 4, :].rearrange("p (k s) -> p k s", k=4)).then_inc(x_hi, 1)
                nc.scalar.activation(xin[:, t % 4], xin[:, t % 4], ACT.Square,
                                     accum_out=ssq[:, t:t + 1]).then_inc(x_sq, 1)
                if t == 0:
                    act.wait_ge(wa_sc, 2)
                    nc.scalar.copy(WHI[:, :, :, :].rearrange("p a k (b c) -> p (a k b) c", c=P)[:, :, 0:RANK],
                                   wa[:, :, :]).then_inc(wa_hi, 1)
            act.wait_ge(ss_pe, 1)
            for j in range(NH):
                nc.scalar.activation(RSTD[:, j * HALF:(j + 1) * HALF], PS[:, j, :], ACT.Sqrt,
                                     scale=1.0 / D, bias=eps_t[:, 0:1]).then_inc(ms_rt, 1)
            act.wait_ge(al_pe, 1)
            splits(0, g_a, 0)
            splits(0, g_a, 1, 2, 3)
            splits(1, g_a, 0)
            with act.Fori(1, KA0) as nb:
                splits(nb, g_a, 1, 2, 3)
                splits(nb + 1, g_a, 0)
            for nb in range(KA0, VA0):
                h = nb - KA0
                splits(nb, g_a, 1)
                if h > 0:
                    copy_T(nb - 1, h - 1)
                splits(nb, g_a, 2, 3)
                for i in range(2):
                    n = 2 * h + i
                    e = bufA[:, 1]
                    act.wait_ge(l_abs, n + 1)
                    nc.scalar.activation(e, e, ACT.Exp).then_inc(l_log, 1)
                    act.wait_ge(l_log, 3 * n + 1)
                    nc.scalar.activation(e, e, ACT.Ln, bias=ones[:, 0:1]).then_inc(l_log, 1)
                    act.wait_ge(l_cum, n + 1)
                    nc.scalar.activation(bufB[:, i], bufB[:, i], ACT.Exp, scale=1.0 / TAU).then_inc(l_exp, 1)
                    nc.scalar.activation(dc[:, n, :], bufA[:, 1].rearrange("p (c s) -> p c s", s=CHUNK)[:, :, CHUNK - 1],
                                         ACT.Exp, scale=1.0 / TAU).then_inc(l_log, 1)
                splits(nb + 1, g_a, 0)
            splits(VA0, g_a, 1)
            copy_T(VA0 - 1, 3)
            splits(VA0, g_a, 2, 3)
            splits(VA0 + 1, g_a, 0)
            with act.Fori(VA0 + 1, GA0) as nb:
                splits(nb, g_a, 1)
                copy_T(nb - 1, nb - (1 + KA0))
                splits(nb, g_a, 2, 3)
                splits(nb + 1, g_a, 0)
            splits(GA0, g_a, 1)
            copy_T(GA0 - 1, GA0 - 1 - KA0)
            splits(GA0, g_a, 2, 3)
            splits(GA0 + 1, g_a, 0)
            silu(GA0, 0)
            with act.Fori(GA0 + 1, OA0 - 1) as nb:
                splits(nb, g_a, 1, 2, 3)
                splits(nb + 1, g_a, 0)
                silu(nb, nb - GA0)
            splits(OA0 - 1, g_a, 1, 2, 3)
            splits(OA0, g_o, 0)
            silu(OA0 - 1, NG_ - 1)

            def gla_out(t, h):
                n = 4 * t + h
                act.wait_ge(o_pe, 8 * t + 2 * h + 2)
                if not isinstance(n, int) or n >= 1:
                    act.wait_ge(o_tr, n)
                nc.scalar.activation(onrm, PS[:, 4 + h % 2, :], ACT.Square,
                                     accum_out=st1[:, h:h + 1]).then_inc(o_ss, 1)
                act.wait_ge(o_ss, n + 1)
                nc.scalar.activation(st1[:, h:h + 1], st1[:, h:h + 1], ACT.Sqrt, scale=1.0 / DV,
                                     bias=eps_t[:, 0:1]).then_inc(o_rt, 1)
                act.wait_ge(o_rc, n + 1)
                nc.scalar.activation(onrm, PS[:, 4 + h % 2, :], ACT.Copy,
                                     scale=st1[:, 4 + h:5 + h]).then_inc(o_nm, 1)

            def gla_hi(t, h):
                n = 4 * t + h
                act.wait_ge(o_gt, n + 1)
                nc.scalar.copy(XH[:, 4 * h:4 * h + 4, bass.ds(t * P, P)],
                               ogate.rearrange("p (i s) -> p i s", i=4)).then_inc(o_hi, 1)

            def gla_act(t):
                for h in range(GH):
                    gla_out(t, h)
                    gla_hi(t, h)

            gla_act(0)
            with act.Fori(1, ST) as t:
                gla_act(t)

            with act.Fori(OA0, KV0 - 1) as nb:
                splits(nb, g_o, 1, 2, 3)
                splits(nb + 1, g_o, 0)
                act.wait_ge(sum_ok, (nb - OA0) * 2 + 1)
                square(nb, nb - OA0)
                act.wait_ge(sq_done, nb - (OA0 - 1))
                nc.scalar.copy(eps_t[:, 0:1], eps_t[:, 0:1]).then_inc(out_ready, 1)
            nb = KV0 - 1

            def pair_hi(pr, src, unit):
                if unit is not None:
                    act.wait_ge(unit_used, 3 * nb + unit + 1)
                act.wait_ge(rel_in, 16 * (pr + 1)) if pr < 7 else None
                nc.scalar.copy(XH[:, 2 * pr:2 * pr + 2, :], src).then_inc(r_hi, 1)

            splits(nb, g_o, 1, 2)
            pair_hi(0, reload_, 0)
            pair_hi(1, reload_, 0)
            splits(nb, g_o, 3)
            pair_hi(2, reload_, 1)
            pair_hi(3, reload_, 1)
            splits(KV0, g_kv, 0)
            pair_hi(4, reload_, 2)
            pair_hi(5, reload_, 2)
            act.wait_ge(sum_ok, (nb - OA0) * 2 + 1)
            square(nb, nb - OA0)
            act.wait_ge(sq_done, nb - (OA0 - 1))
            nc.scalar.copy(eps_t[:, 0:1], eps_t[:, 0:1]).then_inc(out_ready, 1)
            pair_hi(6, reload_, None)
            pair_hi(7, stageT, None)
            splits(KV0, g_kv, 1, 2)
            act.wait_ge(ss_pe, 2)
            for j in range(NH):
                nc.scalar.activation(RSTD[:, j * HALF:(j + 1) * HALF], PS[:, 4 + j, :], ACT.Sqrt,
                                     scale=1.0 / D, bias=eps_t[:, 0:1]).then_inc(ms_rt, 1)
            splits(KV0, g_kv, 3)
            splits(KV0 + 1, g_kv, 0)
            square(KV0, 8)
            splits(KV0 + 1, g_kv, 1)
            roots(KV0, 0)
            splits(KV0 + 1, g_kv, 2, 3)
            splits(QB0, g_b, 0)
            splits(QB0, g_b, 1)
            copy_T(KV0 + 1, NK_ + NV_)
            splits(QB0, g_b, 2, 3)
            splits(QB0 + 1, g_b, 0)
            square(QB0, 9)
            with act.Fori(QB0 + 1, GB0) as nb:
                splits(nb, g_b, 1)
                roots(nb - 1, nb - QB0)
                splits(nb, g_b, 2, 3)
                splits(nb + 1, g_b, 0)
                square(nb, nb - QB0 + 9)
            splits(GB0, g_b, 1)
            roots(GB0 - 1, GB0 - QB0)
            splits(GB0, g_b, 2, 3)
            splits(GB0 + 1, g_b, 0)
            silu(GB0, 0)
            with act.Fori(GB0 + 1, OB0 - 1) as nb:
                splits(nb, g_b, 1, 2, 3)
                splits(nb + 1, g_b, 0)
                silu(nb, nb - GB0)
            splits(OB0 - 1, g_b, 1, 2, 3)
            splits(OB0, None, 0)
            silu(OB0 - 1, 0)

            def att_act(t, first):
                for s in range(10):
                    if s < 8:
                        n = 8 * t + s
                        lo = 64 if first and s % 2 == 0 else 0
                        act.wait_ge(s_sub, n + 1)
                        if lo:
                            e4 = ex_[:, s % 2, 0:512].rearrange("p (g k) -> p g k", g=4)[:, :, lo:]
                            nc.scalar.activation(e4, e4, ACT.Exp)
                            nc.scalar.activation(ex_[:, s % 2, 512:516], ex_[:, s % 2, 512:516],
                                                 ACT.Exp).then_inc(s_exp, 1)
                        else:
                            nc.scalar.activation(ex_[:, s % 2], ex_[:, s % 2], ACT.Exp).then_inc(s_exp, 1)
                    if 1 <= s <= 8:
                        i = s - 1
                        n = 8 * t + i
                        act.wait_ge(s_tr, n + 1)
                        if not (first and i < 2):
                            act.wait_ge(s_pv, n - 1)
                        nc.scalar.copy(pt_[:, i % 2], PS[:, 4 + i % 2, :].rearrange("p (r k) -> p r k", r=2)
                                       ).then_inc(s_cp, 1)
                    if s >= 2:
                        i = s - 2
                        n = 8 * t + i
                        h, c = i // 2, i % 2
                        act.wait_ge(s_gt, n + 1)
                        nc.scalar.copy(XH[:, 4 * h:4 * h + 4, bass.ds(t * P + CHUNK * c, CHUNK)],
                                       so_[:, i % 2]).then_inc(s_hi, 1)

            att_act(0, True)
            with act.Fori(1, ST) as t:
                att_act(t, False)

            splits(OB0, None, 1, 2, 3)
            splits(OB0 + 1, None, 0)
            with act.Fori(OB0 + 1, END - 1) as nb:
                splits(nb, None, 1)
                copy_T(nb - 1, nb - (1 + OB0) + NK_ + NV_ + 1)
                splits(nb, None, 2, 3)
                splits(nb + 1, None, 0)
            splits(END - 1, None, 1)
            copy_T(END - 2, END - 2 - OB0 + NK_ + NV_ + 1)
            splits(END - 1, None, 2, 3)
            copy_T(END - 1, END - 1 - OB0 + NK_ + NV_ + 1)

        @block.vector
        def _(dve):
            def split_lo(nb, u, gain):
                dve.wait_ge(w_hi, NU * nb + u + 1)
                hi = WHI[:, u % 2].bitcast(F32)
                if gain is None:
                    nc.vector.tensor_tensor(WLO[:, u % 2], WRAW[:, u], hi, ALU.subtract).then_inc(w_lo, 1)
                    return
                for k in range(UK):
                    g = gain[:, (u * UK + k) % gain.shape[1]:(u * UK + k) % gain.shape[1] + 1]
                    last = nc.vector.scalar_tensor_tensor(WLO[:, u % 2, k], WRAW[:, u, k], g, hi[:, k],
                                                          ALU.mult, ALU.subtract)
                last.then_inc(w_lo, 1)

            def splits(nb, gain, *us):
                for u in us:
                    split_lo(nb, u, gain)

            def evac(nb, scale=None, factor=None, add=None, final=False):
                if not (isinstance(nb, int) and nb == 0):
                    dve.wait_ge(stored, 16 * nb)
                for j in range(4):
                    ct, cols = j // NH, slice((j % NH) * HALF, (j % NH + 1) * HALF)
                    dve.wait_ge(acc_ready, 4 * nb + j + 1)
                    dst, src = stageT[:, ct, cols], PS[:, j, :]
                    if add is not None:
                        i = nc.vector.tensor_tensor(dst, src, add[:, ct, cols], ALU.add)
                    elif factor is not None:
                        i = nc.vector.tensor_tensor(dst, src, factor[:, ct, cols], ALU.mult)
                    elif scale is not None:
                        i = nc.vector.scalar_tensor_tensor(dst, src, scale, RSTD[:, cols], ALU.mult, ALU.mult)
                    else:
                        i = nc.vector.tensor_tensor(dst, src, RSTD[:, cols], ALU.mult)
                    i.then_inc(acc_free, 1)
                if final:
                    dve.wait_ge(acc_free, 4 * nb + 8)
                    nc.vector.tensor_copy(st1[:, 0:1], eps_t[:, 0:1]).then_inc(out_ready, 1)

            def head_norm(k, gain):
                dve.wait_ge(n_root, k + 1)
                nc.vector.reciprocal(bufA, bufA).then_inc(n_dve, 1)
                dve.wait_ge(n_dve, k + 1)
                for i in range(CT):
                    last = nc.vector.scalar_tensor_tensor(stageT[:, i], stageT[:, i], gain, bufA[:, i],
                                                          ALU.mult, ALU.mult)
                last.then_inc(out_ready, 1)

            nc.vector.memset(WHI[:, :, :, :].bitcast(F32), 0.0).then_inc(acc_free, 4)
            dve.wait_ge(acc_free, 4)
            dve.wait_ge(v_pe, 2)
            nc.vector.tensor_copy(vcols[:, :], PS[:, 0, 0:NR]).then_inc(v_ok, 1)
            for half in range(2):
                rows = slice(half * HD, (half + 1) * HD)
                nc.vector.tensor_copy(sinks[rows].rearrange("p h (a j) -> p h a j", a=2),
                                      PS[rows, 1, 0:KVH * 8].rearrange("p (h j c a) -> p c h a j", j=2, c=2, a=2)[:, half]
                                      ).then_inc(v_ok, 1)
            dve.wait_ge(v_ok, 3)
            nc.vector.tensor_tensor(wa[:, :, :], wa[:, :, :], g_a.unsqueeze(2).to_broadcast([P, KT, RANK]),
                                    ALU.mult).then_inc(wa_sc, 1)
            nc.vector.scalar_tensor_tensor(kgain[:, 0:1], vcols[:, NR - 2:NR - 1], HD ** -0.5, vcols[:, NR - 1:NR],
                                           ALU.mult, ALU.mult).then_inc(wa_sc, 1)
            wcat = WHI[:, :, :, :].rearrange("p a k (b c) -> p (a k b) c", c=P)
            for i in range(4 * ST):
                dve.wait_ge(x_hi, i + 1)
                if i >= 4:
                    dve.wait_ge(x_st[i % 4], 16 * (i // 4))
                    dve.wait_ge(x_lo, i - 3)
                nc.vector.tensor_copy(xraw[:, i % 4].rearrange("p k s -> p (k s)"), PS[:, 4 + i % 4, :]
                                      ).then_inc(x_cp, 1)
                if i == 4:
                    dve.wait_ge(wa_hi, 1)
                    nc.vector.tensor_tensor(wcat[:, :, 32:32 + RANK], wa[:, :, :],
                                            wcat[:, :, 0:RANK].bitcast(F32), ALU.subtract).then_inc(wa_lo, 1)
            for j in range(NH):
                dve.wait_ge(ms_rt, j + 1)
                nc.vector.reciprocal(RSTD[:, j * HALF:(j + 1) * HALF], RSTD[:, j * HALF:(j + 1) * HALF]
                                     ).then_inc(rstd_ok, 1)
            dve.wait_ge(rstd_ok, NH)
            dve.wait_ge(al_pe, 1)
            for s in range(4):
                dve.wait_ge(x_st[s], 16 * ST)
            dve.wait_ge(x_lo, 4 * ST)
            nc.vector.memset(wup, 0.0).then_inc(al_ok, 1)
            for j in range(NH):
                last = nc.vector.tensor_tensor(alow[:, j * HALF:(j + 1) * HALF], PS[0:64, 4 + j, :],
                                               RSTD[0:64, j * HALF:(j + 1) * HALF], ALU.mult)
            last.then_inc(al_ok, 1)
            splits(0, g_a, 0)
            splits(0, g_a, 1, 2, 3)
            splits(1, g_a, 0)
            evac(0, scale=DK ** -0.5, final=True)
            with dve.Fori(1, KA0) as nb:
                splits(nb, g_a, 1, 2, 3)
                splits(nb + 1, g_a, 0)
                evac(nb, scale=DK ** -0.5, final=True)
            for nb in range(KA0, VA0):
                splits(nb, g_a, 1, 2, 3)
                for i in range(2):
                    n = 2 * (nb - KA0) + i
                    z, e = bufA[:, 0], bufA[:, 1]
                    dve.wait_ge(l_ready, n + 1)
                    if n > 0:
                        dve.wait_ge(l_log, 3 * n)
                    for j in range(NH):
                        last = nc.vector.tensor_scalar(z[:, j * HALF:(j + 1) * HALF], PS[:, 4 + 2 * i + j, :],
                                                       b_al[:, n:n + 1], None, ALU.add)
                    last.then_inc(l_dve, 1)
                    dve.wait_ge(l_dve, 3 * n + 1)
                    nc.vector.scalar_tensor_tensor(e, z, -1.0, z, ALU.mult, ALU.min).then_inc(l_abs, 1)
                    dve.wait_ge(l_log, 3 * n + 2)
                    nc.vector.scalar_tensor_tensor(z, z, 0.0, e, ALU.min, ALU.subtract).then_inc(l_dve, 1)
                    dve.wait_ge(l_dve, 3 * n + 2)
                    for c in range(SEQ // CHUNK):
                        cs = slice(c * CHUNK, (c + 1) * CHUNK)
                        last = nc.vector.tensor_tensor_scan(e[:, cs], ones[:, 0:CHUNK], z[:, cs], 0.0,
                                                            ALU.mult, ALU.add)
                    last.then_inc(l_dve, 1)
                    dve.wait_ge(l_dve, 3 * n + 3)
                    ev = e.rearrange("p (c s) -> p c s", s=CHUNK)
                    nc.vector.tensor_tensor(bufB[:, i].rearrange("p (c s) -> p c s", s=CHUNK),
                                            ev[:, :, CHUNK - 1:CHUNK].to_broadcast([P, SEQ // CHUNK, CHUNK]), ev,
                                            ALU.subtract).then_inc(l_cum, 1)
                    dve.wait_ge(l_exp, n + 1)
                    nc.vector.tensor_tensor(bufB[:, i], bufB[:, i], RSTD[:, :], ALU.mult).then_inc(l_ok, 1)
                splits(nb + 1, g_a, 0)
                dve.wait_ge(l_ok, 2 * (nb - KA0) + 2)
                evac(nb, factor=bufB)
            with dve.Fori(VA0, GA0) as nb:
                splits(nb, g_a, 1, 2, 3)
                splits(nb + 1, g_a, 0)
                evac(nb)
            with dve.Fori(GA0, OA0 - 1) as nb:
                splits(nb, g_a, 1, 2, 3)
                splits(nb + 1, g_a, 0)
                evac(nb)
            splits(OA0 - 1, g_a, 1, 2, 3)
            splits(OA0, g_o, 0)
            evac(OA0 - 1)

            dve.wait_ge(stored, 16 * OA0)
            nc.vector.memset(WORK[:, 0:4096], 0.0).then_inc(s_zero, 1)
            dve.wait_ge(s_zero, 1)

            def gla_update(t, i):
                h, c = i // 2, i % 2
                n = 8 * t + i
                dve.wait_ge(kv_pe, n + 1)
                if not isinstance(n, int) or n >= 1:
                    dve.wait_ge(o_pe, n)
                    dve.wait_ge(st_up, n)
                for k in range(2):
                    last = nc.vector.scalar_tensor_tensor(state[:, h, k], state[:, h, k],
                                                          dc[:, 2 * h + k, bass.ds(2 * t + c, 1)],
                                                          PS[:, 2 * (i % 2) + k, :], ALU.mult, ALU.add)
                last.then_inc(st_up, 1)

            def gla_recip(t, h):
                dve.wait_ge(o_rt, 4 * t + h + 1)
                nc.vector.reciprocal(st1[:, 4 + h:5 + h], st1[:, h:h + 1]).then_inc(o_rc, 1)

            def gla_gate(t, h):
                n = 4 * t + h
                dve.wait_ge(o_tr, n + 1)
                dve.wait_ge(gg_in[h % 2], 16 * (2 * t + h // 2 + 1))
                if not isinstance(n, int) or n >= 1:
                    dve.wait_ge(o_lo, n)
                nc.vector.tensor_tensor(ogate, PS[:, 6 + h % 2, :], gg[:, h % 2].rearrange("p i s -> p (i s)"),
                                        ALU.mult).then_inc(o_gt, 1)

            def gla_lo(t, h):
                n = 4 * t + h
                dve.wait_ge(o_hi, n + 1)
                dst = (slice(None), slice(4 * h, 4 * h + 4), bass.ds(t * P, P))
                nc.vector.tensor_tensor(XL[dst], ogate.rearrange("p (i s) -> p i s", i=4), XH[dst].bitcast(F32),
                                        ALU.subtract).then_inc(o_lo, 1)

            def gla_dve(t):
                for h in range(GH):
                    gla_update(t, 2 * h)
                    if h > 0:
                        gla_recip(t, h - 1)
                    if h > 1:
                        gla_lo(t, h - 2)
                    gla_update(t, 2 * h + 1)
                    if h > 0:
                        gla_gate(t, h - 1)
                gla_recip(t, GH - 1)
                gla_lo(t, GH - 2)
                gla_gate(t, GH - 1)
                gla_lo(t, GH - 1)

            gla_dve(0)
            with dve.Fori(1, ST) as t:
                gla_dve(t)

            def evac_res(nb, k, final=False):
                dve.wait_ge(res_in, 16 * (k + 1))
                evac(nb, add=bufA, final=final)

            with dve.Fori(OA0, KV0 - 1) as nb:
                splits(nb, g_o, 1, 2, 3)
                splits(nb + 1, g_o, 0)
                evac_res(nb, nb - OA0)

            def pair_lo(pr, src):
                dve.wait_ge(r_hi, pr + 1)
                dst = (slice(None), slice(2 * pr, 2 * pr + 2), slice(None))
                nc.vector.tensor_tensor(XL[dst], src, XH[dst].bitcast(F32), ALU.subtract).then_inc(r_lo, 1)

            splits(KV0 - 1, g_o, 1, 2)
            pair_lo(0, reload_)
            pair_lo(1, reload_)
            splits(KV0 - 1, g_o, 3)
            pair_lo(2, reload_)
            pair_lo(3, reload_)
            splits(KV0, g_kv, 0)
            pair_lo(4, reload_)
            pair_lo(5, reload_)
            evac_res(KV0 - 1, 7)
            pair_lo(6, reload_)
            pair_lo(7, stageT)
            splits(KV0, g_kv, 1, 2)
            for j in range(NH):
                dve.wait_ge(ms_rt, NH + j + 1)
                nc.vector.reciprocal(RSTD[:, j * HALF:(j + 1) * HALF], RSTD[:, j * HALF:(j + 1) * HALF]
                                     ).then_inc(rstd_ok, 1)
            dve.wait_ge(rstd_ok, 2 * NH)
            splits(KV0, g_kv, 3)
            splits(KV0 + 1, g_kv, 0)
            evac(KV0)
            splits(KV0 + 1, g_kv, 1)
            head_norm(0, kgain[:, 0:1])
            splits(KV0 + 1, g_kv, 2, 3)
            splits(QB0, g_b, 0)
            evac(KV0 + 1)
            splits(QB0, g_b, 1, 2, 3)
            splits(QB0 + 1, g_b, 0)
            evac(QB0)
            with dve.Fori(QB0 + 1, GB0) as nb:
                splits(nb, g_b, 1)
                head_norm(nb - QB0, ones[:, 0:1])
                splits(nb, g_b, 2, 3)
                splits(nb + 1, g_b, 0)
                evac(nb)
            splits(GB0, g_b, 1)
            head_norm(GB0 - QB0, ones[:, 0:1])
            splits(GB0, g_b, 2, 3)
            splits(GB0 + 1, g_b, 0)
            evac(GB0)
            with dve.Fori(GB0 + 1, OB0 - 1) as nb:
                splits(nb, g_b, 1, 2, 3)
                splits(nb + 1, g_b, 0)
                evac(nb)
            splits(OB0 - 1, g_b, 1, 2, 3)
            splits(OB0, None, 0)
            evac(OB0 - 1)

            dve.wait_ge(stored, 16 * OB0)
            nc.vector.memset(WORK[:, 4096:9216], 0.0).then_inc(s_zero, 1)
            dve.wait_ge(s_zero, 2)

            def scores(i):
                return PS[:, 2 * (i % 2):2 * (i % 2) + 2, 0:256].rearrange("p a (j k) -> p a j k", j=2)

            def att_front(t, i, first):
                n = 8 * t + i
                lo = 64 if first and i % 2 == 0 else 0
                mx = st2[:, 0:4]
                sk = sinks[:, i // 2, :]
                dve.wait_ge(s_pe, n + 1)
                if not (first and i == 0):
                    dve.wait_ge(s_sub, n)
                nc.vector.tensor_reduce(mx.rearrange("p (a j) -> p a j", a=2), scores(i)[:, :, :, lo:], AX.X, ALU.max
                                        ).then_inc(s_mx0, 1)
                dve.wait_ge(s_mx0, 2 * n + 1)
                nc.vector.tensor_tensor(mx, mx, sk, ALU.max).then_inc(s_mx0, 1)
                dve.wait_ge(s_mx0, 2 * n + 2)
                if not (first and i < 2):
                    dve.wait_ge(s_pr, n - 1)
                nc.vector.tensor_tensor(ex_[:, i % 2, 512:516], sk, mx, ALU.subtract)
                nc.vector.tensor_tensor(
                    ex_[:, i % 2, 0:512].rearrange("p (a j k) -> p a j k", a=2, j=2)[:, :, :, lo:],
                    scores(i)[:, :, :, lo:],
                    mx.rearrange("p (a j) -> p a j", a=2).unsqueeze(3).to_broadcast([P, 2, 2, P - lo]),
                    ALU.subtract).then_inc(s_sub, 1)

            def att_back(t, i, first):
                n = 8 * t + i
                sm, rc = st2[:, 4:8], st2[:, 8 + 4 * (i % 2):12 + 4 * (i % 2)]
                dve.wait_ge(s_exp, n + 1)
                if not (first and i == 0):
                    dve.wait_ge(s_sm, 3 * n)
                if not (first and i < 2):
                    dve.wait_ge(s_pr, n - 1)
                nc.vector.tensor_reduce(sm, ex_[:, i % 2, 0:512].rearrange("p (g k) -> p g k", g=4), AX.X, ALU.add
                                        ).then_inc(s_sm, 1)
                dve.wait_ge(s_sm, 3 * n + 1)
                nc.vector.tensor_tensor(sm, sm, ex_[:, i % 2, 512:516], ALU.add).then_inc(s_sm, 1)
                dve.wait_ge(s_sm, 3 * n + 2)
                nc.vector.reciprocal(rc, sm).then_inc(s_sm, 1)

            def att_gate(t, i, first):
                n = 8 * t + i
                h, c = i // 2, i % 2
                dve.wait_ge(s_pv, n + 1)
                if not (first and i < 2):
                    dve.wait_ge(s_lo, n - 1)
                nc.vector.tensor_tensor(so_[:, i % 2], PS[:, 6 + i % 2, 0:256].rearrange("p (i s) -> p i s", i=QCT),
                                        sg_[:, h, :, CHUNK * c:CHUNK * (c + 1)], ALU.mult).then_inc(s_gt, 1)

            def att_lo(t, i):
                n = 8 * t + i
                h, c = i // 2, i % 2
                dve.wait_ge(s_hi, n + 1)
                dst = (slice(None), slice(4 * h, 4 * h + 4), bass.ds(t * P + CHUNK * c, CHUNK))
                nc.vector.tensor_tensor(XL[dst], so_[:, i % 2], XH[dst].bitcast(F32), ALU.subtract
                                        ).then_inc(s_lo, 1)

            def att_dve(t, first):
                for s in range(11):
                    if s < 8:
                        att_front(t, s, first)
                    if 1 <= s <= 8:
                        att_back(t, s - 1, first)
                    if 2 <= s <= 9:
                        att_gate(t, s - 2, first)
                    if s >= 3:
                        att_lo(t, s - 3)
                    if first and s in (6, 7):
                        pass

            att_dve(0, True)
            with dve.Fori(1, ST) as t:
                att_dve(t, False)

            with dve.Fori(OB0, END - 1) as nb:
                splits(nb, None, 1, 2, 3)
                splits(nb + 1, None, 0)
                evac_res(nb, nb - OB0 + 8)
            splits(END - 1, None, 1, 2, 3)
            evac_res(END - 1, 15)

        @block.tensor
        def _(pe):
            def unit(nb, u, ready=None):
                pe.wait_ge(w_lo, NU * nb + u + 1)
                if ready is not None:
                    pe.wait_ge(*ready)
                for j in range(4):
                    ct, cols = j // NH, slice((j % NH) * HALF, (j % NH + 1) * HALF)
                    if u == 0:
                        pe.wait_ge(acc_free, 4 * nb + j + 1)
                    for k in range(UK):
                        kt = UK * u + k
                        hi, lo = (w[:, u % 2, k, ct * P:(ct + 1) * P] for w in (WHI, WLO))
                        nc.tensor.matmul(PS[:, j, :], hi, XH[:, kt, cols], start=kt == 0, stop=False)
                        nc.tensor.matmul(PS[:, j, :], hi, XL[:, kt, cols], start=False, stop=False)
                        last = nc.tensor.matmul(PS[:, j, :], lo, XH[:, kt, cols], start=False, stop=kt == KT - 1)
                    if u == NU - 1:
                        last.then_inc(acc_ready, 1)
                if u < NU - 1:
                    last.then_inc(unit_used, 1)

            def units(nb, *us):
                for u in us:
                    unit(nb, u)

            def transposes(nb, tb):
                pe.wait_ge(acc_free, 4 * nb + 8)
                for g in range(4):
                    for s in range(2):
                        for ct in range(CT):
                            st = 2 * g + s
                            last = nc.tensor.transpose(PS[:, 4 + g, (2 * s + ct) * P:(2 * s + ct + 1) * P],
                                                       stageT[:, ct, st * P:(st + 1) * P], ident[:, :])
                    last.then_inc(t_ready, 1)

            def head_sums(k, sq_count):
                pe.wait_ge(sq_done, sq_count)
                for j in range(4):
                    nc.tensor.matmul(PS[:, 4 + j, :], pair[:, :],
                                     bufB[:, j // NH, (j % NH) * HALF:(j % NH + 1) * HALF],
                                     start=True, stop=True).then_inc(n_ready, 1)

            pe.wait_ge(zeroed, 7)
            pe.wait_ge(consts_in, 16 * NCONST)
            nc.tensor.transpose(PS[:, 0, 0:NR], vrows[:, :], ident[0:NR, 0:NR]).then_inc(v_pe, 1)
            nc.tensor.matmul(PS[:, 1, 0:KVH * 8], ones[0:1, :], srow[:, :], start=True, stop=True).then_inc(v_pe, 1)
            for i in range(4 * ST):
                t, q = i // 4, i % 4
                pe.wait_ge(x_in[t % 4], 16 * (t // 4 + 1))
                if i >= 4:
                    pe.wait_ge(x_cp, i - 3)
                for k in range(4):
                    last = nc.tensor.transpose(PS[:, 4 + i % 4, k * P:(k + 1) * P],
                                               xin[:, t % 4, (4 * q + k) * P:(4 * q + k + 1) * P], ident[:, :])
                last.then_inc(x_tr, 1)
            pe.wait_ge(v_ok, 3)
            for t in range(ST):
                pe.wait_ge(x_sq, t + 1)
                last = nc.tensor.matmul(PS[:, t // 4, (t % 4) * P:(t % 4 + 1) * P],
                                        ssq[:, t:t + 1].to_broadcast([P, P]), ident[:, :], start=True, stop=True)
            last.then_inc(ss_pe, 1)
            pe.wait_ge(x_cp, 4 * ST)
            pe.wait_ge(x_lo, 4 * ST)
            pe.wait_ge(wa_lo, 1)
            wcat = WHI[:, :, :, :].rearrange("p a k (b c) -> p (a k b) c", c=P)
            for j in range(NH):
                cols = slice(j * HALF, (j + 1) * HALF)
                for kt in range(KT):
                    nc.tensor.matmul(PS[:, 4 + j, :], wcat[:, kt, :], XH[:, kt, cols], start=kt == 0, stop=False)
                    last = nc.tensor.matmul(PS[:, 4 + j, :], wcat[:, kt, :], XL[:, kt, cols], start=False,
                                            stop=kt == KT - 1)
            last.then_inc(al_pe, 1)

            pe.wait_ge(ms_rt, NH)
            with pe.Fori(0, KA0) as nb:
                units(nb, 0, 1, 2, 3)
            for nb in range(KA0, VA0):
                h = nb - KA0
                units(nb, 0)
                if h > 0:
                    transposes(nb - 1, h - 1)
                units(nb, 1)
                pe.wait_ge(up_in, 32 * (h + 1))
                pe.wait_ge(al_ok, 2)
                if h > 0:
                    pe.wait_ge(out_ready, nb)
                for i in range(2):
                    for j in range(NH):
                        last = nc.tensor.matmul(PS[:, 4 + 2 * i + j, :], wup[:, i * P:(i + 1) * P],
                                                alow[:, j * HALF:(j + 1) * HALF], start=True, stop=True)
                    last.then_inc(l_ready, 1)
                units(nb, 2, 3)
            units(VA0, 0)
            transposes(VA0 - 1, 3)
            units(VA0, 1, 2, 3)
            with pe.Fori(VA0 + 1, GA0 + 1) as nb:
                units(nb, 0)
                transposes(nb - 1, nb - (1 + KA0))
                units(nb, 1, 2, 3)
            with pe.Fori(GA0 + 1, OA0) as nb:
                units(nb, 0, 1, 2, 3)

            def gla_kv(t, i):
                h, c = i // 2, i % 2
                rows = slice(c * CHUNK, (c + 1) * CHUNK)
                n = 8 * t + i
                pe.wait_ge(qkv_in[h], 48 * (t + 1))
                if not isinstance(n, int) or n >= 2:
                    pe.wait_ge(st_up, n - 1)
                for k in range(2):
                    last = nc.tensor.matmul(PS[:, 2 * (i % 2) + k, :], gk[rows, h, k * P:(k + 1) * P],
                                            gv[rows, h, :], start=True, stop=True)
                last.then_inc(kv_pe, 1)

            def gla_o(t, i):
                h, c = i // 2, i % 2
                rows = slice(c * CHUNK, (c + 1) * CHUNK)
                n = 8 * t + i
                pe.wait_ge(st_up, n + 1)
                if not isinstance(n, int) or n >= 4:
                    pe.wait_ge(o_nm, 4 * t + h - 1)
                for k in range(2):
                    last = nc.tensor.matmul(PS[rows, 4 + h % 2, :], gq[:, h, k, rows], state[:, h, k],
                                            start=k == 0, stop=k == 1)
                last.then_inc(o_pe, 1)

            def gla_tr(t, h):
                n = 4 * t + h
                pe.wait_ge(o_nm, n + 1)
                if not isinstance(n, int) or n >= 2:
                    pe.wait_ge(o_gt, n - 1)
                for k in range(4):
                    last = nc.tensor.transpose(PS[:, 6 + h % 2, k * P:(k + 1) * P], onrm[:, k * P:(k + 1) * P],
                                               ident[:, :])
                last.then_inc(o_tr, 1)

            def gla_pe(t):
                gla_kv(t, 0)
                for i in range(8):
                    if i < 7:
                        gla_kv(t, i + 1)
                    gla_o(t, i)
                    if i % 2 == 0 and i > 0:
                        gla_tr(t, i // 2 - 1)
                gla_tr(t, GH - 1)

            gla_pe(0)
            with pe.Fori(1, ST) as t:
                gla_pe(t)

            pe.wait_ge(o_lo, 4 * ST)
            with pe.Fori(OA0, KV0) as nb:
                units(nb, 0, 1, 2, 3)
            unit(KV0, 0, ready=(r_lo, 2))
            unit(KV0, 1, ready=(r_lo, 4))
            pe.wait_ge(sum_ok, 2 * (D // BC) + 1)
            for j in range(NH):
                last = nc.tensor.matmul(PS[:, 4 + j, :], ones[:, :], sqsum[:, j * HALF:(j + 1) * HALF],
                                        start=True, stop=True)
            last.then_inc(ss_pe, 1)
            unit(KV0, 2, ready=(r_lo, 6))
            unit(KV0, 3, ready=(r_lo, 8))
            units(KV0 + 1, 0)
            head_sums(0, D // BC + 1)
            units(KV0 + 1, 1, 2, 3)
            units(QB0, 0)
            transposes(KV0 + 1, 12)
            units(QB0, 1, 2, 3)
            with pe.Fori(QB0 + 1, GB0 + 1) as nb:
                units(nb, 0)
                head_sums(nb - QB0, nb - QB0 + D // BC + 1)
                units(nb, 1, 2, 3)
            with pe.Fori(GB0 + 1, OB0) as nb:
                units(nb, 0, 1, 2, 3)

            def att_scores(t, i, first):
                n = 8 * t + i
                h, c = i // 2, i % 2
                lo = 64 if first and c == 0 else 0
                if c == 0:
                    pe.wait_ge(att_in[h], 112 * (t + 1))
                if not (first and i < 2):
                    pe.wait_ge(s_sub, n - 1)
                for a in range(2):
                    rows = slice(a * HD, (a + 1) * HD)
                    for j in range(2):
                        last = nc.tensor.matmul(PS[:, 2 * (i % 2) + a, j * P + lo:(j + 1) * P],
                                                sq_[rows, h, c, 2 * j:2 * j + 2, :].rearrange("p i s -> p (i s)"),
                                                sk_[rows, h, c * CHUNK + lo:c * CHUNK + P], start=True, stop=True)
                last.then_inc(s_pe, 1)

            def att_tr(t, i, first):
                n = 8 * t + i
                pe.wait_ge(s_pr, n + 1)
                if not (first and i < 2):
                    pe.wait_ge(s_cp, n - 1)
                for g in range(4):
                    last = nc.tensor.transpose(PS[:, 4 + i % 2, g * P:(g + 1) * P], pr_[:, i % 2, g, :], ident[:, :])
                last.then_inc(s_tr, 1)

            def att_pv(t, i, first):
                n = 8 * t + i
                h, c = i // 2, i % 2
                pe.wait_ge(s_cp, n + 1)
                if not (first and i < 2):
                    pe.wait_ge(s_gt, n - 1)
                for a in range(2):
                    last = nc.tensor.matmul(PS[a * HD:(a + 1) * HD, 6 + i % 2, 0:256], sv_[:, h, c, :],
                                            pt_[:, i % 2, a, :], start=True, stop=True)
                last.then_inc(s_pv, 1)

            def att_pe(t, first):
                for s in range(10):
                    if s < 8:
                        att_scores(t, s, first)
                    if 1 <= s <= 8:
                        att_tr(t, s - 1, first)
                    if s >= 2:
                        att_pv(t, s - 2, first)

            pe.wait_ge(s_zero, 2)
            att_pe(0, True)
            with pe.Fori(1, ST) as t:
                att_pe(t, False)

            pe.wait_ge(s_lo, 8 * ST)
            units(OB0, 0, 1, 2, 3)
            with pe.Fori(OB0 + 1, END) as nb:
                units(nb, 0)
                transposes(nb - 1, nb)
                units(nb, 1, 2, 3)
            transposes(END - 1, END)


_INS = ['x', 'a_norm', 'a_w_in', 'a_w_alpha_up', 'a_b_alpha', 'a_out_norm', 'a_w_out', 'kv_norm', 'w_kv', 'k_norm',
        'b_norm', 'b_w_in', 'b_q_norm', 'b_sinks', 'b_w_out']


def kernel(**inputs):
    import numpy as _np
    import concourse.bacc as _bacc
    from concourse import mybir as _mybir
    from concourse.bass_utils import run_bass_kernel_spmd as _run

    nc = _bacc.Bacc("TRN2", target_bir_lowering=False, num_devices=1)
    arrays, args = {}, []
    for name in _INS:
        a = _np.ascontiguousarray(inputs[name])
        arrays[f"in_{name}_dram"] = a
        args.append(nc.dram_tensor(f"in_{name}_dram", a.shape, _mybir.dt.from_np(a.dtype), kind="ExternalInput").ap())
    shape = _np.asarray(inputs['x']).shape
    args.append(nc.dram_tensor("out_0_dram", shape, _mybir.dt.float32, kind="ExternalOutput").ap())
    trunk_kernel(nc, *args)
    r = _run(nc, [arrays], core_ids=[0])
    return r.results[0]["out_0_dram"]
```

```python
import concourse.bass as bass
from concourse import mybir
from contextlib import ExitStack

F32 = mybir.dt.float32
F32R = mybir.dt.float32r
ALU = mybir.AluOpType
ACT = mybir.ActivationFunctionType
AX = mybir.AxisListType


def trunk_kernel(nc, x, a_norm, a_w_in, a_w_alpha_up, a_b_alpha, a_out_norm, a_w_out,
                 kv_norm, w_kv, k_norm, b_norm, b_w_in, b_q_norm, b_sinks, b_w_out, out):
    P = 128
    SEQ, D = x.shape[1], x.shape[2]
    KT = D // P
    ST = SEQ // P
    HALF = 512
    NH = SEQ // HALF
    UK, BC = 4, 256
    NU = KT // UK
    CT = BC // P
    CHUNK = 64
    GH, DK, DV = 4, 256, 512
    RANK = a_w_alpha_up.shape[1]
    TAU = 16.0
    HD = 64
    KVH = 4
    QCT = 4
    EPS = 1e-6
    NQ, NK_, NV_, NG_ = GH * DK // BC, GH * DK // BC, GH * DV // BC, GH * DV // BC
    KA0 = NQ
    VA0 = KA0 + NK_
    GA0 = VA0 + NV_
    OA0 = GA0 + NG_
    KV0 = OA0 + D // BC
    QB0 = KV0 + 2
    GB0 = QB0 + D // BC
    OB0 = GB0 + D // BC
    END = OB0 + D // BC

    def scratch(name, shape):
        return nc.dram_tensor(name, shape, F32).ap()

    xT_s = scratch("xT_s", [D, SEQ])
    qa_s = scratch("qa_s", [GH * DK, SEQ])
    ka_s = scratch("ka_s", [SEQ, GH * DK])
    va_s = scratch("va_s", [SEQ, GH * DV])
    ga_s = scratch("ga_s", [GH * DV, SEQ])
    x1_s = scratch("x1_s", [D, SEQ])
    kb_s = scratch("kb_s", [KVH * HD, SEQ])
    vb_s = scratch("vb_s", [SEQ, KVH * HD])
    qb_s = scratch("qb_s", [D // BC, P, CT * SEQ])
    ob_s = scratch("ob_s", [D, SEQ])

    x2d, out2d = x[0], out[0]

    ctx = ExitStack()
    with ctx:
        def sb(name, shape, dt=F32):
            return ctx.enter_context(nc.sbuf_tensor(name, shape, dt))

        def sem(name):
            return ctx.enter_context(nc.semaphore(name))

        XH = sb("XH", [P, KT, SEQ], F32R)
        XL = sb("XL", [P, KT, SEQ], F32R)
        WRAW = sb("WRAW", [P, NU, UK, BC])
        WHI = sb("WHI", [P, 2, UK, BC], F32R)
        WLO = sb("WLO", [P, 2, UK, BC], F32R)
        RSTD = sb("RSTD", [P, SEQ])
        WORK = sb("WORK", [P, 10240])
        ident = sb("ident", [P, P])
        pair = sb("pair", [P, P])
        ones = sb("ones", [P, P])
        NR = 3 * KT + DV // P + GH * DK // P + 2
        vrows = sb("vrows", [NR, P])
        vcols = sb("vcols", [P, NR])
        g_a, g_kv, g_b = (vcols[:, i * KT:(i + 1) * KT] for i in range(3))
        g_o = vcols[:, 3 * KT:3 * KT + DV // P]
        b_al = vcols[:, 3 * KT + DV // P:NR - 2]
        srow = sb("srow", [1, KVH * 8])
        kgain = sb("kgain", [P, 1])
        sinks = sb("sinks", [P, D // BC, 4])
        nsinks = sb("nsinks", [P, D // BC, 4])
        dc = sb("dc", [P, GH * DK // P, SEQ // CHUNK])
        wa = WRAW[:, 3, 0, :].rearrange("p (k r) -> p k r", r=RANK)
        ssq = sb("ssq", [P, ST])
        eps_t = sb("eps_t", [P, 1])
        st1 = sb("st1", [P, 8])
        mhalf = sb("mhalf", [P, 4])
        st2 = sb("st2", [P, 2, 8, 4])

        PS = ctx.enter_context(nc.psum_tensor("PS", [P, 8, 512], F32))

        xin = WORK[:, 0:4 * D].rearrange("p (n d) -> p n d", n=4)
        xraw = WORK[:, 8192:10240].rearrange("p (n k s) -> p n k s", n=4, k=4)
        stageT = WORK[:, 0:2048].rearrange("p (i s) -> p i s", i=CT)
        stageN = WORK[:, 2048:4096].rearrange("p (s c) -> p s c", s=ST)
        stageX = WORK[:, 0:2048].rearrange("p (x i s) -> p x i s", x=SEQ // CHUNK, i=CT)
        reload_ = WORK[:, 2048:4096].rearrange("p (n s) -> p n s", n=2)
        bufA = WORK[:, 4096:6144].rearrange("p (i s) -> p i s", i=CT)
        bufB = WORK[:, 6144:8192].rearrange("p (i s) -> p i s", i=CT)
        alow = WORK[0:64, 8192:9216]
        wup = WORK[0:64, 9216:9216 + BC]
        sqsum = WORK[:, 8192:9216]
        state = WORK[:, 0:4096].rearrange("p (h i v) -> p h i v", h=GH, i=2)
        gq = WORK[:, 4096:5120].rearrange("p (h i s) -> p h i s", h=GH, i=2)
        gk = WORK[:, 5120:6144].rearrange("p (h k) -> p h k", h=GH)
        gv = WORK[:, 6144:8192].rearrange("p (h v) -> p h v", h=GH)
        gg = WORK[:, 8192:9216].rearrange("p (n i s) -> p n i s", n=2, i=4)
        onrm = WORK[:, 9216:9728]
        ogate = WORK[:, 9728:10240]
        aq = [WORK[:, at:at + 2048].rearrange("p (t c x) -> p t c x", t=ST, c=2) for at in (2048, 4096)]
        ae = WORK[:, 6144:7168].rearrange("p (n g k) -> p n g k", n=2, g=4)
        apt = WORK[:, 7168:7680].rearrange("p (g r) -> p g r", g=4)
        aq2 = WORK[:, 7680:8192].rearrange("p (n c x) -> p n c x", n=2, c=2)
        ak = WORK[:, 8192:9216]
        av = WORK[:, 9216:10240].rearrange("p (c t d) -> p c t d", c=2, t=ST)

        v_pe = sem("v_pe")
        v_ok = sem("v_ok")
        consts_in = sem("consts_in")
        zeroed = sem("zeroed")
        x_in = [sem(f"x_in{i}") for i in range(4)]
        x_tr = sem("x_tr")
        x_hi = sem("x_hi")
        x_cp = sem("x_cp")
        x_lo = sem("x_lo")
        x_sq = sem("x_sq")
        x_st = [sem(f"x_st{i}") for i in range(4)]
        ss_pe = sem("ss_pe")
        ms_rt = sem("ms_rt")
        rstd_ok = sem("rstd_ok")
        wa_sc = sem("wa_sc")
        wa_hi = sem("wa_hi")
        wa_lo = sem("wa_lo")
        al_pe = sem("al_pe")
        al_ok = sem("al_ok")
        w_in = [sem(f"w_in{i}") for i in range(NU)]
        w_hi = sem("w_hi")
        w_lo = sem("w_lo")
        unit_used = sem("unit_used")
        acc_ready = sem("acc_ready")
        acc_free = sem("acc_free")
        out_ready = sem("out_ready")
        stored = sem("stored")
        silu_in = sem("silu_in")
        t_ready = sem("t_ready")
        t_free = sem("t_free")
        sq_done = sem("sq_done")
        n_ready = sem("n_ready")
        n_root = sem("n_root")
        n_dve = sem("n_dve")
        up_in = sem("up_in")
        l_ready = sem("l_ready")
        l_abs = sem("l_abs")
        l_log = sem("l_log")
        l_dve = sem("l_dve")
        l_cum = sem("l_cum")
        l_exp = sem("l_exp")
        l_ok = sem("l_ok")
        res_in = sem("res_in")
        sum_ok = sem("sum_ok")
        rel_in = [sem(f"rel_in{i}") for i in range(2)]
        r_hi = sem("r_hi")
        r_lo = sem("r_lo")
        s_zero = sem("s_zero")
        qkv_in = [sem(f"qkv_in{i}") for i in range(GH)]
        gg_in = [sem(f"gg_in{i}") for i in range(2)]
        kv_pe = sem("kv_pe")
        st_up = sem("st_up")
        o_pe = sem("o_pe")
        o_ss = sem("o_ss")
        o_rt = sem("o_rt")
        o_rc = sem("o_rc")
        o_nm = sem("o_nm")
        o_tr = sem("o_tr")
        o_gt = sem("o_gt")
        o_hi = sem("o_hi")
        o_lo = sem("o_lo")
        q_in = [sem(f"q_in{i}") for i in range(2)]
        k_in = [sem(f"k_in{i}") for i in range(2)]
        va_in = [sem(f"va_in{i}") for i in range(2)]
        a_vz = sem("a_vz")
        a_q2 = sem("a_q2")
        a_pe = sem("a_pe")
        a_ms = sem("a_ms")
        a_rq = sem("a_rq")
        a_mx = sem("a_mx")
        a_nm = sem("a_nm")
        a_ex = sem("a_ex")
        a_ez = sem("a_ez")
        a_sm = sem("a_sm")
        a_rc = sem("a_rc")
        a_pr = sem("a_pr")
        a_tr = sem("a_tr")
        a_cp = sem("a_cp")
        a_pv = sem("a_pv")
        a_oc = sem("a_oc")
        silu_b = sem("silu_b")

        NCONST = 11

        LEAD = 4

        def item(h, e, s, back):
            v = s + LEAD - back
            e2, t = e + v // 8, v % 8
            hh, ee = h + e2 // 2, e2 % 2
            if isinstance(h, int) and not 0 <= 2 * hh + ee < D // BC:
                return None
            return hh, ee, t, 16 * hh + 8 * ee + t

        block = ctx.enter_context(nc.Block())

        def weights(w, b, u):
            return w[u * UK * P:(u + 1) * UK * P, bass.ds(b * BC, BC)].rearrange("(k p) c -> p k c", p=P)

        wa_in_w, wa_out_w, wb_in_w, wb_out_w = a_w_in[0], a_w_out[0], b_w_in[0], b_w_out[0]

        @block.sync
        def _(sp):
            def load_w(w, nb, b, first=False):
                for u in range(NU):
                    load_unit(w, nb, b, u, first)

            def load_unit(w, nb, b, u, first=False):
                if not first:
                    sp.wait_ge(w_lo, (nb - 1) * NU + u + 1)
                sp.dma_start(WRAW[:, u], weights(w, b, u)).then_inc(w_in[u], 16)

            def store_T(dst, nb, b):
                sp.wait_ge(out_ready, nb + 1)
                sp.dma_start(dst[bass.ds(b * BC, BC), :].rearrange("(i p) s -> p i s", p=P),
                             stageT).then_inc(stored, 16)

            def store_N(dst, nb, b):
                sp.wait_ge(out_ready, nb + 1)
                sp.dma_start(dst[:, bass.ds(b * BC, BC)].rearrange("(s p) c -> p s c", p=P),
                             stageN).then_inc(stored, 16)

            def store_x(i):
                t, q = i // 4, i % 4
                sp.wait_ge(x_cp, i + 1)
                sp.dma_start(xT_s[q * 4 * P:(q + 1) * 4 * P, t * P:(t + 1) * P].rearrange("(k p) s -> p k s", p=P),
                             xraw[:, i % 4]).then_inc(x_st[i % 4], 16)

            for t in range(4):
                sp.dma_start(xin[:, t], x2d[t * P:(t + 1) * P, :]).then_inc(x_in[t], 16)
            at = 0
            for v in (a_norm[0], kv_norm, b_norm[0], a_out_norm[0], a_b_alpha[0]):
                n = v.shape[0] // P
                sp.dma_start(vrows[at:at + n, :], v.rearrange("(k p) -> k p", p=P)).then_inc(consts_in, 16)
                at += n
            for v in (k_norm, b_q_norm[0]):
                for half in range(2):
                    sp.dma_start(vrows[at:at + 1, half * HD:(half + 1) * HD],
                                 v.rearrange("(o p) -> o p", o=1)).then_inc(consts_in, 16)
                at += 1
            sp.dma_start(srow[:, :], b_sinks).then_inc(consts_in, 16)
            sp.dma_start(wa[:, :, :], wa_in_w[:, OA0 * BC:].rearrange("(k p) r -> p k r", p=P)
                         ).then_inc(consts_in, 16)
            for u in range(3):
                load_unit(wa_in_w, 0, 0, u, first=True)
            for t in range(4, ST):
                sp.wait_ge(x_sq, t - 3)
                sp.dma_start(xin[:, t % 4], x2d[t * P:(t + 1) * P, :]).then_inc(x_in[t % 4], 16)
                for i in range(4 * (t - 4), 4 * (t - 3)):
                    store_x(i)
                if t == 6:
                    sp.wait_ge(wa_lo, 1)
                    load_unit(wa_in_w, 0, 0, 3, first=True)
            for i in range(4 * (ST - 4), 4 * ST):
                store_x(i)

            with sp.Fori(1, KA0) as nb:
                load_w(wa_in_w, nb, nb)
                store_T(qa_s, nb - 1, nb - 1)
            for nb in range(KA0, VA0):
                load_w(wa_in_w, nb, nb)
                if nb > KA0:
                    sp.wait_ge(l_ready, 2 * (nb - KA0))
                else:
                    sp.wait_ge(al_ok, 2)
                for r in range(2):
                    sp.dma_start(wup[32 * r:32 * r + RANK, :],
                                 a_w_alpha_up[0][:, (nb - KA0) * DK:(nb - KA0 + 1) * DK]).then_inc(up_in, 16)
                if nb == KA0:
                    store_T(qa_s, nb - 1, nb - 1)
                else:
                    store_N(ka_s, nb - 1, nb - 1 - KA0)
            load_w(wa_in_w, VA0, VA0)
            store_N(ka_s, VA0 - 1, VA0 - 1 - KA0)
            with sp.Fori(VA0 + 1, GA0 + 1) as nb:
                load_w(wa_in_w, nb, nb)
                store_N(va_s, nb - 1, nb - (1 + VA0))
            with sp.Fori(GA0 + 1, OA0) as nb:
                load_w(wa_in_w, nb, nb)
                store_T(ga_s, nb - 1, nb - (1 + GA0))
            load_w(wa_out_w, OA0, 0)
            store_T(ga_s, OA0 - 1, NG_ - 1)

            sp.wait_ge(stored, 16 * OA0)

            def load_head(t, h, first):
                if not first:
                    sp.wait_ge(o_pe, 8 * (t - 1) + 2 * h + 2)
                else:
                    sp.wait_ge(s_zero, 1)
                sp.dma_start(gq[:, h], qa_s[h * DK:(h + 1) * DK, bass.ds(t * P, P)]
                             .rearrange("(i p) s -> p i s", p=P)).then_inc(qkv_in[h], 16)
                sp.dma_start(gk[:, h], ka_s[bass.ds(t * P, P), h * DK:(h + 1) * DK]).then_inc(qkv_in[h], 16)
                sp.dma_start(gv[:, h], va_s[bass.ds(t * P, P), h * DV:(h + 1) * DV]).then_inc(qkv_in[h], 16)
                if not (first and h < 2):
                    sp.wait_ge(o_gt, 4 * t + h - 1)
                sp.dma_start(gg[:, h % 2], ga_s[h * DV:(h + 1) * DV, bass.ds(t * P, P)]
                             .rearrange("(i p) s -> p i s", p=P)).then_inc(gg_in[h % 2], 16)

            for h in range(GH):
                load_head(0, h, True)
            with sp.Fori(1, ST) as t:
                for h in range(GH):
                    load_head(t, h, False)

            def load_res(src, nb, b, first, work_free=None):
                if first:
                    sp.wait_ge(*work_free)
                else:
                    sp.wait_ge(acc_free, (nb + 1) * 4)
                sp.dma_start(bufA, src[bass.ds(b * BC, BC), :].rearrange("(i p) s -> p i s", p=P)
                             ).then_inc(res_in, 16)

            load_res(xT_s, OA0, 0, True, (o_lo, 4 * ST))
            with sp.Fori(OA0 + 1, KV0) as nb:
                load_w(wa_out_w, nb, nb - OA0)
                load_res(xT_s, nb, nb - OA0, False)
                store_T(x1_s, nb - 1, nb - (1 + OA0))
            def reload_tiles(src, base, loads, w, nb):
                sp.wait_ge(stored, 16 * (nb - 1))
                for kt in range(KT - 2):
                    if kt >= 2:
                        sp.wait_ge(r_lo, base + kt - 1)
                    sp.dma_start(reload_[:, kt % 2], src[kt * P:(kt + 1) * P, :]).then_inc(rel_in[kt % 2], 16)
                    if kt in loads:
                        load_unit(w, nb, 0, loads.index(kt))

            reload_tiles(x1_s, 0, (0, 1, 5, 9), w_kv, KV0)
            store_T(x1_s, KV0 - 1, 7)
            load_w(w_kv, KV0 + 1, 1)
            store_T(kb_s, KV0, 0)
            load_w(wb_in_w, QB0, 0)
            store_N(vb_s, KV0 + 1, 0)
            def store_q(nb):
                sp.wait_ge(out_ready, nb + 1)
                sp.dma_start(qb_s[bass.ds(nb - QB0, 1)].rearrange("o p x -> p (o x)"), WORK[:, 0:2048]
                             ).then_inc(stored, 16)

            def load_q(b, e):
                sp.dma_start(aq[e].rearrange("p t c x -> p (t c x)"),
                             qb_s[bass.ds(b, 1)].rearrange("o p x -> p (o x)")).then_inc(q_in[e], 16)

            def load_k(h, half):
                cols = slice(half * HALF, (half + 1) * HALF)
                for a in range(2):
                    sp.dma_start(ak[a * HD:(a + 1) * HD, cols], kb_s[bass.ds(h * HD, HD), cols]
                                 ).then_inc(k_in[half], 16)

            def load_v(h, half, ahead=0):
                cols = bass.ds(h * HD + ahead * HD, HD)
                sp.dma_start(av[:, 1, 4 * half:4 * half + 4],
                             vb_s[half * HALF:(half + 1) * HALF, cols].rearrange("(t p) d -> p t d", p=P)
                             ).then_inc(va_in[half], 16)
                if half == 0:
                    sp.dma_start(av[64:128, 0, 0], vb_s[0:64, cols]).then_inc(va_in[0], 16)
                first = 1 if half == 0 else 4
                sp.dma_start(av[:, 0, first:4 * half + 4],
                             vb_s[first * P - 64:(half + 1) * HALF - 64, cols].rearrange("(t p) d -> p t d", p=P)
                             ).then_inc(va_in[half], 16)

            with sp.Fori(QB0 + 1, GB0 - 1) as nb:
                load_w(wb_in_w, nb, nb - QB0)
                store_q(nb - 1)
            load_w(wb_in_w, GB0 - 1, GB0 - 1 - QB0)
            sp.wait_ge(stored, 16 * (GB0 - 2))
            load_q(0, 0)
            load_q(1, 1)
            for half in range(2):
                load_k(0, half)
                load_v(0, half)
            store_q(GB0 - 2)
            load_w(wb_in_w, GB0, GB0 - QB0)
            store_q(GB0 - 1)

            def next_block(nb, h, e, w, b, more):
                n = 16 * h + 8 * e
                head = e == 1 and more
                load_unit(w, nb, b, 0)
                load_unit(w, nb, b, 1)
                if not (isinstance(h, int) and h == 0 and e == 0):
                    sp.wait_ge(out_ready, nb - 1)
                    sp.wait_ge(stored, 16 * nb - 32)
                    if more or e == 0:
                        load_q(2 * h + e + 1, 1 - e)
                    store_T(ob_s, nb - 2, nb - (2 + GB0))
                if head:
                    sp.wait_ge(a_pe, n + 5)
                    load_k(h + 1, 0)
                load_unit(w, nb, b, 2)
                if head:
                    sp.wait_ge(a_pv, n + 4)
                    load_v(h, 0, 1)
                    sp.wait_ge(a_pe, n + 8)
                    load_k(h + 1, 1)
                load_unit(w, nb, b, 3)
                if head:
                    sp.wait_ge(a_pv, n + 8)
                    load_v(h, 1, 1)

            next_block(GB0 + 1, 0, 0, wb_in_w, GB0 + 1 - QB0, True)
            next_block(GB0 + 2, 0, 1, wb_in_w, GB0 + 2 - QB0, True)
            with sp.Fori(1, KVH - 1) as h:
                for e in range(2):
                    next_block(2 * h + (GB0 + 1 + e), h, e, wb_in_w, 2 * h + (GB0 - QB0 + 1 + e), True)
            next_block(OB0 - 1, KVH - 1, 0, wb_in_w, OB0 - 1 - QB0, False)
            sp.wait_ge(out_ready, OB0 - 1)
            store_T(ob_s, OB0 - 2, D // BC - 2)
            reload_tiles(ob_s, KT, (0, 1, 5, 9), wb_out_w, OB0)
            store_T(ob_s, OB0 - 1, D // BC - 1)

            load_res(x1_s, OB0, 0, True, (out_ready, OB0))
            with sp.Fori(OB0 + 1, END) as nb:
                load_w(wb_out_w, nb, nb - OB0)
                load_res(x1_s, nb, nb - OB0, False)
                store_N(out2d, nb - 1, nb - (1 + OB0))
            store_N(out2d, END - 1, D // BC - 1)
            sp.wait_ge(stored, 16 * END)

        @block.gpsimd
        def _(pool):
            nc.gpsimd.memset(ident[:, :], 0.0).then_inc(zeroed, 1)
            nc.gpsimd.memset(ones[:, :], 1.0).then_inc(zeroed, 1)
            nc.gpsimd.memset(pair[:, :], 1.0).then_inc(zeroed, 1)
            nc.gpsimd.memset(eps_t[:, :], EPS).then_inc(zeroed, 1)
            nc.gpsimd.memset(mhalf[:, :], -0.5).then_inc(zeroed, 1)
            pool.wait_ge(zeroed, 5)
            nc.gpsimd.affine_select(out=ident[:, :], in_=ident[:, :], compare_op=ALU.not_equal, fill=1.0, base=0,
                                    pattern=[[-1, P]], channel_multiplier=1).then_inc(zeroed, 1)
            nc.gpsimd.affine_select(out=pair[:, 64:128], in_=pair[:, 64:128], compare_op=ALU.is_ge, fill=0.0,
                                    base=-64, pattern=[[0, 64]], channel_multiplier=1).then_inc(zeroed, 1)
            nc.gpsimd.affine_select(out=pair[:, 0:64], in_=pair[:, 0:64], compare_op=ALU.is_ge, fill=0.0,
                                    base=63, pattern=[[0, 64]], channel_multiplier=-1).then_inc(zeroed, 1)
            for i in range(4 * ST):
                t, q = i // 4, i % 4
                pool.wait_ge(x_cp, i + 1)
                dst = (slice(None), slice(4 * q, 4 * q + 4), slice(t * P, (t + 1) * P))
                nc.gpsimd.tensor_tensor(XL[dst], xraw[:, i % 4], XH[dst].bitcast(F32), ALU.subtract
                                        ).then_inc(x_lo, 1)
            pool.wait_ge(o_lo, 4 * ST)
            nc.gpsimd.memset(sqsum, 0.0).then_inc(sum_ok, 1)
            with pool.Fori(OA0, KV0) as nb:
                for i in range(CT):
                    if i == 0:
                        pool.wait_ge(sq_done, nb - OA0 + 1)
                    pool.wait_ge(sum_ok, (nb - OA0) * 2 + i + 1)
                    nc.gpsimd.tensor_tensor(sqsum, sqsum, bufB[:, i], ALU.add).then_inc(sum_ok, 1)
            def squares(h, e, t, n):
                pool.wait_ge(q_in[e], 16 * h + 16)
                q = aq[e][:, t]
                nc.gpsimd.tensor_tensor(aq2[:, n_par(t)], q, q, ALU.mult).then_inc(a_q2, 1)

            def n_par(t):
                return t % 2

            def att_pool(h, e, s):
                last = item(h, e, s, 1)
                if last:
                    _, _, t, n = last
                    pool.wait_ge(a_rc, n + 1)
                    if t == 0:
                        pool.wait_ge(a_ez, zeros_of(last))
                    nc.gpsimd.tensor_tensor(ae[:, t % 2], ae[:, t % 2],
                                            st2[:, t % 2, 7].unsqueeze(2).to_broadcast([P, 4, P]),
                                            ALU.mult).then_inc(a_pr, 1)
                now = item(h, e, s, 0)
                if now:
                    _, _, t, n = now
                    pool.wait_ge(a_ms, n + 1)
                    nc.gpsimd.tensor_tensor(st2[:, t % 2, 1], st2[:, t % 2, 0], mhalf[:, :], ALU.pow
                                            ).then_inc(a_rq, 1)
                    if t == 0:
                        if not (isinstance(n, int) and n < 2):
                            pool.wait_ge(a_tr, n - 1)
                        one = ones[:, :].rearrange("p (a k) -> p a k", a=2)
                        nc.gpsimd.tensor_tensor(ae[:, 0].rearrange("p (a c) k -> p a c k", a=2)[:, :, 0, 0:CHUNK],
                                                one, one, ALU.subtract).then_inc(a_ez, 1)
                nxt = item(h, e, s, -1)
                if nxt:
                    squares(*nxt)

            def zeros_of(it):
                return 2 * it[0] + it[1] + 1

            pool.wait_ge(out_ready, QB0 + 1)
            pool.wait_ge(stored, 16 * (KV0 + 1))
            nc.gpsimd.memset(av[0:64, 0, 0], 0.0).then_inc(a_vz, 1)
            squares(0, 0, 0, 0)
            for s in range(4, 8):
                att_pool(-1, 1, s)
            with pool.Fori(0, KVH - 1) as h:
                for e in range(2):
                    for s in range(8):
                        att_pool(h, e, s)
            for e in range(2):
                for s in range(8):
                    att_pool(KVH - 1, e, s)

        @block.scalar
        def _(act):
            def split_hi(nb, u, gain):
                act.wait_ge(w_in[u], 16 * (nb + 1))
                if isinstance(nb, int) and nb == 0 and u < 2:
                    pass
                elif u == 1:
                    act.wait_ge(acc_ready, 4 * nb)
                elif u >= 2:
                    act.wait_ge(unit_used, 3 * nb + u - 1)
                else:
                    act.wait_ge(unit_used, 3 * nb)
                if gain is None:
                    nc.scalar.copy(WHI[:, u % 2], WRAW[:, u]).then_inc(w_hi, 1)
                    return
                for k in range(UK):
                    g = gain[:, (u * UK + k) % gain.shape[1]:(u * UK + k) % gain.shape[1] + 1]
                    last = nc.scalar.activation(WHI[:, u % 2, k], WRAW[:, u, k], ACT.Copy, scale=g)
                last.then_inc(w_hi, 1)

            def splits(nb, gain, *us):
                for u in us:
                    split_hi(nb, u, gain)

            def copy_T(nb, tb):
                for g in range(4):
                    act.wait_ge(t_ready, 4 * tb + g + 1)
                    last = nc.scalar.copy(stageN[:, 2 * g:2 * g + 2, :],
                                          PS[:, 4 + g, :].rearrange("p (s c) -> p s c", s=2))
                    if g < 3:
                        last.then_inc(t_free, 1)
                last.then_inc(out_ready, 1)

            def square(nb, k):
                act.wait_ge(acc_free, 4 * nb + 8)
                nc.scalar.activation(bufB, stageT, ACT.Square).then_inc(sq_done, 1)

            def roots(nb, k):
                for j in range(4):
                    act.wait_ge(n_ready, 4 * k + j + 1)
                    last = nc.scalar.activation(bufA[:, j // 2, (j % 2) * HALF:(j % 2 + 1) * HALF], PS[:, 4 + j, :],
                                                ACT.Sqrt, scale=1.0 / HD, bias=eps_t[:, 0:1])
                last.then_inc(n_root, 1)

            def silu(nb, k):
                act.wait_ge(acc_free, 4 * nb + 8)
                nc.scalar.activation(stageT, stageT, ACT.Silu).then_inc(out_ready, 1)

            act.wait_ge(zeroed, 8)
            for t in range(ST):
                for q in range(4):
                    i = 4 * t + q
                    act.wait_ge(x_tr, i + 1)
                    nc.scalar.copy(XH[:, 4 * q:4 * q + 4, t * P:(t + 1) * P],
                                   PS[:, 4 + i % 4, :].rearrange("p (k s) -> p k s", k=4)).then_inc(x_hi, 1)
                nc.scalar.activation(xin[:, t % 4], xin[:, t % 4], ACT.Square,
                                     accum_out=ssq[:, t:t + 1]).then_inc(x_sq, 1)
                if t == 0:
                    act.wait_ge(wa_sc, 3)
                    nc.scalar.copy(WHI[:, :, :, :].rearrange("p a k (b c) -> p (a k b) c", c=P)[:, :, 0:RANK],
                                   wa[:, :, :]).then_inc(wa_hi, 1)
            act.wait_ge(ss_pe, 1)
            for j in range(NH):
                nc.scalar.activation(RSTD[:, j * HALF:(j + 1) * HALF], PS[:, j, :], ACT.Sqrt,
                                     scale=1.0 / D, bias=eps_t[:, 0:1]).then_inc(ms_rt, 1)
            act.wait_ge(al_pe, 1)
            splits(0, g_a, 0)
            splits(0, g_a, 1, 2, 3)
            splits(1, g_a, 0)
            with act.Fori(1, KA0) as nb:
                splits(nb, g_a, 1, 2, 3)
                splits(nb + 1, g_a, 0)
            for nb in range(KA0, VA0):
                h = nb - KA0
                splits(nb, g_a, 1)
                if h > 0:
                    copy_T(nb - 1, h - 1)
                splits(nb, g_a, 2, 3)
                for i in range(2):
                    n = 2 * h + i
                    e = bufA[:, 1]
                    act.wait_ge(l_abs, n + 1)
                    nc.scalar.activation(e, e, ACT.Exp).then_inc(l_log, 1)
                    act.wait_ge(l_log, 3 * n + 1)
                    nc.scalar.activation(e, e, ACT.Ln, bias=ones[:, 0:1]).then_inc(l_log, 1)
                    act.wait_ge(l_cum, n + 1)
                    nc.scalar.activation(bufB[:, i], bufB[:, i], ACT.Exp, scale=1.0 / TAU).then_inc(l_exp, 1)
                    nc.scalar.activation(dc[:, n, :], bufA[:, 1].rearrange("p (c s) -> p c s", s=CHUNK)[:, :, CHUNK - 1],
                                         ACT.Exp, scale=1.0 / TAU).then_inc(l_log, 1)
                splits(nb + 1, g_a, 0)
            splits(VA0, g_a, 1)
            copy_T(VA0 - 1, 3)
            splits(VA0, g_a, 2, 3)
            splits(VA0 + 1, g_a, 0)
            with act.Fori(VA0 + 1, GA0) as nb:
                splits(nb, g_a, 1)
                copy_T(nb - 1, nb - (1 + KA0))
                splits(nb, g_a, 2, 3)
                splits(nb + 1, g_a, 0)
            splits(GA0, g_a, 1)
            copy_T(GA0 - 1, GA0 - 1 - KA0)
            splits(GA0, g_a, 2, 3)
            splits(GA0 + 1, g_a, 0)
            silu(GA0, 0)
            with act.Fori(GA0 + 1, OA0 - 1) as nb:
                splits(nb, g_a, 1, 2, 3)
                splits(nb + 1, g_a, 0)
                silu(nb, nb - GA0)
            splits(OA0 - 1, g_a, 1, 2, 3)
            splits(OA0, g_o, 0)
            silu(OA0 - 1, NG_ - 1)

            def gla_out(t, h):
                n = 4 * t + h
                act.wait_ge(o_pe, 8 * t + 2 * h + 2)
                if not isinstance(n, int) or n >= 1:
                    act.wait_ge(o_tr, n)
                nc.scalar.activation(onrm, PS[:, 4 + h % 2, :], ACT.Square,
                                     accum_out=st1[:, h:h + 1]).then_inc(o_ss, 1)
                act.wait_ge(o_ss, n + 1)
                nc.scalar.activation(st1[:, h:h + 1], st1[:, h:h + 1], ACT.Sqrt, scale=1.0 / DV,
                                     bias=eps_t[:, 0:1]).then_inc(o_rt, 1)
                act.wait_ge(o_rc, n + 1)
                nc.scalar.activation(onrm, PS[:, 4 + h % 2, :], ACT.Copy,
                                     scale=st1[:, 4 + h:5 + h]).then_inc(o_nm, 1)

            def gla_hi(t, h):
                n = 4 * t + h
                act.wait_ge(o_gt, n + 1)
                nc.scalar.copy(XH[:, 4 * h:4 * h + 4, bass.ds(t * P, P)],
                               ogate.rearrange("p (i s) -> p i s", i=4)).then_inc(o_hi, 1)

            def gla_act(t):
                for h in range(GH):
                    gla_out(t, h)
                    gla_hi(t, h)

            gla_act(0)
            with act.Fori(1, ST) as t:
                gla_act(t)

            with act.Fori(OA0, KV0 - 1) as nb:
                splits(nb, g_o, 1, 2, 3)
                splits(nb + 1, g_o, 0)
                act.wait_ge(sum_ok, (nb - OA0) * 2 + 1)
                square(nb, nb - OA0)
                act.wait_ge(sq_done, nb - (OA0 - 1))
                nc.scalar.copy(eps_t[:, 0:1], eps_t[:, 0:1]).then_inc(out_ready, 1)
            nb = KV0 - 1

            def tiles_hi(base, nb, kts):
                for kt in kts:
                    if kt // UK < NU - 1:
                        act.wait_ge(unit_used, 3 * nb + kt // UK + 1)
                    else:
                        act.wait_ge(acc_ready, 4 * nb + 4)
                    if kt < KT - 2:
                        act.wait_ge(rel_in[kt % 2], (112 if base else 0) + 16 * (kt // 2 + 1))
                        src = reload_[:, kt % 2]
                    else:
                        src = stageT[:, kt % 2]
                    nc.scalar.copy(XH[:, kt, :], src).then_inc(r_hi, 1)

            splits(nb, g_o, 1, 2)
            tiles_hi(0, nb, range(0, 4))
            splits(nb, g_o, 3)
            tiles_hi(0, nb, range(4, 8))
            splits(KV0, g_kv, 0)
            tiles_hi(0, nb, range(8, 12))
            act.wait_ge(sum_ok, (nb - OA0) * 2 + 1)
            square(nb, nb - OA0)
            act.wait_ge(sq_done, nb - (OA0 - 1))
            nc.scalar.copy(eps_t[:, 0:1], eps_t[:, 0:1]).then_inc(out_ready, 1)
            splits(KV0, g_kv, 1)
            tiles_hi(0, nb, range(12, 16))
            splits(KV0, g_kv, 2)
            act.wait_ge(ss_pe, 2)
            for j in range(NH):
                nc.scalar.activation(RSTD[:, j * HALF:(j + 1) * HALF], PS[:, 4 + j, :], ACT.Sqrt,
                                     scale=1.0 / D, bias=eps_t[:, 0:1]).then_inc(ms_rt, 1)
            splits(KV0, g_kv, 3)
            splits(KV0 + 1, g_kv, 0)
            square(KV0, 8)
            splits(KV0 + 1, g_kv, 1)
            roots(KV0, 0)
            splits(KV0 + 1, g_kv, 2, 3)
            splits(QB0, g_b, 0)
            splits(QB0, g_b, 1)
            copy_T(KV0 + 1, NK_ + NV_)
            splits(QB0, g_b, 2, 3)
            splits(QB0 + 1, g_b, 0)
            with act.Fori(QB0 + 1, GB0 - 1) as nb:
                splits(nb, g_b, 1, 2, 3)
                splits(nb + 1, g_b, 0)

            def att_act(h, e, s):
                it = item(h, e, s, 3)
                if it:
                    _, e2, t, n = it
                    act.wait_ge(a_pv, n + 1)
                    nc.scalar.copy(aq[e2][:, t], PS[:, 7, 0:256].rearrange("p (c x) -> p c x", c=2)
                                   ).then_inc(a_oc, 1)
                it = item(h, e, s, 2)
                if it:
                    _, _, t, n = it
                    act.wait_ge(a_tr, n + 1)
                    if not (isinstance(n, int) and n == 0):
                        act.wait_ge(a_pv, n)
                    nc.scalar.copy(apt, PS[:, 6, :].rearrange("p (g r) -> p g r", g=4)).then_inc(a_cp, 1)
                it = item(h, e, s, 0)
                if it:
                    _, _, t, n = it
                    i = t % 2
                    act.wait_ge(a_nm, n + 1)
                    if not (isinstance(n, int) and n < 2):
                        act.wait_ge(a_tr, n - 1)
                    for a in range(2):
                        for c in range(2):
                            g, lo = 2 * a + c, (CHUNK if t == 0 and c == 0 else 0)
                            nc.scalar.activation(ae[:, i, g, lo:], PS[:, 4 + a, c * P + lo:(c + 1) * P], ACT.Exp,
                                                 scale=st2[:, i, 1, g:g + 1], bias=st2[:, i, 4, g:g + 1],
                                                 accum_out=st2[:, i, 6, g:g + 1])
                    nc.scalar.activation(st2[:, i, 5], st2[:, i, 5], ACT.Exp).then_inc(a_ex, 1)

            def g_block(nb, h, e, last=False):
                for u in range(NU):
                    if u < NU - 1:
                        splits(nb, g_b, u + 1)
                    else:
                        splits(nb + 1, None if last else g_b, 0)
                    for i in range(2):
                        att_act(h, e, 2 * u + i)
                        if last and u > 0:
                            tiles_hi(KT, nb, range(UK * (u - 1) + 2 * i, UK * (u - 1) + 2 * i + 2))
                act.wait_ge(acc_free, 4 * nb + 8)
                nc.scalar.activation(stageT, stageT, ACT.Silu).then_inc(silu_b, 1)

            splits(GB0 - 1, g_b, 1, 2, 3)
            for i in range(2):
                att_act(-1, 1, 4 + i)
            splits(GB0, g_b, 0)
            for i in range(2):
                att_act(-1, 1, 6 + i)
            with act.Fori(0, KVH - 1) as h:
                for e in range(2):
                    g_block(2 * h + (GB0 + e), h, e)
            g_block(OB0 - 2, KVH - 1, 0)
            g_block(OB0 - 1, KVH - 1, 1, last=True)
            tiles_hi(KT, OB0 - 1, range(12, 14))
            splits(OB0, None, 1)
            act.wait_ge(out_ready, OB0)
            tiles_hi(KT, OB0 - 1, range(14, 16))
            splits(OB0, None, 2, 3)
            splits(OB0 + 1, None, 0)
            with act.Fori(OB0 + 1, END - 1) as nb:
                splits(nb, None, 1)
                copy_T(nb - 1, nb - (1 + OB0) + NK_ + NV_ + 1)
                splits(nb, None, 2, 3)
                splits(nb + 1, None, 0)
            splits(END - 1, None, 1)
            copy_T(END - 2, END - 2 - OB0 + NK_ + NV_ + 1)
            splits(END - 1, None, 2, 3)
            copy_T(END - 1, END - 1 - OB0 + NK_ + NV_ + 1)

        @block.vector
        def _(dve):
            def split_lo(nb, u, gain):
                dve.wait_ge(w_hi, NU * nb + u + 1)
                hi = WHI[:, u % 2].bitcast(F32)
                if gain is None:
                    nc.vector.tensor_tensor(WLO[:, u % 2], WRAW[:, u], hi, ALU.subtract).then_inc(w_lo, 1)
                    return
                for k in range(UK):
                    g = gain[:, (u * UK + k) % gain.shape[1]:(u * UK + k) % gain.shape[1] + 1]
                    last = nc.vector.scalar_tensor_tensor(WLO[:, u % 2, k], WRAW[:, u, k], g, hi[:, k],
                                                          ALU.mult, ALU.subtract)
                last.then_inc(w_lo, 1)

            def splits(nb, gain, *us):
                for u in us:
                    split_lo(nb, u, gain)

            def evac(nb, scale=None, factor=None, add=None, final=False, chunked=False, banks=range(4)):
                if 0 in banks and not (isinstance(nb, int) and nb == 0):
                    dve.wait_ge(stored, 16 * nb)
                for j in banks:
                    ct, cols = j // NH, slice((j % NH) * HALF, (j % NH + 1) * HALF)
                    dve.wait_ge(acc_ready, 4 * nb + j + 1)
                    dst, src = stageT[:, ct, cols], PS[:, j, :]
                    if add is not None:
                        i = nc.vector.tensor_tensor(dst, src, add[:, ct, cols], ALU.add)
                    elif factor is not None:
                        i = nc.vector.tensor_tensor(dst, src, factor[:, ct, cols], ALU.mult)
                    elif scale is not None:
                        i = nc.vector.scalar_tensor_tensor(dst, src, scale, RSTD[:, cols], ALU.mult, ALU.mult)
                    elif chunked:
                        i = nc.vector.tensor_tensor(stageX[:, 8 * (j % NH):8 * (j % NH) + 8, ct],
                                                    src.rearrange("p (x s) -> p x s", s=CHUNK),
                                                    RSTD[:, cols].rearrange("p (x s) -> p x s", s=CHUNK), ALU.mult)
                    else:
                        i = nc.vector.tensor_tensor(dst, src, RSTD[:, cols], ALU.mult)
                    i.then_inc(acc_free, 1)
                if final:
                    dve.wait_ge(acc_free, 4 * nb + 8)
                    nc.vector.tensor_copy(st1[:, 0:1], eps_t[:, 0:1]).then_inc(out_ready, 1)

            def head_norm(k, gain):
                dve.wait_ge(n_root, k + 1)
                nc.vector.reciprocal(bufA, bufA).then_inc(n_dve, 1)
                dve.wait_ge(n_dve, k + 1)
                for i in range(CT):
                    last = nc.vector.scalar_tensor_tensor(stageT[:, i], stageT[:, i], gain, bufA[:, i],
                                                          ALU.mult, ALU.mult)
                last.then_inc(out_ready, 1)

            nc.vector.memset(WHI[:, :, :, :].bitcast(F32), 0.0).then_inc(acc_free, 4)
            dve.wait_ge(acc_free, 4)
            dve.wait_ge(v_pe, 2)
            nc.vector.tensor_copy(vcols[:, :], PS[:, 0, 0:NR]).then_inc(v_ok, 1)
            for half in range(2):
                rows = slice(half * HD, (half + 1) * HD)
                heads = PS[rows, 1, 0:KVH * 8].rearrange("p (b i a) -> p i b a", i=2, a=2)[:, half]
                nc.vector.tensor_copy(sinks[rows].rearrange("p b (a c) -> p b a c", a=2),
                                      heads.unsqueeze(3).to_broadcast([HD, D // BC, 2, 2])).then_inc(v_ok, 1)
            dve.wait_ge(v_ok, 3)
            nc.vector.tensor_tensor(wa[:, :, :], wa[:, :, :], g_a.unsqueeze(2).to_broadcast([P, KT, RANK]),
                                    ALU.mult).then_inc(wa_sc, 1)
            nc.vector.tensor_scalar(nsinks[:, :, :], sinks[:, :, :], -1.0, None, ALU.mult).then_inc(wa_sc, 1)
            nc.vector.scalar_tensor_tensor(kgain[:, 0:1], vcols[:, NR - 2:NR - 1], HD ** -0.5, vcols[:, NR - 1:NR],
                                           ALU.mult, ALU.mult).then_inc(wa_sc, 1)
            wcat = WHI[:, :, :, :].rearrange("p a k (b c) -> p (a k b) c", c=P)
            for i in range(4 * ST):
                dve.wait_ge(x_hi, i + 1)
                if i >= 4:
                    dve.wait_ge(x_st[i % 4], 16 * (i // 4))
                    dve.wait_ge(x_lo, i - 3)
                nc.vector.tensor_copy(xraw[:, i % 4].rearrange("p k s -> p (k s)"), PS[:, 4 + i % 4, :]
                                      ).then_inc(x_cp, 1)
                if i == 4:
                    dve.wait_ge(wa_hi, 1)
                    nc.vector.tensor_tensor(wcat[:, :, 32:32 + RANK], wa[:, :, :],
                                            wcat[:, :, 0:RANK].bitcast(F32), ALU.subtract).then_inc(wa_lo, 1)
            for j in range(NH):
                dve.wait_ge(ms_rt, j + 1)
                nc.vector.reciprocal(RSTD[:, j * HALF:(j + 1) * HALF], RSTD[:, j * HALF:(j + 1) * HALF]
                                     ).then_inc(rstd_ok, 1)
            dve.wait_ge(rstd_ok, NH)
            dve.wait_ge(al_pe, 1)
            for s in range(4):
                dve.wait_ge(x_st[s], 16 * ST)
            dve.wait_ge(x_lo, 4 * ST)
            nc.vector.memset(wup, 0.0).then_inc(al_ok, 1)
            for j in range(NH):
                last = nc.vector.tensor_tensor(alow[:, j * HALF:(j + 1) * HALF], PS[0:64, 4 + j, :],
                                               RSTD[0:64, j * HALF:(j + 1) * HALF], ALU.mult)
            last.then_inc(al_ok, 1)
            splits(0, g_a, 0)
            splits(0, g_a, 1, 2, 3)
            splits(1, g_a, 0)
            evac(0, scale=DK ** -0.5, final=True)
            with dve.Fori(1, KA0) as nb:
                splits(nb, g_a, 1, 2, 3)
                splits(nb + 1, g_a, 0)
                evac(nb, scale=DK ** -0.5, final=True)
            for nb in range(KA0, VA0):
                splits(nb, g_a, 1, 2, 3)
                for i in range(2):
                    n = 2 * (nb - KA0) + i
                    z, e = bufA[:, 0], bufA[:, 1]
                    dve.wait_ge(l_ready, n + 1)
                    if n > 0:
                        dve.wait_ge(l_log, 3 * n)
                    for j in range(NH):
                        last = nc.vector.tensor_scalar(z[:, j * HALF:(j + 1) * HALF], PS[:, 4 + 2 * i + j, :],
                                                       b_al[:, n:n + 1], None, ALU.add)
                    last.then_inc(l_dve, 1)
                    dve.wait_ge(l_dve, 3 * n + 1)
                    nc.vector.scalar_tensor_tensor(e, z, -1.0, z, ALU.mult, ALU.min).then_inc(l_abs, 1)
                    dve.wait_ge(l_log, 3 * n + 2)
                    nc.vector.scalar_tensor_tensor(z, z, 0.0, e, ALU.min, ALU.subtract).then_inc(l_dve, 1)
                    dve.wait_ge(l_dve, 3 * n + 2)
                    for c in range(SEQ // CHUNK):
                        cs = slice(c * CHUNK, (c + 1) * CHUNK)
                        last = nc.vector.tensor_tensor_scan(e[:, cs], ones[:, 0:CHUNK], z[:, cs], 0.0,
                                                            ALU.mult, ALU.add)
                    last.then_inc(l_dve, 1)
                    dve.wait_ge(l_dve, 3 * n + 3)
                    ev = e.rearrange("p (c s) -> p c s", s=CHUNK)
                    nc.vector.tensor_tensor(bufB[:, i].rearrange("p (c s) -> p c s", s=CHUNK),
                                            ev[:, :, CHUNK - 1:CHUNK].to_broadcast([P, SEQ // CHUNK, CHUNK]), ev,
                                            ALU.subtract).then_inc(l_cum, 1)
                    dve.wait_ge(l_exp, n + 1)
                    nc.vector.tensor_tensor(bufB[:, i], bufB[:, i], RSTD[:, :], ALU.mult).then_inc(l_ok, 1)
                splits(nb + 1, g_a, 0)
                dve.wait_ge(l_ok, 2 * (nb - KA0) + 2)
                evac(nb, factor=bufB)
            with dve.Fori(VA0, GA0) as nb:
                splits(nb, g_a, 1, 2, 3)
                splits(nb + 1, g_a, 0)
                evac(nb)
            with dve.Fori(GA0, OA0 - 1) as nb:
                splits(nb, g_a, 1, 2, 3)
                splits(nb + 1, g_a, 0)
                evac(nb)
            splits(OA0 - 1, g_a, 1, 2, 3)
            splits(OA0, g_o, 0)
            evac(OA0 - 1)

            dve.wait_ge(stored, 16 * OA0)
            nc.vector.memset(WORK[:, 0:4096], 0.0).then_inc(s_zero, 1)
            dve.wait_ge(s_zero, 1)

            def gla_update(t, i):
                h, c = i // 2, i % 2
                n = 8 * t + i
                dve.wait_ge(kv_pe, n + 1)
                if not isinstance(n, int) or n >= 1:
                    dve.wait_ge(o_pe, n)
                    dve.wait_ge(st_up, n)
                for k in range(2):
                    last = nc.vector.scalar_tensor_tensor(state[:, h, k], state[:, h, k],
                                                          dc[:, 2 * h + k, bass.ds(2 * t + c, 1)],
                                                          PS[:, 2 * (i % 2) + k, :], ALU.mult, ALU.add)
                last.then_inc(st_up, 1)

            def gla_recip(t, h):
                dve.wait_ge(o_rt, 4 * t + h + 1)
                nc.vector.reciprocal(st1[:, 4 + h:5 + h], st1[:, h:h + 1]).then_inc(o_rc, 1)

            def gla_gate(t, h):
                n = 4 * t + h
                dve.wait_ge(o_tr, n + 1)
                dve.wait_ge(gg_in[h % 2], 16 * (2 * t + h // 2 + 1))
                if not isinstance(n, int) or n >= 1:
                    dve.wait_ge(o_lo, n)
                nc.vector.tensor_tensor(ogate, PS[:, 6 + h % 2, :], gg[:, h % 2].rearrange("p i s -> p (i s)"),
                                        ALU.mult).then_inc(o_gt, 1)

            def gla_lo(t, h):
                n = 4 * t + h
                dve.wait_ge(o_hi, n + 1)
                dst = (slice(None), slice(4 * h, 4 * h + 4), bass.ds(t * P, P))
                nc.vector.tensor_tensor(XL[dst], ogate.rearrange("p (i s) -> p i s", i=4), XH[dst].bitcast(F32),
                                        ALU.subtract).then_inc(o_lo, 1)

            def gla_dve(t):
                for h in range(GH):
                    gla_update(t, 2 * h)
                    if h > 0:
                        gla_recip(t, h - 1)
                    if h > 1:
                        gla_lo(t, h - 2)
                    gla_update(t, 2 * h + 1)
                    if h > 0:
                        gla_gate(t, h - 1)
                gla_recip(t, GH - 1)
                gla_lo(t, GH - 2)
                gla_gate(t, GH - 1)
                gla_lo(t, GH - 1)

            gla_dve(0)
            with dve.Fori(1, ST) as t:
                gla_dve(t)

            def evac_res(nb, k, final=False):
                dve.wait_ge(res_in, 16 * (k + 1))
                evac(nb, add=bufA, final=final)

            with dve.Fori(OA0, KV0 - 1) as nb:
                splits(nb, g_o, 1, 2, 3)
                splits(nb + 1, g_o, 0)
                evac_res(nb, nb - OA0)

            def tiles_lo(base, kts):
                for kt in kts:
                    dve.wait_ge(r_hi, base + kt + 1)
                    src = reload_[:, kt % 2] if kt < KT - 2 else stageT[:, kt % 2]
                    nc.vector.tensor_tensor(XL[:, kt, :], src, XH[:, kt, :].bitcast(F32), ALU.subtract
                                            ).then_inc(r_lo, 1)

            splits(KV0 - 1, g_o, 1, 2)
            tiles_lo(0, range(0, 4))
            splits(KV0 - 1, g_o, 3)
            tiles_lo(0, range(4, 8))
            splits(KV0, g_kv, 0)
            tiles_lo(0, range(8, 12))
            evac_res(KV0 - 1, 7)
            splits(KV0, g_kv, 1)
            tiles_lo(0, range(12, 16))
            splits(KV0, g_kv, 2)
            for j in range(NH):
                dve.wait_ge(ms_rt, NH + j + 1)
                nc.vector.reciprocal(RSTD[:, j * HALF:(j + 1) * HALF], RSTD[:, j * HALF:(j + 1) * HALF]
                                     ).then_inc(rstd_ok, 1)
            dve.wait_ge(rstd_ok, 2 * NH)
            splits(KV0, g_kv, 3)
            splits(KV0 + 1, g_kv, 0)
            evac(KV0)
            splits(KV0 + 1, g_kv, 1)
            head_norm(0, kgain[:, 0:1])
            splits(KV0 + 1, g_kv, 2, 3)
            splits(QB0, g_b, 0)
            evac(KV0 + 1)
            splits(QB0, g_b, 1, 2, 3)
            splits(QB0 + 1, g_b, 0)
            evac(QB0, chunked=True, final=True)
            with dve.Fori(QB0 + 1, GB0 - 1) as nb:
                splits(nb, g_b, 1, 2, 3)
                splits(nb + 1, g_b, 0)
                evac(nb, chunked=True, final=True)

            def att_dve(h, e, s):
                it = item(h, e, s, 1)
                if it:
                    _, _, t, n = it
                    i = t % 2
                    dve.wait_ge(a_ex, n + 1)
                    nc.vector.tensor_tensor(st2[:, i, 6], st2[:, i, 6], st2[:, i, 5], ALU.add).then_inc(a_sm, 1)
                    dve.wait_ge(a_sm, n + 1)
                    nc.vector.reciprocal(st2[:, i, 7], st2[:, i, 6]).then_inc(a_rc, 1)
                it = item(h, e, s, 0)
                if not it:
                    return
                hh, ee, t, n = it
                i = t % 2
                m, rq, mx, mr, nm, sd = (st2[:, i, k] for k in range(6))
                dve.wait_ge(a_pe, n + 1)
                if not (isinstance(n, int) and n < 2):
                    dve.wait_ge(a_pr, n - 1)
                nc.vector.tensor_scalar(m.rearrange("p (a c) -> p a c", a=2), PS[:, 4:6, 256:258], 1.0 / HD, EPS,
                                        ALU.mult, ALU.add).then_inc(a_ms, 1)
                sc = PS[:, 4:6, 0:256].rearrange("p a (c k) -> p a c k", c=2)
                if t == 0:
                    for c in range(2):
                        last = nc.vector.tensor_reduce(mx.rearrange("p (a c) -> p a c", a=2)[:, :, c],
                                                       sc[:, :, c, CHUNK * (1 - c):], AX.X, ALU.max)
                else:
                    last = nc.vector.tensor_reduce(mx.rearrange("p (a c) -> p a c", a=2), sc, AX.X, ALU.max)
                last.then_inc(a_mx, 1)
                dve.wait_ge(a_mx, 3 * n + 1)
                dve.wait_ge(a_rq, n + 1)
                nc.vector.tensor_tensor(mr, mx, rq, ALU.mult).then_inc(a_mx, 1)
                dve.wait_ge(a_mx, 3 * n + 2)
                b = bass.ds(2 * hh + ee, 1)
                nc.vector.scalar_tensor_tensor(nm, mr, -1.0, nsinks[:, b].rearrange("p o g -> p (o g)"),
                                               ALU.mult, ALU.min).then_inc(a_mx, 1)
                dve.wait_ge(a_mx, 3 * n + 3)
                nc.vector.tensor_tensor(sd, nm, sinks[:, b].rearrange("p o g -> p (o g)"), ALU.add).then_inc(a_nm, 1)

            def gate(nb, b, e):
                dve.wait_ge(silu_b, nb - (GB0 - 1))
                dve.wait_ge(a_oc, 8 * b + 8)
                for ct in range(CT):
                    g = stageT[:, ct].rearrange("p (t c s) -> p t c s", c=2, s=CHUNK)
                    o = aq[e].rearrange("p t c (i s) -> p i t c s", i=CT)[:, ct]
                    last = nc.vector.tensor_tensor(g, g, o, ALU.mult)
                last.then_inc(out_ready, 1)

            def g_block(nb, h, e, first=False, last=False):
                for u in range(NU):
                    if u < NU - 1:
                        splits(nb, g_b, u + 1)
                    else:
                        splits(nb + 1, None if last else g_b, 0)
                    for i in range(2):
                        if u == NU - 1:
                            evac(nb, banks=(2 * i, 2 * i + 1))
                        att_dve(h, e, 2 * u + i)
                        if u == 0 and i == 0 and not first:
                            gate(nb - 1, 2 * h + e - 1, 1 - e)
                        if last and u > 0:
                            tiles_lo(KT, range(UK * (u - 1) + 2 * i, UK * (u - 1) + 2 * i + 2))

            splits(GB0 - 1, g_b, 1, 2, 3)
            for i in range(2):
                att_dve(-1, 1, 4 + i)
            splits(GB0, g_b, 0)
            for i in range(2):
                evac(GB0 - 1, chunked=True, banks=(2 * i, 2 * i + 1), final=i == 1)
                att_dve(-1, 1, 6 + i)
            for e in range(2):
                g_block(GB0 + e, 0, e, first=e == 0)
            with dve.Fori(1, KVH - 1) as h:
                for e in range(2):
                    g_block(2 * h + (GB0 + e), h, e)
            g_block(OB0 - 2, KVH - 1, 0)
            g_block(OB0 - 1, KVH - 1, 1, last=True)
            gate(OB0 - 1, D // BC - 1, 1)
            tiles_lo(KT, range(12, 14))
            splits(OB0, None, 1)
            tiles_lo(KT, range(14, 16))

            splits(OB0, None, 2, 3)
            splits(OB0 + 1, None, 0)
            evac_res(OB0, 8)
            with dve.Fori(OB0 + 1, END - 1) as nb:
                splits(nb, None, 1, 2, 3)
                splits(nb + 1, None, 0)
                evac_res(nb, nb - OB0 + 8)
            splits(END - 1, None, 1, 2, 3)
            evac_res(END - 1, 15)

        @block.tensor
        def _(pe):
            def unit(nb, u, ready=None, beside=None):
                pe.wait_ge(w_lo, NU * nb + u + 1)
                if ready is not None:
                    pe.wait_ge(*ready)
                for j in range(4):
                    ct, cols = j // NH, slice((j % NH) * HALF, (j % NH + 1) * HALF)
                    if u == 0:
                        pe.wait_ge(acc_free, 4 * nb + j + 1)
                    for k in range(UK):
                        kt = UK * u + k
                        hi, lo = (w[:, u % 2, k, ct * P:(ct + 1) * P] for w in (WHI, WLO))
                        nc.tensor.matmul(PS[:, j, :], hi, XH[:, kt, cols], start=kt == 0, stop=False)
                        nc.tensor.matmul(PS[:, j, :], hi, XL[:, kt, cols], start=False, stop=False)
                        last = nc.tensor.matmul(PS[:, j, :], lo, XH[:, kt, cols], start=False, stop=kt == KT - 1)
                    if u == NU - 1:
                        last.then_inc(acc_ready, 1)
                    elif j == 3:
                        last.then_inc(unit_used, 1)
                    if beside is not None and j % 2:
                        beside(2 * u + j // 2)

            def units(nb, *us):
                for u in us:
                    unit(nb, u)

            def transposes(nb, tb):
                pe.wait_ge(acc_free, 4 * nb + 8)
                for g in range(4):
                    for s in range(2):
                        for ct in range(CT):
                            st = 2 * g + s
                            last = nc.tensor.transpose(PS[:, 4 + g, (2 * s + ct) * P:(2 * s + ct + 1) * P],
                                                       stageT[:, ct, st * P:(st + 1) * P], ident[:, :])
                    last.then_inc(t_ready, 1)

            def head_sums(k, sq_count):
                pe.wait_ge(sq_done, sq_count)
                for j in range(4):
                    nc.tensor.matmul(PS[:, 4 + j, :], pair[:, :],
                                     bufB[:, j // NH, (j % NH) * HALF:(j % NH + 1) * HALF],
                                     start=True, stop=True).then_inc(n_ready, 1)

            pe.wait_ge(zeroed, 8)
            pe.wait_ge(consts_in, 16 * NCONST)
            nc.tensor.transpose(PS[:, 0, 0:NR], vrows[:, :], ident[0:NR, 0:NR]).then_inc(v_pe, 1)
            nc.tensor.matmul(PS[:, 1, 0:KVH * 8], ones[0:1, :], srow[:, :], start=True, stop=True).then_inc(v_pe, 1)
            for i in range(4 * ST):
                t, q = i // 4, i % 4
                pe.wait_ge(x_in[t % 4], 16 * (t // 4 + 1))
                if i >= 4:
                    pe.wait_ge(x_cp, i - 3)
                for k in range(4):
                    last = nc.tensor.transpose(PS[:, 4 + i % 4, k * P:(k + 1) * P],
                                               xin[:, t % 4, (4 * q + k) * P:(4 * q + k + 1) * P], ident[:, :])
                last.then_inc(x_tr, 1)
            pe.wait_ge(v_ok, 3)
            for t in range(ST):
                pe.wait_ge(x_sq, t + 1)
                last = nc.tensor.matmul(PS[:, t // 4, (t % 4) * P:(t % 4 + 1) * P],
                                        ssq[:, t:t + 1].to_broadcast([P, P]), ident[:, :], start=True, stop=True)
            last.then_inc(ss_pe, 1)
            pe.wait_ge(x_cp, 4 * ST)
            pe.wait_ge(x_lo, 4 * ST)
            pe.wait_ge(wa_lo, 1)
            wcat = WHI[:, :, :, :].rearrange("p a k (b c) -> p (a k b) c", c=P)
            for j in range(NH):
                cols = slice(j * HALF, (j + 1) * HALF)
                for kt in range(KT):
                    nc.tensor.matmul(PS[:, 4 + j, :], wcat[:, kt, :], XH[:, kt, cols], start=kt == 0, stop=False)
                    last = nc.tensor.matmul(PS[:, 4 + j, :], wcat[:, kt, :], XL[:, kt, cols], start=False,
                                            stop=kt == KT - 1)
            last.then_inc(al_pe, 1)

            pe.wait_ge(ms_rt, NH)
            with pe.Fori(0, KA0) as nb:
                units(nb, 0, 1, 2, 3)
            for nb in range(KA0, VA0):
                h = nb - KA0
                units(nb, 0)
                if h > 0:
                    transposes(nb - 1, h - 1)
                units(nb, 1)
                pe.wait_ge(up_in, 32 * (h + 1))
                pe.wait_ge(al_ok, 2)
                if h > 0:
                    pe.wait_ge(out_ready, nb)
                for i in range(2):
                    for j in range(NH):
                        last = nc.tensor.matmul(PS[:, 4 + 2 * i + j, :], wup[:, i * P:(i + 1) * P],
                                                alow[:, j * HALF:(j + 1) * HALF], start=True, stop=True)
                    last.then_inc(l_ready, 1)
                units(nb, 2, 3)
            units(VA0, 0)
            transposes(VA0 - 1, 3)
            units(VA0, 1, 2, 3)
            with pe.Fori(VA0 + 1, GA0 + 1) as nb:
                units(nb, 0)
                transposes(nb - 1, nb - (1 + KA0))
                units(nb, 1, 2, 3)
            with pe.Fori(GA0 + 1, OA0) as nb:
                units(nb, 0, 1, 2, 3)

            def gla_kv(t, i):
                h, c = i // 2, i % 2
                rows = slice(c * CHUNK, (c + 1) * CHUNK)
                n = 8 * t + i
                pe.wait_ge(qkv_in[h], 48 * (t + 1))
                if not isinstance(n, int) or n >= 2:
                    pe.wait_ge(st_up, n - 1)
                for k in range(2):
                    last = nc.tensor.matmul(PS[:, 2 * (i % 2) + k, :], gk[rows, h, k * P:(k + 1) * P],
                                            gv[rows, h, :], start=True, stop=True)
                last.then_inc(kv_pe, 1)

            def gla_o(t, i):
                h, c = i // 2, i % 2
                rows = slice(c * CHUNK, (c + 1) * CHUNK)
                n = 8 * t + i
                pe.wait_ge(st_up, n + 1)
                if not isinstance(n, int) or n >= 4:
                    pe.wait_ge(o_nm, 4 * t + h - 1)
                for k in range(2):
                    last = nc.tensor.matmul(PS[rows, 4 + h % 2, :], gq[:, h, k, rows], state[:, h, k],
                                            start=k == 0, stop=k == 1)
                last.then_inc(o_pe, 1)

            def gla_tr(t, h):
                n = 4 * t + h
                pe.wait_ge(o_nm, n + 1)
                if not isinstance(n, int) or n >= 2:
                    pe.wait_ge(o_gt, n - 1)
                for k in range(4):
                    last = nc.tensor.transpose(PS[:, 6 + h % 2, k * P:(k + 1) * P], onrm[:, k * P:(k + 1) * P],
                                               ident[:, :])
                last.then_inc(o_tr, 1)

            def gla_pe(t):
                gla_kv(t, 0)
                for i in range(8):
                    if i < 7:
                        gla_kv(t, i + 1)
                    gla_o(t, i)
                    if i % 2 == 0 and i > 0:
                        gla_tr(t, i // 2 - 1)
                gla_tr(t, GH - 1)

            gla_pe(0)
            with pe.Fori(1, ST) as t:
                gla_pe(t)

            pe.wait_ge(o_lo, 4 * ST)
            with pe.Fori(OA0, KV0) as nb:
                units(nb, 0, 1, 2, 3)
            unit(KV0, 0, ready=(r_lo, 4))
            unit(KV0, 1, ready=(r_lo, 8))
            pe.wait_ge(sum_ok, 2 * (D // BC) + 1)
            for j in range(NH):
                last = nc.tensor.matmul(PS[:, 4 + j, :], ones[:, :], sqsum[:, j * HALF:(j + 1) * HALF],
                                        start=True, stop=True)
            last.then_inc(ss_pe, 1)
            unit(KV0, 2, ready=(r_lo, 12))
            unit(KV0, 3, ready=(r_lo, 16))
            units(KV0 + 1, 0)
            head_sums(0, D // BC + 1)
            units(KV0 + 1, 1, 2, 3)
            units(QB0, 0)
            transposes(KV0 + 1, 12)
            units(QB0, 1, 2, 3)
            with pe.Fori(QB0 + 1, GB0 - 1) as nb:
                units(nb, 0, 1, 2, 3)

            def att_pe(h, e, s):
                it = item(h, e, s, 0)
                if it:
                    hh, ee, t, n = it
                    pe.wait_ge(q_in[ee], 16 * hh + 16)
                    pe.wait_ge(k_in[0], 32 * hh + 32)
                    if t >= 4:
                        pe.wait_ge(k_in[1], 32 * hh + 32)
                    pe.wait_ge(a_q2, n + 1)
                    if not (isinstance(n, int) and n == 0):
                        pe.wait_ge(a_ex, n)
                    for a in range(2):
                        rows = slice(a * HD, (a + 1) * HD)
                        for c in range(2):
                            x, lo = 2 * t + c, (CHUNK if t == 0 and c == 0 else 0)
                            nc.tensor.matmul(PS[:, 4 + a, c * P + lo:(c + 1) * P], aq[ee][rows, t, c],
                                             ak[rows, (x - 1) * CHUNK + lo:(x + 1) * CHUNK], start=True, stop=True)
                            last = nc.tensor.matmul(PS[:, 4 + a, 256 + c:257 + c], aq2[rows, t % 2, c],
                                                    ones[rows, 0:1], start=True, stop=True)
                    last.then_inc(a_pe, 1)
                it = item(h, e, s, 3)
                if it:
                    hh, _, t, n = it
                    pe.wait_ge(a_cp, n + 1)
                    pe.wait_ge(va_in[0], 48 * hh + 48)
                    if t == 0:
                        pe.wait_ge(a_vz, 1)
                    if t >= 4:
                        pe.wait_ge(va_in[1], 32 * hh + 32)
                    if not (isinstance(n, int) and n == 0):
                        pe.wait_ge(a_oc, n)
                    for a in range(2):
                        for c in range(2):
                            last = nc.tensor.matmul(PS[a * HD:(a + 1) * HD, 7, c * P:(c + 1) * P], av[:, c, t],
                                                    apt[:, 2 * a + c], start=True, stop=True)
                    last.then_inc(a_pv, 1)
                it = item(h, e, s, 2)
                if it:
                    _, _, t, n = it
                    pe.wait_ge(a_pr, n + 1)
                    if not (isinstance(n, int) and n == 0):
                        pe.wait_ge(a_cp, n)
                    for g in range(4):
                        last = nc.tensor.transpose(PS[:, 6, g * P:(g + 1) * P], ae[:, t % 2, g], ident[:, :])
                    last.then_inc(a_tr, 1)

            def beside(h, e):
                return lambda s: att_pe(h, e, s)

            units(GB0 - 1, 0, 1)
            for u in (2, 3):
                unit(GB0 - 1, u, beside=beside(-1, 1))
            with pe.Fori(0, KVH - 1) as h:
                for e in range(2):
                    for u in range(NU):
                        unit(2 * h + (GB0 + e), u, beside=beside(h, e))
            for e in range(2):
                for u in range(NU):
                    unit(OB0 - 2 + e, u, beside=beside(KVH - 1, e))

            for u in range(NU):
                unit(OB0, u, ready=(r_lo, KT + UK * (u + 1)))
            with pe.Fori(OB0 + 1, END) as nb:
                units(nb, 0)
                transposes(nb - 1, nb)
                units(nb, 1, 2, 3)
            transposes(END - 1, END)


_INS = ['x', 'a_norm', 'a_w_in', 'a_w_alpha_up', 'a_b_alpha', 'a_out_norm', 'a_w_out', 'kv_norm', 'w_kv', 'k_norm',
        'b_norm', 'b_w_in', 'b_q_norm', 'b_sinks', 'b_w_out']


def kernel(**inputs):
    import numpy as _np
    import concourse.bacc as _bacc
    from concourse import mybir as _mybir
    from concourse.bass_utils import run_bass_kernel_spmd as _run

    nc = _bacc.Bacc("TRN2", target_bir_lowering=False, num_devices=1)
    arrays, args = {}, []
    for name in _INS:
        a = _np.ascontiguousarray(inputs[name])
        arrays[f"in_{name}_dram"] = a
        args.append(nc.dram_tensor(f"in_{name}_dram", a.shape, _mybir.dt.from_np(a.dtype), kind="ExternalInput").ap())
    shape = _np.asarray(inputs['x']).shape
    args.append(nc.dram_tensor("out_0_dram", shape, _mybir.dt.float32, kind="ExternalOutput").ap())
    trunk_kernel(nc, *args)
    r = _run(nc, [arrays], core_ids=[0])
    return r.results[0]["out_0_dram"]
```

```python
import concourse.bass as bass
from concourse import mybir
from contextlib import ExitStack

F32 = mybir.dt.float32
F32R = mybir.dt.float32r
ALU = mybir.AluOpType
ACT = mybir.ActivationFunctionType
AX = mybir.AxisListType


def trunk_kernel(nc, x, a_norm, a_w_in, a_w_alpha_up, a_b_alpha, a_out_norm, a_w_out,
                 kv_norm, w_kv, k_norm, b_norm, b_w_in, b_q_norm, b_sinks, b_w_out, out):
    P = 128
    SEQ, D = x.shape[1], x.shape[2]
    KT = D // P
    ST = SEQ // P
    HALF = 512
    NH = SEQ // HALF
    UK, BC = 4, 256
    NU = KT // UK
    CT = BC // P
    CHUNK = 64
    GH, DK, DV = 4, 256, 512
    RANK = a_w_alpha_up.shape[1]
    TAU = 16.0
    HD = 64
    KVH = 4
    EPS = 1e-6
    NQ, NK_, NV_, NG_ = GH * DK // BC, GH * DK // BC, GH * DV // BC, GH * DV // BC
    KA0 = NQ
    VA0 = KA0 + NK_
    GA0 = VA0 + NV_
    OA0 = GA0 + NG_
    KV0 = OA0 + D // BC
    QB0 = KV0 + 2
    GB0 = QB0 + D // BC
    OB0 = GB0 + D // BC
    END = OB0 + D // BC

    def scratch(name, shape):
        return nc.dram_tensor(name, shape, F32).ap()

    xT_s = scratch("xT_s", [D, SEQ])
    qa_s = scratch("qa_s", [GH * DK, SEQ])
    kt_s = scratch("kt_s", [GH * DK, SEQ])
    ka_s = scratch("ka_s", [SEQ, GH * DK])
    va_s = scratch("va_s", [SEQ, GH * DV])
    ga_s = scratch("ga_s", [GH * DV, SEQ])
    x1_s = scratch("x1_s", [D, SEQ])
    kb_s = scratch("kb_s", [KVH * HD, SEQ])
    vb_s = scratch("vb_s", [SEQ, KVH * HD])
    qb_s = scratch("qb_s", [D // BC, P, CT * SEQ])
    ob_s = scratch("ob_s", [D, SEQ])

    x2d, out2d = x[0], out[0]

    ctx = ExitStack()
    with ctx:
        def sb(name, shape, dt=F32):
            return ctx.enter_context(nc.sbuf_tensor(name, shape, dt))

        def sem(name):
            return ctx.enter_context(nc.semaphore(name))

        XH = sb("XH", [P, KT, SEQ], F32R)
        XL = sb("XL", [P, KT, SEQ], F32R)
        WRAW = sb("WRAW", [P, NU, UK, BC])
        WHI = sb("WHI", [P, 2, UK, BC], F32R)
        WLO = sb("WLO", [P, 2, UK, BC], F32R)
        RSTD = sb("RSTD", [P, SEQ])
        WORK = sb("WORK", [P, 10240])
        ident = sb("ident", [P, P])
        pair = sb("pair", [P, P])
        ones = sb("ones", [P, P])
        NR = 3 * KT + DV // P + GH * DK // P + 2
        vrows = WRAW[0:NR, 3, 1, 0:P]
        vcols = sb("vcols", [P, NR])
        g_a, g_kv, g_b = (vcols[:, i * KT:(i + 1) * KT] for i in range(3))
        g_o = vcols[:, 3 * KT:3 * KT + DV // P]
        b_al = vcols[:, 3 * KT + DV // P:NR - 2]
        srow = sb("srow", [1, KVH * 8])
        kgain = sb("kgain", [P, 1])
        sinks = sb("sinks", [P, D // BC, 4])
        nsinks = sb("nsinks", [P, D // BC, 4])
        dc = sb("dc", [P, GH * DK // P, SEQ // CHUNK])
        wcat = [w[:, 1].rearrange("p k (b c) -> p (k b) c", c=P) for w in (WHI, WLO)]
        XB = (4, 5, 6, 0)
        wa = WRAW[:, 3, 0, :].rearrange("p (k r) -> p k r", r=RANK)
        dcum = sb("dcum", [P, GH * DK // P, ST, 2])
        ssq = sb("ssq", [P, ST])
        eps_t = sb("eps_t", [P, 1])
        st1 = sb("st1", [P, 8])
        mhalf = sb("mhalf", [P, 4])
        st2 = sb("st2", [P, 2, 8, 4])

        PS = ctx.enter_context(nc.psum_tensor("PS", [P, 8, 512], F32))

        NX = 5
        xin = WORK[:, 0:NX * D].rearrange("p (n d) -> p n d", n=NX)
        xsum = WORK[:, 4096:8192].rearrange("p (n s) -> p n s", n=4)
        stageT = WORK[:, 0:2048].rearrange("p (i s) -> p i s", i=CT)
        stageN = WORK[:, 2048:4096].rearrange("p (s c) -> p s c", s=ST)
        stageX = WORK[:, 0:2048].rearrange("p (x i s) -> p x i s", x=SEQ // CHUNK, i=CT)
        reload_ = WORK[:, 2048:4096].rearrange("p (n s) -> p n s", n=2)
        bufA = WORK[:, 4096:6144].rearrange("p (i s) -> p i s", i=CT)
        bufB = WORK[:, 6144:8192].rearrange("p (i s) -> p i s", i=CT)
        alow = WORK[0:64, 8192:9216]
        wup = WORK[0:64, 9216:9216 + BC]
        sqsum = WORK[:, 8192:9216]
        state = WORK[:, 0:4096].rearrange("p (h i v) -> p h i v", h=GH, i=2)
        gq = WORK[:, 4096:5120].rearrange("p (h i s) -> p h i s", h=GH, i=2)
        gk = WORK[:, 5120:6144].rearrange("p (h k) -> p h k", h=GH)
        gv = WORK[:, 6144:8192].rearrange("p (h v) -> p h v", h=GH)
        gg = WORK[:, 8192:9216].rearrange("p (n i s) -> p n i s", n=2, i=4)
        gkt = WORK[:, 9216:10240].rearrange("p (h i s) -> p h i s", h=GH, i=2)
        spare = WRAW[:, 0].rearrange("p k c -> p (k c)")
        onrm, ogate = spare[:, 0:512], spare[:, 512:1024]
        qs = RSTD[:, 0:512].rearrange("p (n i s) -> p n i s", n=2, i=2)
        qc = RSTD[:, 512:1024].rearrange("p (n i s) -> p n i s", n=2, i=2)
        qk = pair
        aq = [WORK[:, at:at + 2048].rearrange("p (t c x) -> p t c x", t=ST, c=2) for at in (2048, 4096)]
        ae = WORK[:, 6144:7168].rearrange("p (n g k) -> p n g k", n=2, g=4)
        apt = WORK[:, 7168:7680].rearrange("p (g r) -> p g r", g=4)
        aq2 = WORK[:, 7680:8192].rearrange("p (n c x) -> p n c x", n=2, c=2)
        ak = WORK[:, 8192:9216]
        av = WORK[:, 9216:10240].rearrange("p (c t d) -> p c t d", c=2, t=ST)

        v_pe = sem("v_pe")
        v_ok = sem("v_ok")
        consts_in = sem("consts_in")
        zeroed = sem("zeroed")
        x_in = [sem(f"x_in{i}") for i in range(NX)]
        x_tr = sem("x_tr")
        x_hi = sem("x_hi")
        x_lo = sem("x_lo")
        x_sq = sem("x_sq")
        x_sum = sem("x_sum")
        x_st = [sem(f"x_st{i}") for i in range(4)]
        ss_pe = sem("ss_pe")
        ms_rt = sem("ms_rt")
        rstd_ok = sem("rstd_ok")
        wa_sc = sem("wa_sc")
        wa_hi = sem("wa_hi")
        wa_lo = sem("wa_lo")
        al_pe = sem("al_pe")
        al_ok = sem("al_ok")
        w_in = [sem(f"w_in{i}") for i in range(NU)]
        w_hi = sem("w_hi")
        w_lo = sem("w_lo")
        unit_used = sem("unit_used")
        acc_ready = sem("acc_ready")
        acc_free = sem("acc_free")
        out_ready = sem("out_ready")
        stored = sem("stored")
        t_ready = sem("t_ready")
        t_free = sem("t_free")
        sq_done = sem("sq_done")
        n_ready = sem("n_ready")
        n_root = sem("n_root")
        n_dve = sem("n_dve")
        up_in = sem("up_in")
        l_ready = sem("l_ready")
        l_add = sem("l_add")
        l_abs = sem("l_abs")
        l_log = sem("l_log")
        l_dve = sem("l_dve")
        l_cum = sem("l_cum")
        l_exp = sem("l_exp")
        l_ok = sem("l_ok")
        res_in = sem("res_in")
        sum_ok = sem("sum_ok")
        rel_in = [sem(f"rel_in{i}") for i in range(2)]
        r_hi = sem("r_hi")
        r_lo = sem("r_lo")
        pair_ok = sem("pair_ok")
        g_init = sem("g_init")
        qkv_in = [sem(f"qkv_in{i}") for i in range(GH)]
        gg_in = [sem(f"gg_in{i}") for i in range(2)]
        kt_st = sem("kt_st")
        k2_ok = sem("k2_ok")
        gs_ok = sem("gs_ok")
        qk_pe = sem("qk_pe")
        qk_ok = sem("qk_ok")
        kv_pe = sem("kv_pe")
        st_up = sem("st_up")
        o_pe = sem("o_pe")
        o_ss = sem("o_ss")
        o_rt = sem("o_rt")
        o_rc = sem("o_rc")
        o_nm = sem("o_nm")
        o_tr = sem("o_tr")
        o_gt = sem("o_gt")
        o_hi = sem("o_hi")
        o_lo = sem("o_lo")
        q_in = [sem(f"q_in{i}") for i in range(2)]
        k_in = [sem(f"k_in{i}") for i in range(2)]
        va_in = [sem(f"va_in{i}") for i in range(2)]
        a_vz = sem("a_vz")
        a_q2 = sem("a_q2")
        a_pe = sem("a_pe")
        a_ms = sem("a_ms")
        a_rq = sem("a_rq")
        a_mx = sem("a_mx")
        a_nm = sem("a_nm")
        a_ex = sem("a_ex")
        a_ez = sem("a_ez")
        a_sm = sem("a_sm")
        a_rc = sem("a_rc")
        a_pr = sem("a_pr")
        a_tr = sem("a_tr")
        a_cp = sem("a_cp")
        a_pv = sem("a_pv")
        a_oc = sem("a_oc")
        silu_b = sem("silu_b")

        END_T = END - 1 - OB0 + NK_ + NV_ + 1
        NCONST = 11

        LEAD = 4

        def gla_item(t, h, back, heads=GH):
            if back > h:
                t, h = t - 1, h + heads
            if isinstance(t, int) and not 0 <= t < ST:
                return None
            return t, h - back

        def gla_steps(engine, step, tail):
            for h in range(GH):
                step(0, h)
            step(1, 0)
            with engine.Fori(1, ST - 1) as t:
                for h in range(1, GH):
                    step(t, h)
                step(t + 1, 0)
            for h in range(1, GH):
                step(ST - 1, h)
            for h in range(tail):
                step(ST, h)

        def item(h, e, s, back):
            v = s + LEAD - back
            e2, t = e + v // 8, v % 8
            hh, ee = h + e2 // 2, e2 % 2
            if isinstance(h, int) and not 0 <= 2 * hh + ee < D // BC:
                return None
            return hh, ee, t, 16 * hh + 8 * ee + t

        block = ctx.enter_context(nc.Block())

        def weights(w, b, u):
            return w[u * UK * P:(u + 1) * UK * P, bass.ds(b * BC, BC)].rearrange("(k p) c -> p k c", p=P)

        wa_in_w, wa_out_w, wb_in_w, wb_out_w = a_w_in[0], a_w_out[0], b_w_in[0], b_w_out[0]

        @block.sync
        def _(sp):
            def load_w(w, nb, b, first=False):
                for u in range(NU):
                    load_unit(w, nb, b, u, first)

            def load_unit(w, nb, b, u, first=False):
                if not first:
                    sp.wait_ge(w_lo, (nb - 1) * NU + u + 1)
                sp.dma_start(WRAW[:, u], weights(w, b, u)).then_inc(w_in[u], 16)

            def store_T(dst, nb, b):
                sp.wait_ge(out_ready, nb + 1)
                sp.dma_start(dst[bass.ds(b * BC, BC), :].rearrange("(i p) s -> p i s", p=P),
                             stageT).then_inc(stored, 16)

            def store_N(dst, nb, b):
                sp.wait_ge(out_ready, nb + 1)
                sp.dma_start(dst[:, bass.ds(b * BC, BC)].rearrange("(s p) c -> p s c", p=P),
                             stageN).then_inc(stored, 16)

            def store_kt(nb):
                sp.wait_ge(acc_free, 4 * nb + 8)
                sp.dma_start(kt_s[(nb - KA0) * BC:(nb - KA0 + 1) * BC, :].rearrange("(i p) s -> p i s", p=P),
                             stageT).then_inc(kt_st, 16)

            def store_x(kt):
                sp.wait_ge(x_sum, kt + 1)
                sp.dma_start(xT_s[kt * P:(kt + 1) * P, :], xsum[:, kt % 4]).then_inc(x_st[kt % 4], 16)

            def load_x(t):
                if t >= NX:
                    sp.wait_ge(x_sq, t - NX + 1)
                sp.dma_start(xin[:, t % NX], x2d[t * P:(t + 1) * P, :]).then_inc(x_in[t % NX], 16)

            load_x(0)
            load_x(1)
            at = 0
            for v in (a_norm[0], kv_norm, b_norm[0], a_out_norm[0], a_b_alpha[0]):
                n = v.shape[0] // P
                sp.dma_start(vrows[at:at + n, :], v.rearrange("(k p) -> k p", p=P)).then_inc(consts_in, 16)
                at += n
            for v in (k_norm, b_q_norm[0]):
                for half in range(2):
                    sp.dma_start(vrows[at:at + 1, half * HD:(half + 1) * HD],
                                 v.rearrange("(o p) -> o p", o=1)).then_inc(consts_in, 16)
                at += 1
            sp.dma_start(srow[:, :], b_sinks).then_inc(consts_in, 16)
            sp.dma_start(wa[:, :, :], wa_in_w[:, OA0 * BC:].rearrange("(k p) r -> p k r", p=P)
                         ).then_inc(consts_in, 16)
            for t in range(2, NX + 1):
                load_x(t)
            load_unit(wa_in_w, 0, 0, 0, first=True)
            for t in range(NX + 1, ST):
                load_x(t)
            load_unit(wa_in_w, 0, 0, 1, first=True)
            load_unit(wa_in_w, 0, 0, 2, first=True)
            sp.wait_ge(wa_lo, 1)
            load_unit(wa_in_w, 0, 0, 3, first=True)

            for nb in range(1, KA0):
                load_w(wa_in_w, nb, nb)
                for kt in range(8 * (nb - 1), 8 * nb if nb < 3 else 0):
                    store_x(kt)
                store_T(qa_s, nb - 1, nb - 1)
            for nb in range(KA0, VA0):
                for u in range(NU):
                    load_unit(wa_in_w, nb, nb, u)
                    if u == 0 and nb > KA0:
                        sp.wait_ge(l_ready, 2 * (nb - KA0))
                    elif u == 0:
                        sp.wait_ge(al_ok, 2)
                    for r in range(2 if u == 0 else 0):
                        sp.dma_start(wup[32 * r:32 * r + RANK, :],
                                     a_w_alpha_up[0][:, (nb - KA0) * DK:(nb - KA0 + 1) * DK]).then_inc(up_in, 16)
                if nb == KA0:
                    store_T(qa_s, nb - 1, nb - 1)
                else:
                    store_kt(nb - 1)
                    store_N(ka_s, nb - 1, nb - 1 - KA0)
            load_w(wa_in_w, VA0, VA0)
            store_kt(VA0 - 1)
            store_N(ka_s, VA0 - 1, VA0 - 1 - KA0)
            with sp.Fori(VA0 + 1, GA0 + 1) as nb:
                load_w(wa_in_w, nb, nb)
                store_N(va_s, nb - 1, nb - (1 + VA0))
            with sp.Fori(GA0 + 1, OA0 - 1) as nb:
                load_w(wa_in_w, nb, nb)
                store_T(ga_s, nb - 1, nb - (1 + GA0))
            load_w(wa_in_w, OA0 - 1, OA0 - 1)
            store_T(ga_s, OA0 - 2, NG_ - 2)
            load_w(wa_out_w, OA0, 0)

            def load_head(t, h):
                if not isinstance(t, int):
                    sp.wait_ge(o_pe, 4 * t + h - 3)
                tile = bass.ds(t * P, P)
                for dst, src in ((gq, qa_s), (gkt, kt_s)):
                    sp.dma_start(dst[:, h], src[h * DK:(h + 1) * DK, tile].rearrange("(i p) s -> p i s", p=P)
                                 ).then_inc(qkv_in[h], 16)
                sp.dma_start(gk[:, h], ka_s[tile, h * DK:(h + 1) * DK]).then_inc(qkv_in[h], 16)
                sp.dma_start(gv[:, h], va_s[tile, h * DV:(h + 1) * DV]).then_inc(qkv_in[h], 16)

            def load_gate(t, h):
                if not isinstance(t, int) or h >= 2:
                    sp.wait_ge(o_gt, 4 * t + h - 1)
                sp.dma_start(gg[:, h % 2], ga_s[h * DV:(h + 1) * DV, bass.ds(t * P, P)]
                             .rearrange("(i p) s -> p i s", p=P)).then_inc(gg_in[h % 2], 16)

            sp.wait_ge(kt_st, 16 * GH)
            sp.wait_ge(stored, 16 * (OA0 - 2))
            for h in range(GH):
                load_head(0, h)
            for h in range(2):
                load_gate(0, h)
            store_T(ga_s, OA0 - 1, NG_ - 1)
            sp.wait_ge(stored, 16 * OA0)
            with sp.Fori(1, ST) as t:
                for h in range(GH):
                    load_head(t, h)
                    load_gate(*gla_item(t, h, 2))
            for h in range(2):
                load_gate(*gla_item(ST, h, 2))

            def load_res(src, nb, b, first, work_free=None):
                if first:
                    sp.wait_ge(*work_free)
                else:
                    sp.wait_ge(acc_free, (nb + 1) * 4)
                sp.dma_start(bufA, src[bass.ds(b * BC, BC), :].rearrange("(i p) s -> p i s", p=P)
                             ).then_inc(res_in, 16)

            load_res(xT_s, OA0, 0, True, (o_lo, 4 * ST))
            with sp.Fori(OA0 + 1, KV0) as nb:
                load_w(wa_out_w, nb, nb - OA0)
                load_res(xT_s, nb, nb - OA0, False)
                store_T(x1_s, nb - 1, nb - (1 + OA0))
            def reload_tiles(src, base, loads, w, nb):
                sp.wait_ge(stored, 16 * (nb - 1))
                for kt in range(KT - 2):
                    if kt >= 2:
                        sp.wait_ge(r_lo, base + kt - 1)
                    sp.dma_start(reload_[:, kt % 2], src[kt * P:(kt + 1) * P, :]).then_inc(rel_in[kt % 2], 16)
                    if kt in loads:
                        load_unit(w, nb, 0, loads.index(kt))

            reload_tiles(x1_s, 0, (0, 1, 5, 9), w_kv, KV0)
            store_T(x1_s, KV0 - 1, 7)
            load_w(w_kv, KV0 + 1, 1)
            store_T(kb_s, KV0, 0)
            load_w(wb_in_w, QB0, 0)
            store_N(vb_s, KV0 + 1, 0)
            def store_q(nb):
                sp.wait_ge(out_ready, nb + 1)
                sp.dma_start(qb_s[bass.ds(nb - QB0, 1)].rearrange("o p x -> p (o x)"), WORK[:, 0:2048]
                             ).then_inc(stored, 16)

            def load_q(b, e):
                sp.dma_start(aq[e].rearrange("p t c x -> p (t c x)"),
                             qb_s[bass.ds(b, 1)].rearrange("o p x -> p (o x)")).then_inc(q_in[e], 16)

            def load_k(h, half):
                cols = slice(half * HALF, (half + 1) * HALF)
                for a in range(2):
                    sp.dma_start(ak[a * HD:(a + 1) * HD, cols], kb_s[bass.ds(h * HD, HD), cols]
                                 ).then_inc(k_in[half], 16)

            def load_v(h, half, ahead=0):
                cols = bass.ds(h * HD + ahead * HD, HD)
                sp.dma_start(av[:, 1, 4 * half:4 * half + 4],
                             vb_s[half * HALF:(half + 1) * HALF, cols].rearrange("(t p) d -> p t d", p=P)
                             ).then_inc(va_in[half], 16)
                if half == 0:
                    sp.dma_start(av[64:128, 0, 0], vb_s[0:64, cols]).then_inc(va_in[0], 16)
                first = 1 if half == 0 else 4
                sp.dma_start(av[:, 0, first:4 * half + 4],
                             vb_s[first * P - 64:(half + 1) * HALF - 64, cols].rearrange("(t p) d -> p t d", p=P)
                             ).then_inc(va_in[half], 16)

            with sp.Fori(QB0 + 1, GB0 - 1) as nb:
                load_w(wb_in_w, nb, nb - QB0)
                store_q(nb - 1)
            load_w(wb_in_w, GB0 - 1, GB0 - 1 - QB0)
            sp.wait_ge(stored, 16 * (GB0 - 2))
            load_q(0, 0)
            load_q(1, 1)
            for half in range(2):
                load_k(0, half)
                load_v(0, half)
            store_q(GB0 - 2)
            load_w(wb_in_w, GB0, GB0 - QB0)
            store_q(GB0 - 1)

            def next_block(nb, h, e, w, b, more):
                n = 16 * h + 8 * e
                head = e == 1 and more
                load_unit(w, nb, b, 0)
                load_unit(w, nb, b, 1)
                if not (isinstance(h, int) and h == 0 and e == 0):
                    sp.wait_ge(out_ready, nb - 1)
                    sp.wait_ge(stored, 16 * nb - 32)
                    if more or e == 0:
                        load_q(2 * h + e + 1, 1 - e)
                    store_T(ob_s, nb - 2, nb - (2 + GB0))
                if head:
                    sp.wait_ge(a_pe, n + 5)
                    load_k(h + 1, 0)
                load_unit(w, nb, b, 2)
                if head:
                    sp.wait_ge(a_pv, n + 4)
                    load_v(h, 0, 1)
                    sp.wait_ge(a_pe, n + 8)
                    load_k(h + 1, 1)
                load_unit(w, nb, b, 3)
                if head:
                    sp.wait_ge(a_pv, n + 8)
                    load_v(h, 1, 1)

            next_block(GB0 + 1, 0, 0, wb_in_w, GB0 + 1 - QB0, True)
            next_block(GB0 + 2, 0, 1, wb_in_w, GB0 + 2 - QB0, True)
            with sp.Fori(1, KVH - 1) as h:
                for e in range(2):
                    next_block(2 * h + (GB0 + 1 + e), h, e, wb_in_w, 2 * h + (GB0 - QB0 + 1 + e), True)
            next_block(OB0 - 1, KVH - 1, 0, wb_in_w, OB0 - 1 - QB0, False)
            sp.wait_ge(out_ready, OB0 - 1)
            store_T(ob_s, OB0 - 2, D // BC - 2)
            reload_tiles(ob_s, KT, (0, 1, 5, 9), wb_out_w, OB0)
            store_T(ob_s, OB0 - 1, D // BC - 1)

            load_res(x1_s, OB0, 0, True, (out_ready, OB0))
            with sp.Fori(OB0 + 1, END) as nb:
                load_w(wb_out_w, nb, nb - OB0)
                load_res(x1_s, nb, nb - OB0, False)
                store_N(out2d, nb - 1, nb - (1 + OB0))
            for g in range(4):
                if g < 3:
                    sp.wait_ge(t_free, 3 * END_T + g + 1)
                else:
                    sp.wait_ge(out_ready, END)
                sp.dma_start(out2d[g * 2 * P:(g + 1) * 2 * P, D - BC:D].rearrange("(s p) c -> p s c", p=P),
                             stageN[:, 2 * g:2 * g + 2]).then_inc(stored, 16)
            sp.wait_ge(stored, 16 * (END + 3))

        @block.gpsimd
        def _(pool):
            nc.gpsimd.memset(ident[:, :], 0.0).then_inc(zeroed, 1)
            nc.gpsimd.memset(ones[:, :], 1.0).then_inc(zeroed, 1)
            nc.gpsimd.memset(eps_t[:, :], EPS).then_inc(zeroed, 1)
            nc.gpsimd.memset(mhalf[:, :], -0.5).then_inc(zeroed, 1)
            pool.wait_ge(zeroed, 4)
            nc.gpsimd.affine_select(out=ident[:, :], in_=ident[:, :], compare_op=ALU.not_equal, fill=1.0, base=0,
                                    pattern=[[-1, P]], channel_multiplier=1).then_inc(zeroed, 1)
            pool.wait_ge(x_lo, 4 * ST)
            pool.wait_ge(x_sq, ST)
            for kt in range(KT):
                if kt >= 4:
                    pool.wait_ge(x_st[kt % 4], 16 * (kt // 4))
                nc.gpsimd.tensor_tensor(xsum[:, kt % 4], XH[:, kt, :].bitcast(F32), XL[:, kt, :].bitcast(F32), ALU.add
                                        ).then_inc(x_sum, 1)
            for h in range(GH):
                pool.wait_ge(acc_free, 4 * (KA0 + h) + 8)
                pool.wait_ge(l_log, 6 * h + 6)
                for i in range(CT):
                    src, dst = (b[:, i].rearrange("p (t c s) -> p t c s", c=2, s=CHUNK) for b in (stageT, bufA))
                    d1 = dc[:, 2 * h + i, :].rearrange("p (t c) -> p t c", c=2)[:, :, 1]
                    nc.gpsimd.tensor_tensor(dst[:, :, 0], src[:, :, 0],
                                            d1.unsqueeze(2).to_broadcast([P, ST, CHUNK]), ALU.mult)
                    last = nc.gpsimd.tensor_copy(dst[:, :, 1], src[:, :, 1])
                last.then_inc(k2_ok, 1)

            def scale_q(t, h):
                pool.wait_ge(qkv_in[h], 64 * t + 64)
                if not (isinstance(t, int) and 4 * t + h < 2):
                    pool.wait_ge(o_pe, 4 * t + h - 1)
                tile = bass.ds(t, 1)
                q = gq[:, h].rearrange("p i (c s) -> p i c s", c=2)
                d = dcum[:, 2 * h:2 * h + 2, tile, :].rearrange("p n o c -> p n (o c)")
                nc.gpsimd.tensor_tensor(qs[:, h % 2].rearrange("p i (c s) -> p i c s", c=2), q,
                                        d.unsqueeze(3).to_broadcast([P, 2, 2, CHUNK]), ALU.mult)
                d1 = dc[:, 2 * h:2 * h + 2, :].rearrange("p n (t c) -> p n t c", c=2)[:, :, tile, 1]
                out = qc[:, h % 2].rearrange("p i (c s) -> p i c s", c=2)
                nc.gpsimd.tensor_copy(out[:, :, 0], q[:, :, 0])
                nc.gpsimd.tensor_tensor(out[:, :, 1], q[:, :, 1], d1.to_broadcast([P, 2, CHUNK]), ALU.mult
                                        ).then_inc(gs_ok, 1)

            pool.wait_ge(g_init, 3)
            pool.wait_ge(acc_free, 4 * OA0 + 4)
            for h in range(GH):
                scale_q(0, h)
            with pool.Fori(1, ST) as t:
                for h in range(GH):
                    scale_q(t, h)
            pool.wait_ge(o_pe, GH * ST)
            nc.gpsimd.memset(pair[:, :], 1.0).then_inc(pair_ok, 1)
            pool.wait_ge(pair_ok, 1)
            nc.gpsimd.affine_select(out=pair[:, 64:128], in_=pair[:, 64:128], compare_op=ALU.is_ge, fill=0.0,
                                    base=-64, pattern=[[0, 64]], channel_multiplier=1).then_inc(pair_ok, 1)
            nc.gpsimd.affine_select(out=pair[:, 0:64], in_=pair[:, 0:64], compare_op=ALU.is_ge, fill=0.0,
                                    base=63, pattern=[[0, 64]], channel_multiplier=-1).then_inc(pair_ok, 1)
            pool.wait_ge(o_lo, 4 * ST)
            nc.gpsimd.memset(sqsum, 0.0).then_inc(sum_ok, 1)
            with pool.Fori(OA0, KV0) as nb:
                for i in range(CT):
                    if i == 0:
                        pool.wait_ge(sq_done, nb - OA0 + 1)
                    pool.wait_ge(sum_ok, (nb - OA0) * 2 + i + 1)
                    nc.gpsimd.tensor_tensor(sqsum, sqsum, bufB[:, i], ALU.add).then_inc(sum_ok, 1)
            def squares(h, e, t, n):
                pool.wait_ge(q_in[e], 16 * h + 16)
                q = aq[e][:, t]
                nc.gpsimd.tensor_tensor(aq2[:, t % 2], q, q, ALU.mult).then_inc(a_q2, 1)

            def zeros_of(it):
                return 2 * it[0] + it[1] + 1

            def att_pool(h, e, s):
                last = item(h, e, s, 1)
                if last:
                    _, _, t, n = last
                    pool.wait_ge(a_rc, n + 1)
                    if t == 0:
                        pool.wait_ge(a_ez, zeros_of(last))
                    nc.gpsimd.tensor_tensor(ae[:, t % 2], ae[:, t % 2],
                                            st2[:, t % 2, 7].unsqueeze(2).to_broadcast([P, 4, P]),
                                            ALU.mult).then_inc(a_pr, 1)
                now = item(h, e, s, 0)
                if now:
                    _, _, t, n = now
                    pool.wait_ge(a_ms, n + 1)
                    nc.gpsimd.tensor_tensor(st2[:, t % 2, 1], st2[:, t % 2, 0], mhalf[:, :], ALU.pow
                                            ).then_inc(a_rq, 1)
                    if t == 0:
                        if not (isinstance(n, int) and n < 2):
                            pool.wait_ge(a_tr, n - 1)
                        one = ones[:, :].rearrange("p (a k) -> p a k", a=2)
                        nc.gpsimd.tensor_tensor(ae[:, 0].rearrange("p (a c) k -> p a c k", a=2)[:, :, 0, 0:CHUNK],
                                                one, one, ALU.subtract).then_inc(a_ez, 1)
                nxt = item(h, e, s, -1)
                if nxt:
                    squares(*nxt)

            pool.wait_ge(out_ready, QB0 + 1)
            pool.wait_ge(stored, 16 * (KV0 + 1))
            nc.gpsimd.memset(av[0:64, 0, 0], 0.0).then_inc(a_vz, 1)
            squares(0, 0, 0, 0)
            for s in range(4, 8):
                att_pool(-1, 1, s)
            with pool.Fori(0, KVH - 1) as h:
                for e in range(2):
                    for s in range(8):
                        att_pool(h, e, s)
            for e in range(2):
                for s in range(8):
                    att_pool(KVH - 1, e, s)

        @block.scalar
        def _(act):
            def split_hi(nb, u, gain):
                act.wait_ge(w_in[u], 16 * (nb + 1))
                if isinstance(nb, int) and nb == 0 and u < 2:
                    pass
                elif u == 1:
                    act.wait_ge(acc_ready, 4 * nb)
                elif u >= 2:
                    act.wait_ge(unit_used, 3 * nb + u - 1)
                else:
                    act.wait_ge(unit_used, 3 * nb)
                if gain is None:
                    nc.scalar.copy(WHI[:, u % 2], WRAW[:, u]).then_inc(w_hi, 1)
                    return
                for k in range(UK):
                    g = gain[:, (u * UK + k) % gain.shape[1]:(u * UK + k) % gain.shape[1] + 1]
                    last = nc.scalar.activation(WHI[:, u % 2, k], WRAW[:, u, k], ACT.Copy, scale=g)
                last.then_inc(w_hi, 1)

            def splits(nb, gain, *us):
                for u in us:
                    split_hi(nb, u, gain)

            def copy_T(nb, tb):
                for g in range(4):
                    act.wait_ge(t_ready, 4 * tb + g + 1)
                    last = nc.scalar.copy(stageN[:, 2 * g:2 * g + 2, :],
                                          PS[:, 4 + g, :].rearrange("p (s c) -> p s c", s=2))
                    if g < 3:
                        last.then_inc(t_free, 1)
                last.then_inc(out_ready, 1)

            def square(nb, k):
                act.wait_ge(acc_free, 4 * nb + 8)
                nc.scalar.activation(bufB, stageT, ACT.Square).then_inc(sq_done, 1)

            def roots(nb, k):
                for j in range(4):
                    act.wait_ge(n_ready, 4 * k + j + 1)
                    last = nc.scalar.activation(bufA[:, j // 2, (j % 2) * HALF:(j % 2 + 1) * HALF], PS[:, 4 + j, :],
                                                ACT.Sqrt, scale=1.0 / HD, bias=eps_t[:, 0:1])
                last.then_inc(n_root, 1)

            def silu(nb, k):
                act.wait_ge(acc_free, 4 * nb + 8)
                nc.scalar.activation(stageT, stageT, ACT.Silu).then_inc(out_ready, 1)

            act.wait_ge(zeroed, 5)
            for t in range(ST):
                for q in range(4):
                    i = 4 * t + q
                    act.wait_ge(x_tr, i + 1)
                    nc.scalar.copy(XH[:, 4 * q:4 * q + 4, t * P:(t + 1) * P],
                                   PS[:, XB[i % 4], :].rearrange("p (k s) -> p k s", k=4)).then_inc(x_hi, 1)
                for ts in (() if t == ST - 2 else (t - 1, t) if t == ST - 1 else (t,)):
                    nc.scalar.activation(xin[:, ts % NX], xin[:, ts % NX], ACT.Square,
                                         accum_out=ssq[:, ts:ts + 1]).then_inc(x_sq, 1)
                if t == 2:
                    act.wait_ge(wa_sc, 3)
                    for i, w in enumerate(wcat):
                        nc.scalar.copy(w[:, :, 0:RANK], wa[:, 8 * i:8 * i + 8, :]).then_inc(wa_hi, 1)
            splits(0, g_a, 0)
            act.wait_ge(ss_pe, 1)
            for j in range(NH):
                nc.scalar.activation(RSTD[:, j * HALF:(j + 1) * HALF], PS[:, 4 + 2 * j, :], ACT.Sqrt,
                                     scale=1.0 / D, bias=eps_t[:, 0:1]).then_inc(ms_rt, 1)
            act.wait_ge(al_pe, 1)
            splits(0, g_a, 1, 2, 3)
            splits(1, g_a, 0)
            with act.Fori(1, KA0) as nb:
                splits(nb, g_a, 1, 2, 3)
                splits(nb + 1, g_a, 0)
            for nb in range(KA0, VA0):
                h = nb - KA0
                splits(nb, g_a, 1)
                if h > 0:
                    copy_T(nb - 1, h - 1)
                splits(nb, g_a, 2)
                for i in range(2):
                    act.wait_ge(l_abs, 2 * h + i + 1)
                    nc.scalar.activation(bufA[:, i], bufA[:, i], ACT.Exp).then_inc(l_log, 1)
                for i in range(2):
                    act.wait_ge(l_log, 6 * h + i + 1)
                    nc.scalar.activation(bufA[:, i], bufA[:, i], ACT.Ln, bias=ones[:, 0:1]).then_inc(l_log, 1)
                splits(nb, g_a, 3)
                for i in range(2):
                    n = 2 * h + i
                    act.wait_ge(l_cum, n + 1)
                    nc.scalar.activation(bufB[:, i], bufB[:, i], ACT.Exp, scale=1.0 / TAU).then_inc(l_exp, 1)
                    nc.scalar.activation(dc[:, n, :], bufA[:, i].rearrange("p (c s) -> p c s", s=CHUNK)[:, :, CHUNK - 1],
                                         ACT.Exp, scale=1.0 / TAU).then_inc(l_log, 1)
                splits(nb + 1, g_a, 0)
            splits(VA0, g_a, 1)
            copy_T(VA0 - 1, 3)
            splits(VA0, g_a, 2, 3)
            splits(VA0 + 1, g_a, 0)
            with act.Fori(VA0 + 1, GA0) as nb:
                splits(nb, g_a, 1)
                copy_T(nb - 1, nb - (1 + KA0))
                splits(nb, g_a, 2, 3)
                splits(nb + 1, g_a, 0)
            splits(GA0, g_a, 1)
            copy_T(GA0 - 1, GA0 - 1 - KA0)
            splits(GA0, g_a, 2, 3)
            splits(GA0 + 1, g_a, 0)
            silu(GA0, 0)
            with act.Fori(GA0 + 1, OA0 - 1) as nb:
                splits(nb, g_a, 1, 2, 3)
                splits(nb + 1, g_a, 0)
                silu(nb, nb - GA0)
            splits(OA0 - 1, g_a, 1, 2, 3)
            splits(OA0, g_o, 0)
            silu(OA0 - 1, NG_ - 1)

            def gla_qk(t, h):
                n = 4 * t + h
                act.wait_ge(qk_pe, n + 1)
                if not (isinstance(n, int) and n == 0):
                    act.wait_ge(o_pe, n)
                nc.scalar.copy(qk[0:64, :], PS[0:64, 7, 0:P])
                nc.scalar.copy(qk[64:128, CHUNK:P], PS[64:128, 7, CHUNK:P]).then_inc(qk_ok, 1)

            def gla_out(t, h):
                n = 4 * t + h
                act.wait_ge(o_pe, n + 1)
                if not isinstance(n, int) or n >= 1:
                    act.wait_ge(o_tr, n)
                nc.scalar.activation(onrm, PS[:, 4 + h % 2, :], ACT.Square,
                                     accum_out=st1[:, h:h + 1]).then_inc(o_ss, 1)
                act.wait_ge(o_ss, n + 1)
                nc.scalar.activation(st1[:, h:h + 1], st1[:, h:h + 1], ACT.Sqrt, scale=1.0 / DV,
                                     bias=eps_t[:, 0:1]).then_inc(o_rt, 1)
                act.wait_ge(o_rc, n + 1)
                nc.scalar.activation(onrm, PS[:, 4 + h % 2, :], ACT.Copy,
                                     scale=st1[:, 4 + h:5 + h]).then_inc(o_nm, 1)

            def gla_hi(t, h):
                n = 4 * t + h
                act.wait_ge(o_gt, n + 1)
                nc.scalar.copy(XH[:, 4 * h:4 * h + 4, bass.ds(t * P, P)],
                               ogate.rearrange("p (i s) -> p i s", i=4)).then_inc(o_hi, 1)

            def gla_act(t, h):
                for stage, back in ((gla_hi, 3), (gla_qk, 0), (gla_out, 1)):
                    it = gla_item(t, h, back)
                    if it:
                        stage(*it)

            act.wait_ge(g_init, 3)
            gla_steps(act, gla_act, 3)

            with act.Fori(OA0, KV0 - 1) as nb:
                splits(nb, g_o, 1, 2, 3)
                splits(nb + 1, g_o, 0)
                act.wait_ge(sum_ok, (nb - OA0) * 2 + 1)
                square(nb, nb - OA0)
                act.wait_ge(sq_done, nb - (OA0 - 1))
                nc.scalar.copy(eps_t[:, 0:1], eps_t[:, 0:1]).then_inc(out_ready, 1)
            nb = KV0 - 1

            def tiles_hi(base, nb, kts):
                for kt in kts:
                    if kt // UK < NU - 1:
                        act.wait_ge(unit_used, 3 * nb + kt // UK + 1)
                    else:
                        act.wait_ge(acc_ready, 4 * nb + 4)
                    if kt < KT - 2:
                        act.wait_ge(rel_in[kt % 2], (112 if base else 0) + 16 * (kt // 2 + 1))
                        src = reload_[:, kt % 2]
                    else:
                        src = stageT[:, kt % 2]
                    nc.scalar.copy(XH[:, kt, :], src).then_inc(r_hi, 1)

            splits(nb, g_o, 1, 2)
            tiles_hi(0, nb, range(0, 4))
            splits(nb, g_o, 3)
            tiles_hi(0, nb, range(4, 8))
            splits(KV0, g_kv, 0)
            tiles_hi(0, nb, range(8, 10))
            act.wait_ge(sum_ok, (nb - OA0) * 2 + 1)
            square(nb, nb - OA0)
            act.wait_ge(sq_done, nb - (OA0 - 1))
            nc.scalar.copy(eps_t[:, 0:1], eps_t[:, 0:1]).then_inc(out_ready, 1)
            splits(KV0, g_kv, 1)
            tiles_hi(0, nb, range(10, 16))
            splits(KV0, g_kv, 2)
            act.wait_ge(ss_pe, 2)
            for j in range(NH):
                nc.scalar.activation(RSTD[:, j * HALF:(j + 1) * HALF], PS[:, 4 + j, :], ACT.Sqrt,
                                     scale=1.0 / D, bias=eps_t[:, 0:1]).then_inc(ms_rt, 1)
            splits(KV0, g_kv, 3)
            splits(KV0 + 1, g_kv, 0)
            square(KV0, 8)
            splits(KV0 + 1, g_kv, 1, 2)
            roots(KV0, 0)
            splits(KV0 + 1, g_kv, 3)
            splits(QB0, g_b, 0)
            splits(QB0, g_b, 1)
            copy_T(KV0 + 1, NK_ + NV_)
            splits(QB0, g_b, 2, 3)
            splits(QB0 + 1, g_b, 0)
            with act.Fori(QB0 + 1, GB0 - 1) as nb:
                splits(nb, g_b, 1, 2, 3)
                splits(nb + 1, g_b, 0)

            def att_act(h, e, s):
                it = item(h, e, s, 3)
                if it:
                    _, e2, t, n = it
                    act.wait_ge(a_pv, n + 1)
                    nc.scalar.copy(aq[e2][:, t], PS[:, 7, 0:256].rearrange("p (c x) -> p c x", c=2)
                                   ).then_inc(a_oc, 1)
                it = item(h, e, s, 2)
                if it:
                    _, _, t, n = it
                    act.wait_ge(a_tr, n + 1)
                    if not (isinstance(n, int) and n == 0):
                        act.wait_ge(a_pv, n)
                    nc.scalar.copy(apt, PS[:, 6, :].rearrange("p (g r) -> p g r", g=4)).then_inc(a_cp, 1)
                it = item(h, e, s, 0)
                if it:
                    _, _, t, n = it
                    i = t % 2
                    act.wait_ge(a_nm, n + 1)
                    if not (isinstance(n, int) and n < 2):
                        act.wait_ge(a_tr, n - 1)
                    for a in range(2):
                        for c in range(2):
                            g, lo = 2 * a + c, (CHUNK if t == 0 and c == 0 else 0)
                            nc.scalar.activation(ae[:, i, g, lo:], PS[:, 4 + a, c * P + lo:(c + 1) * P], ACT.Exp,
                                                 scale=st2[:, i, 1, g:g + 1], bias=st2[:, i, 4, g:g + 1],
                                                 accum_out=st2[:, i, 6, g:g + 1])
                    nc.scalar.activation(st2[:, i, 5], st2[:, i, 5], ACT.Exp).then_inc(a_ex, 1)

            def g_block(nb, h, e, last=False):
                for u in range(NU):
                    if u < NU - 1:
                        splits(nb, g_b, u + 1)
                    else:
                        splits(nb + 1, None if last else g_b, 0)
                    for i in range(2):
                        att_act(h, e, 2 * u + i)
                        if last and 0 < u and 2 * u + i < 7:
                            tiles_hi(KT, nb, range(UK * (u - 1) + 2 * i, UK * (u - 1) + 2 * i + 2))
                act.wait_ge(acc_free, 4 * nb + 8)
                nc.scalar.activation(stageT, stageT, ACT.Silu).then_inc(silu_b, 1)

            splits(GB0 - 1, g_b, 1, 2, 3)
            for i in range(2):
                att_act(-1, 1, 4 + i)
            splits(GB0, g_b, 0)
            for i in range(2):
                att_act(-1, 1, 6 + i)
            with act.Fori(0, KVH - 1) as h:
                for e in range(2):
                    g_block(2 * h + (GB0 + e), h, e)
            g_block(OB0 - 2, KVH - 1, 0)
            g_block(OB0 - 1, KVH - 1, 1, last=True)
            splits(OB0, None, 1)
            tiles_hi(KT, OB0 - 1, range(10, 14))
            act.wait_ge(out_ready, OB0)
            tiles_hi(KT, OB0 - 1, range(14, 16))
            splits(OB0, None, 2, 3)
            splits(OB0 + 1, None, 0)
            with act.Fori(OB0 + 1, END - 1) as nb:
                splits(nb, None, 1)
                copy_T(nb - 1, nb - (1 + OB0) + NK_ + NV_ + 1)
                splits(nb, None, 2, 3)
                splits(nb + 1, None, 0)
            splits(END - 1, None, 1)
            copy_T(END - 2, END - 2 - OB0 + NK_ + NV_ + 1)
            splits(END - 1, None, 2, 3)
            copy_T(END - 1, END_T)

        @block.vector
        def _(dve):
            def split_lo(nb, u, gain):
                dve.wait_ge(w_hi, NU * nb + u + 1)
                hi = WHI[:, u % 2].bitcast(F32)
                if gain is None:
                    nc.vector.tensor_tensor(WLO[:, u % 2], WRAW[:, u], hi, ALU.subtract).then_inc(w_lo, 1)
                    return
                for k in range(UK):
                    g = gain[:, (u * UK + k) % gain.shape[1]:(u * UK + k) % gain.shape[1] + 1]
                    last = nc.vector.scalar_tensor_tensor(WLO[:, u % 2, k], WRAW[:, u, k], g, hi[:, k],
                                                          ALU.mult, ALU.subtract)
                last.then_inc(w_lo, 1)

            def splits(nb, gain, *us):
                for u in us:
                    split_lo(nb, u, gain)

            def evac(nb, scale=None, factor=None, add=None, final=False, chunked=False, banks=range(4)):
                if 0 in banks and not (isinstance(nb, int) and nb == 0):
                    dve.wait_ge(stored, 16 * nb)
                for j in banks:
                    ct, cols = j // NH, slice((j % NH) * HALF, (j % NH + 1) * HALF)
                    dve.wait_ge(acc_ready, 4 * nb + j + 1)
                    dst, src = stageT[:, ct, cols], PS[:, j, :]
                    if add is not None:
                        i = nc.vector.tensor_tensor(dst, src, add[:, ct, cols], ALU.add)
                    elif factor is not None:
                        i = nc.vector.tensor_tensor(dst, src, factor[:, ct, cols], ALU.mult)
                    elif scale is not None:
                        i = nc.vector.scalar_tensor_tensor(dst, src, scale, RSTD[:, cols], ALU.mult, ALU.mult)
                    elif chunked:
                        i = nc.vector.tensor_tensor(stageX[:, 8 * (j % NH):8 * (j % NH) + 8, ct],
                                                    src.rearrange("p (x s) -> p x s", s=CHUNK),
                                                    RSTD[:, cols].rearrange("p (x s) -> p x s", s=CHUNK), ALU.mult)
                    else:
                        i = nc.vector.tensor_tensor(dst, src, RSTD[:, cols], ALU.mult)
                    i.then_inc(acc_free, 1)
                if final:
                    dve.wait_ge(acc_free, 4 * nb + 8)
                    nc.vector.tensor_copy(st1[:, 0:1], eps_t[:, 0:1]).then_inc(out_ready, 1)

            def head_norm(k, gain):
                dve.wait_ge(n_root, k + 1)
                nc.vector.reciprocal(bufA, bufA).then_inc(n_dve, 1)
                dve.wait_ge(n_dve, k + 1)
                for i in range(CT):
                    last = nc.vector.scalar_tensor_tensor(stageT[:, i], stageT[:, i], gain, bufA[:, i],
                                                          ALU.mult, ALU.mult)
                last.then_inc(out_ready, 1)

            nc.vector.memset(WHI[:, 1].bitcast(F32), 0.0)
            nc.vector.memset(WLO[:, 1].bitcast(F32), 0.0).then_inc(acc_free, 4)
            dve.wait_ge(acc_free, 4)

            def constants():
                dve.wait_ge(v_pe, 2)
                nc.vector.tensor_copy(vcols[:, :], PS[:, 1, 0:NR]).then_inc(v_ok, 1)
                for half in range(2):
                    rows = slice(half * HD, (half + 1) * HD)
                    heads = PS[rows, 1, 256:256 + KVH * 8].rearrange("p (b i a) -> p i b a", i=2, a=2)[:, half]
                    nc.vector.tensor_copy(sinks[rows].rearrange("p b (a c) -> p b a c", a=2),
                                          heads.unsqueeze(3).to_broadcast([HD, D // BC, 2, 2])).then_inc(v_ok, 1)
                dve.wait_ge(v_ok, 3)
                nc.vector.tensor_tensor(wa[:, :, :], wa[:, :, :], g_a.unsqueeze(2).to_broadcast([P, KT, RANK]),
                                        ALU.mult).then_inc(wa_sc, 1)
                nc.vector.tensor_scalar(nsinks[:, :, :], sinks[:, :, :], -1.0, None, ALU.mult).then_inc(wa_sc, 1)
                nc.vector.scalar_tensor_tensor(kgain[:, 0:1], vcols[:, NR - 2:NR - 1], HD ** -0.5,
                                               vcols[:, NR - 1:NR], ALU.mult, ALU.mult).then_inc(wa_sc, 1)

            for i in range(4 * ST):
                t, q = i // 4, i % 4
                if i == 8:
                    constants()
                if i == 16:
                    dve.wait_ge(wa_hi, 2)
                    for j, w in enumerate(wcat):
                        last = nc.vector.tensor_tensor(w[:, :, 32:32 + RANK], wa[:, 8 * j:8 * j + 8, :],
                                                       w[:, :, 0:RANK].bitcast(F32), ALU.subtract)
                    last.then_inc(wa_lo, 1)
                dve.wait_ge(x_hi, i + 1)
                dst = (slice(None), slice(4 * q, 4 * q + 4), slice(t * P, (t + 1) * P))
                nc.vector.tensor_tensor(XL[dst], PS[:, XB[i % 4], :].rearrange("p (k s) -> p k s", k=4),
                                        XH[dst].bitcast(F32), ALU.subtract).then_inc(x_lo, 1)
            splits(0, g_a, 0)
            splits(0, g_a, 1)
            for j in range(NH):
                dve.wait_ge(ms_rt, j + 1)
                nc.vector.reciprocal(RSTD[:, j * HALF:(j + 1) * HALF], RSTD[:, j * HALF:(j + 1) * HALF]
                                     ).then_inc(rstd_ok, 1)
            dve.wait_ge(rstd_ok, NH)
            dve.wait_ge(al_pe, 1)
            nc.vector.memset(wup, 0.0).then_inc(al_ok, 1)
            for j in range(NH):
                last = nc.vector.tensor_tensor(alow[:, j * HALF:(j + 1) * HALF], PS[0:64, 7 - 2 * j, :],
                                               RSTD[0:64, j * HALF:(j + 1) * HALF], ALU.mult)
            last.then_inc(al_ok, 1)
            splits(0, g_a, 2, 3)
            splits(1, g_a, 0)
            evac(0, scale=DK ** -0.5, final=True)
            with dve.Fori(1, KA0) as nb:
                splits(nb, g_a, 1, 2, 3)
                splits(nb + 1, g_a, 0)
                evac(nb, scale=DK ** -0.5, final=True)
            for i in range(4):
                dve.wait_ge(x_st[i], 16 * KT // 4)
            for nb in range(KA0, VA0):
                h = nb - KA0
                dve.wait_ge(l_ready, 2 * h + 2)
                dve.wait_ge(acc_free, 4 * nb + 4)
                for i in range(2):
                    for j in range(NH):
                        last = nc.vector.tensor_scalar(bufB[:, i, j * HALF:(j + 1) * HALF], PS[:, 4 + 2 * i + j, :],
                                                       b_al[:, 2 * h + i:2 * h + i + 1], None, ALU.add)
                last.then_inc(l_add, 1)
                splits(nb, g_a, 1)
                dve.wait_ge(l_add, h + 1)
                if h > 0:
                    dve.wait_ge(t_ready, 4 * h)
                for i in range(2):
                    z, e = bufB[:, i], bufA[:, i]
                    nc.vector.scalar_tensor_tensor(e, z, -1.0, z, ALU.mult, ALU.min).then_inc(l_abs, 1)
                splits(nb, g_a, 2)
                for i in range(2):
                    n = 2 * h + i
                    z, e = bufB[:, i], bufA[:, i]
                    dve.wait_ge(l_log, 6 * h + 3 + i)
                    nc.vector.scalar_tensor_tensor(z, z, 0.0, e, ALU.min, ALU.subtract).then_inc(l_dve, 1)
                    dve.wait_ge(l_dve, 2 * n + 1)
                    for c in range(SEQ // CHUNK):
                        cs = slice(c * CHUNK, (c + 1) * CHUNK)
                        last = nc.vector.tensor_tensor_scan(e[:, cs], ones[:, 0:CHUNK], z[:, cs], 0.0,
                                                            ALU.mult, ALU.add)
                    last.then_inc(l_dve, 1)
                    dve.wait_ge(l_dve, 2 * n + 2)
                    ev = e.rearrange("p (c s) -> p c s", s=CHUNK)
                    nc.vector.tensor_tensor(z.rearrange("p (c s) -> p c s", s=CHUNK),
                                            ev[:, :, CHUNK - 1:CHUNK].to_broadcast([P, SEQ // CHUNK, CHUNK]), ev,
                                            ALU.subtract).then_inc(l_cum, 1)
                splits(nb, g_a, 3)
                for i in range(2):
                    z = bufB[:, i]
                    dve.wait_ge(l_exp, 2 * h + i + 1)
                    nc.vector.tensor_tensor(z, z, RSTD[:, :], ALU.mult).then_inc(l_ok, 1)
                splits(nb + 1, g_a, 0)
                dve.wait_ge(l_ok, 2 * h + 2)
                if h > 0:
                    dve.wait_ge(kt_st, 16 * h)
                evac(nb, factor=bufB)
            dve.wait_ge(kt_st, 16 * GH)
            with dve.Fori(VA0, GA0) as nb:
                splits(nb, g_a, 1, 2, 3)
                splits(nb + 1, g_a, 0)
                evac(nb)
            with dve.Fori(GA0, OA0 - 1) as nb:
                splits(nb, g_a, 1, 2, 3)
                splits(nb + 1, g_a, 0)
                evac(nb)
            splits(OA0 - 1, g_a, 1, 2, 3)
            splits(OA0, g_o, 0)
            nc.vector.memset(qk[64:128, 0:CHUNK], 0.0).then_inc(g_init, 1)
            dt = dc[:, :, :].rearrange("p n (t c) -> p n t c", c=2)
            nc.vector.tensor_copy(dcum[:, :, :, 0], dt[:, :, :, 0]).then_inc(g_init, 1)
            nc.vector.tensor_tensor(dcum[:, :, :, 1], dt[:, :, :, 0], dt[:, :, :, 1], ALU.mult).then_inc(g_init, 1)
            evac(OA0 - 1)
            dve.wait_ge(g_init, 3)

            def gla_update(t, h):
                n = 4 * t + h
                dve.wait_ge(kv_pe, n + 1)
                first = isinstance(t, int) and t == 0
                if first and h == 0:
                    dve.wait_ge(stored, 16 * OA0)
                if not first:
                    dve.wait_ge(o_pe, n + 1)
                    dve.wait_ge(st_up, n - 3)
                for k in range(2):
                    kv = PS[:, 2 * (h % 2) + k, :]
                    if first:
                        last = nc.vector.tensor_copy(state[:, h, k], kv)
                    else:
                        last = nc.vector.scalar_tensor_tensor(
                            state[:, h, k], state[:, h, k],
                            dcum[:, 2 * h + k, bass.ds(t, 1), 1], kv, ALU.mult, ALU.add)
                last.then_inc(st_up, 1)

            def gla_recip(t, h):
                dve.wait_ge(o_rt, 4 * t + h + 1)
                nc.vector.reciprocal(st1[:, 4 + h:5 + h], st1[:, h:h + 1]).then_inc(o_rc, 1)

            def gla_gate(t, h):
                n = 4 * t + h
                dve.wait_ge(o_tr, n + 1)
                dve.wait_ge(gg_in[h % 2], 16 * (2 * t + h // 2 + 1))
                if not isinstance(n, int) or n >= 1:
                    dve.wait_ge(o_lo, n)
                nc.vector.tensor_tensor(ogate, PS[:, 6, :], gg[:, h % 2].rearrange("p i s -> p (i s)"),
                                        ALU.mult).then_inc(o_gt, 1)

            def gla_lo(t, h):
                n = 4 * t + h
                dve.wait_ge(o_hi, n + 1)
                dst = (slice(None), slice(4 * h, 4 * h + 4), bass.ds(t * P, P))
                nc.vector.tensor_tensor(XL[dst], ogate.rearrange("p (i s) -> p i s", i=4), XH[dst].bitcast(F32),
                                        ALU.subtract).then_inc(o_lo, 1)

            def gla_dve(t, h):
                for stage, back in ((gla_lo, 3), (gla_update, 1), (gla_recip, 1), (gla_gate, 2)):
                    it = gla_item(t, h, back)
                    if it:
                        stage(*it)

            gla_steps(dve, gla_dve, 3)

            def evac_res(nb, k, final=False):
                dve.wait_ge(res_in, 16 * (k + 1))
                evac(nb, add=bufA, final=final)

            with dve.Fori(OA0, KV0 - 1) as nb:
                splits(nb, g_o, 1, 2, 3)
                splits(nb + 1, g_o, 0)
                evac_res(nb, nb - OA0)

            def tiles_lo(base, kts):
                for kt in kts:
                    dve.wait_ge(r_hi, base + kt + 1)
                    src = reload_[:, kt % 2] if kt < KT - 2 else stageT[:, kt % 2]
                    nc.vector.tensor_tensor(XL[:, kt, :], src, XH[:, kt, :].bitcast(F32), ALU.subtract
                                            ).then_inc(r_lo, 1)

            splits(KV0 - 1, g_o, 1, 2)
            tiles_lo(0, range(0, 4))
            splits(KV0 - 1, g_o, 3)
            tiles_lo(0, range(4, 8))
            splits(KV0, g_kv, 0)
            tiles_lo(0, range(8, 10))
            evac_res(KV0 - 1, 7)
            splits(KV0, g_kv, 1)
            tiles_lo(0, range(10, 16))
            splits(KV0, g_kv, 2)
            for j in range(NH):
                dve.wait_ge(ms_rt, NH + j + 1)
                nc.vector.reciprocal(RSTD[:, j * HALF:(j + 1) * HALF], RSTD[:, j * HALF:(j + 1) * HALF]
                                     ).then_inc(rstd_ok, 1)
            dve.wait_ge(rstd_ok, 2 * NH)
            splits(KV0, g_kv, 3)
            splits(KV0 + 1, g_kv, 0)
            evac(KV0)
            splits(KV0 + 1, g_kv, 1, 2)
            head_norm(0, kgain[:, 0:1])
            splits(KV0 + 1, g_kv, 3)
            splits(QB0, g_b, 0)
            evac(KV0 + 1)
            splits(QB0, g_b, 1, 2, 3)
            splits(QB0 + 1, g_b, 0)
            evac(QB0, chunked=True, final=True)
            with dve.Fori(QB0 + 1, GB0 - 1) as nb:
                splits(nb, g_b, 1, 2, 3)
                splits(nb + 1, g_b, 0)
                evac(nb, chunked=True, final=True)

            def denominator(h, e, s):
                it = item(h, e, s, 1)
                if it:
                    _, _, t, n = it
                    i = t % 2
                    dve.wait_ge(a_ex, n + 1)
                    nc.vector.tensor_tensor(st2[:, i, 6], st2[:, i, 6], st2[:, i, 5], ALU.add).then_inc(a_sm, 1)
                    dve.wait_ge(a_sm, n + 1)
                    nc.vector.reciprocal(st2[:, i, 7], st2[:, i, 6]).then_inc(a_rc, 1)

            def maximum(h, e, s):
                it = item(h, e, s, 0)
                if not it:
                    return
                hh, ee, t, n = it
                i = t % 2
                m, rq, mx, mr, nm, sd = (st2[:, i, k] for k in range(6))
                dve.wait_ge(a_pe, n + 1)
                if not (isinstance(n, int) and n < 2):
                    dve.wait_ge(a_pr, n - 1)
                nc.vector.tensor_scalar(m.rearrange("p (a c) -> p c a", a=2),
                                        PS[:, 5, 256:260].rearrange("p (c a) -> p c a", c=2), 1.0 / HD, EPS,
                                        ALU.mult, ALU.add).then_inc(a_ms, 1)
                sc = PS[:, 4:6, 0:256].rearrange("p a (c k) -> p a c k", c=2)
                if t == 0:
                    for c in range(2):
                        last = nc.vector.tensor_reduce(mx.rearrange("p (a c) -> p a c", a=2)[:, :, c],
                                                       sc[:, :, c, CHUNK * (1 - c):], AX.X, ALU.max)
                else:
                    last = nc.vector.tensor_reduce(mx.rearrange("p (a c) -> p a c", a=2), sc, AX.X, ALU.max)
                last.then_inc(a_mx, 1)
                dve.wait_ge(a_mx, 3 * n + 1)
                dve.wait_ge(a_rq, n + 1)
                nc.vector.tensor_tensor(mr, mx, rq, ALU.mult).then_inc(a_mx, 1)
                dve.wait_ge(a_mx, 3 * n + 2)
                b = bass.ds(2 * hh + ee, 1)
                nc.vector.scalar_tensor_tensor(nm, mr, -1.0, nsinks[:, b].rearrange("p o g -> p (o g)"),
                                               ALU.mult, ALU.min).then_inc(a_mx, 1)
                dve.wait_ge(a_mx, 3 * n + 3)
                nc.vector.tensor_tensor(sd, nm, sinks[:, b].rearrange("p o g -> p (o g)"), ALU.add).then_inc(a_nm, 1)

            def att_dve(h, e, s):
                denominator(h, e, s)
                maximum(h, e, s)

            def gate(nb, b, e):
                dve.wait_ge(silu_b, nb - (GB0 - 1))
                dve.wait_ge(a_oc, 8 * b + 8)
                for ct in range(CT):
                    g = stageT[:, ct].rearrange("p (t c s) -> p t c s", c=2, s=CHUNK)
                    o = aq[e].rearrange("p t c (i s) -> p i t c s", i=CT)[:, ct]
                    last = nc.vector.tensor_tensor(g, g, o, ALU.mult)
                last.then_inc(out_ready, 1)

            def g_block(nb, h, e, first=False, last=False):
                for u in range(NU):
                    denominator(h, e, 2 * u)
                    if u == 0:
                        maximum(h, e, 0)
                    if u < NU - 1:
                        splits(nb, g_b, u + 1)
                    else:
                        splits(nb + 1, None if last else g_b, 0)
                    for i in range(2):
                        if i == 1:
                            denominator(h, e, 2 * u + 1)
                        if u == NU - 1:
                            evac(nb, banks=(2 * i, 2 * i + 1))
                        if u + i > 0:
                            maximum(h, e, 2 * u + i)
                        if u == 0 and i == 0 and not first:
                            gate(nb - 1, 2 * h + e - 1, 1 - e)
                        if last and 0 < u and 2 * u + i < 7:
                            tiles_lo(KT, range(UK * (u - 1) + 2 * i, UK * (u - 1) + 2 * i + 2))

            splits(GB0 - 1, g_b, 1, 2, 3)
            for i in range(2):
                att_dve(-1, 1, 4 + i)
            splits(GB0, g_b, 0)
            for i in range(2):
                evac(GB0 - 1, chunked=True, banks=(2 * i, 2 * i + 1), final=i == 1)
                att_dve(-1, 1, 6 + i)
            for e in range(2):
                g_block(GB0 + e, 0, e, first=e == 0)
            with dve.Fori(1, KVH - 1) as h:
                for e in range(2):
                    g_block(2 * h + (GB0 + e), h, e)
            g_block(OB0 - 2, KVH - 1, 0)
            g_block(OB0 - 1, KVH - 1, 1, last=True)
            gate(OB0 - 1, D // BC - 1, 1)
            splits(OB0, None, 1)
            tiles_lo(KT, range(10, 16))

            splits(OB0, None, 2, 3)
            splits(OB0 + 1, None, 0)
            evac_res(OB0, 8)
            with dve.Fori(OB0 + 1, END - 1) as nb:
                splits(nb, None, 1, 2, 3)
                splits(nb + 1, None, 0)
                evac_res(nb, nb - OB0 + 8)
            splits(END - 1, None, 1, 2, 3)
            evac_res(END - 1, 15)

        @block.tensor
        def _(pe):
            def unit(nb, u, ready=None, beside=None):
                pe.wait_ge(w_lo, NU * nb + u + 1)
                if ready is not None:
                    pe.wait_ge(*ready)
                for j in range(4):
                    ct, cols = j // NH, slice((j % NH) * HALF, (j % NH + 1) * HALF)
                    if u == 0:
                        pe.wait_ge(acc_free, 4 * nb + j + 1)
                    for k in range(UK):
                        kt = UK * u + k
                        hi, lo = (w[:, u % 2, k, ct * P:(ct + 1) * P] for w in (WHI, WLO))
                        nc.tensor.matmul(PS[:, j, :], hi, XH[:, kt, cols], start=kt == 0, stop=False)
                        nc.tensor.matmul(PS[:, j, :], hi, XL[:, kt, cols], start=False, stop=False)
                        last = nc.tensor.matmul(PS[:, j, :], lo, XH[:, kt, cols], start=False, stop=kt == KT - 1)
                    if u == NU - 1:
                        last.then_inc(acc_ready, 1)
                    elif j == 3:
                        last.then_inc(unit_used, 1)
                    if beside is not None and j % 2:
                        beside(2 * u + j // 2)

            def units(nb, *us):
                for u in us:
                    unit(nb, u)

            def transposes(nb, tb, src=stageT):
                pe.wait_ge(acc_free, 4 * nb + 8)
                for g in range(4):
                    for s in range(2):
                        for ct in range(CT):
                            st = 2 * g + s
                            last = nc.tensor.transpose(PS[:, 4 + g, (2 * s + ct) * P:(2 * s + ct + 1) * P],
                                                       src[:, ct, st * P:(st + 1) * P], ident[:, :])
                    last.then_inc(t_ready, 1)

            def head_sums(k, sq_count):
                pe.wait_ge(sq_done, sq_count)
                pe.wait_ge(pair_ok, 3)
                for j in range(4):
                    nc.tensor.matmul(PS[:, 4 + j, :], pair[:, :],
                                     bufB[:, j // NH, (j % NH) * HALF:(j % NH + 1) * HALF],
                                     start=True, stop=True).then_inc(n_ready, 1)

            pe.wait_ge(zeroed, 5)

            def gate_rank(j):
                pe.wait_ge(x_lo, 16 * (j + 1))
                cols = slice(j * HALF, (j + 1) * HALF)
                for kt in range(KT):
                    w = wcat[kt // 8][:, kt % 8, :]
                    nc.tensor.matmul(PS[:, 7 - 2 * j, :], w, XH[:, kt, cols], start=kt == 0, stop=False)
                    last = nc.tensor.matmul(PS[:, 7 - 2 * j, :], w, XL[:, kt, cols], start=False, stop=kt == KT - 1)
                return last

            for t in range(ST):
                for q in range(4):
                    i = 4 * t + q
                    pe.wait_ge(x_in[t % NX], 16 * (t // NX + 1))
                    if i >= 4:
                        pe.wait_ge(x_lo, i - 3)
                    for k in range(4):
                        last = nc.tensor.transpose(PS[:, XB[i % 4], k * P:(k + 1) * P],
                                                   xin[:, t % NX, (4 * q + k) * P:(4 * q + k + 1) * P], ident[:, :])
                    last.then_inc(x_tr, 1)
                if t == 1:
                    pe.wait_ge(consts_in, 16 * NCONST)
                    nc.tensor.transpose(PS[:, 1, 0:NR], vrows[:, :], ident[0:NR, 0:NR]).then_inc(v_pe, 1)
                    nc.tensor.matmul(PS[:, 1, 256:256 + KVH * 8], ones[0:1, :], srow[:, :], start=True, stop=True
                                     ).then_inc(v_pe, 1)
                if t == 5:
                    pe.wait_ge(wa_lo, 1)
                    gate_rank(0)
            gate_rank(1).then_inc(al_pe, 1)
            for t in range(ST):
                pe.wait_ge(x_sq, t + 1)
                last = nc.tensor.matmul(PS[:, 4 + 2 * (t // 4), (t % 4) * P:(t % 4 + 1) * P],
                                        ssq[:, t:t + 1].to_broadcast([P, P]), ident[:, :], start=True, stop=True)
            last.then_inc(ss_pe, 1)

            pe.wait_ge(v_ok, 3)
            with pe.Fori(0, KA0) as nb:
                units(nb, 0, 1, 2, 3)
            def logits(h):
                pe.wait_ge(up_in, 32 * (h + 1))
                if h == 0:
                    pe.wait_ge(al_ok, 2)
                else:
                    pe.wait_ge(l_add, h)
                if h > 1:
                    pe.wait_ge(out_ready, KA0 + h - 1)
                for i in range(2):
                    for j in range(NH):
                        last = nc.tensor.matmul(PS[:, 4 + 2 * i + j, :], wup[:, i * P:(i + 1) * P],
                                                alow[:, j * HALF:(j + 1) * HALF], start=True, stop=True)
                    last.then_inc(l_ready, 1)

            logits(0)
            for nb in range(KA0, VA0):
                h = nb - KA0
                units(nb, 0)
                if h > 0:
                    pe.wait_ge(l_add, h + 1)
                    pe.wait_ge(k2_ok, h)
                    transposes(nb - 1, h - 1, bufA)
                units(nb, 1, 2)
                if h < GH - 1:
                    logits(h + 1)
                units(nb, 3)
            units(VA0, 0)
            pe.wait_ge(k2_ok, GH)
            transposes(VA0 - 1, 3, bufA)
            units(VA0, 1, 2, 3)
            with pe.Fori(VA0 + 1, GA0 + 1) as nb:
                units(nb, 0)
                transposes(nb - 1, nb - (1 + KA0))
                units(nb, 1, 2, 3)
            with pe.Fori(GA0 + 1, OA0) as nb:
                units(nb, 0, 1, 2, 3)

            def gla_qk(t, h):
                n = 4 * t + h
                pe.wait_ge(qkv_in[h], 64 * t + 64)
                pe.wait_ge(gs_ok, n + 1)
                if not (isinstance(n, int) and n == 0):
                    pe.wait_ge(qk_ok, n)
                for k in range(2):
                    nc.tensor.matmul(PS[0:CHUNK, 7, 0:P], gkt[:, h, k, 0:CHUNK], qc[:, h % 2, k],
                                     start=k == 0, stop=k == 1)
                for k in range(2):
                    last = nc.tensor.matmul(PS[CHUNK:P, 7, CHUNK:P], gkt[:, h, k, CHUNK:P], gq[:, h, k, CHUNK:P],
                                            start=k == 0, stop=k == 1)
                last.then_inc(qk_pe, 1)

            def gla_o(t, h):
                n = 4 * t + h
                first = isinstance(t, int) and t == 0
                pe.wait_ge(qk_ok, n + 1)
                if not first:
                    pe.wait_ge(st_up, n - 3)
                if not (isinstance(n, int) and n < 2):
                    pe.wait_ge(o_nm, n - 1)
                for k in range(0 if first else 2):
                    nc.tensor.matmul(PS[:, 4 + h % 2, :], qs[:, h % 2, k], state[:, h, k], start=k == 0, stop=False)
                nc.tensor.matmul(PS[:, 4 + h % 2, :], qk[:, :], gv[:, h, :], start=first, stop=True
                                 ).then_inc(o_pe, 1)

            def gla_kv(t, h):
                n = 4 * t + h
                pe.wait_ge(qkv_in[h], 64 * t + 64)
                if isinstance(n, int) and n < 2:
                    pe.wait_ge(acc_free, 4 * OA0 + 4)
                else:
                    pe.wait_ge(st_up, n - 1)
                for k in range(2):
                    last = nc.tensor.matmul(PS[:, 2 * (h % 2) + k, :], gk[:, h, k * P:(k + 1) * P], gv[:, h, :],
                                            start=True, stop=True)
                last.then_inc(kv_pe, 1)

            def gla_tr(t, h):
                n = 4 * t + h
                pe.wait_ge(o_nm, n + 1)
                if not isinstance(n, int) or n >= 1:
                    pe.wait_ge(o_gt, n)
                for k in range(4):
                    last = nc.tensor.transpose(PS[:, 6, k * P:(k + 1) * P], onrm[:, k * P:(k + 1) * P], ident[:, :])
                last.then_inc(o_tr, 1)

            def gla_pe(t, h):
                stages = ((gla_qk, 0), (gla_o, 1), (gla_kv, 0), (gla_tr, 2))
                if isinstance(t, int) and (t, h) == (0, 0):
                    stages = ((gla_kv, 0), (gla_qk, 0))
                for stage, back in stages:
                    it = gla_item(t, h, back)
                    if it:
                        stage(*it)

            gla_steps(pe, gla_pe, 1)

            def last_tile(s):
                if s == 0:
                    gla_pe(ST, 1)

            for u in range(NU):
                unit(OA0, u, ready=(o_lo, 4 * (ST - 1) + u + 1), beside=last_tile if u == 0 else None)
            with pe.Fori(OA0 + 1, KV0) as nb:
                units(nb, 0, 1, 2, 3)
            unit(KV0, 0, ready=(r_lo, 4))
            unit(KV0, 1, ready=(r_lo, 8))
            pe.wait_ge(sum_ok, 2 * (D // BC) + 1)
            for j in range(NH):
                last = nc.tensor.matmul(PS[:, 4 + j, :], ones[:, :], sqsum[:, j * HALF:(j + 1) * HALF],
                                        start=True, stop=True)
            last.then_inc(ss_pe, 1)
            unit(KV0, 2, ready=(r_lo, 12))
            unit(KV0, 3, ready=(r_lo, 16))
            units(KV0 + 1, 0)
            head_sums(0, D // BC + 1)
            units(KV0 + 1, 1, 2, 3)
            units(QB0, 0)
            transposes(KV0 + 1, 12)
            units(QB0, 1, 2, 3)
            with pe.Fori(QB0 + 1, GB0 - 1) as nb:
                units(nb, 0, 1, 2, 3)

            def att_pe(h, e, s):
                it = item(h, e, s, 0)
                if it:
                    hh, ee, t, n = it
                    pe.wait_ge(q_in[ee], 16 * hh + 16)
                    pe.wait_ge(k_in[0], 32 * hh + 32)
                    if t >= 4:
                        pe.wait_ge(k_in[1], 32 * hh + 32)
                    pe.wait_ge(a_q2, n + 1)
                    if not (isinstance(n, int) and n == 0):
                        pe.wait_ge(a_ex, n)
                    for a in range(2):
                        rows = slice(a * HD, (a + 1) * HD)
                        for c in range(2):
                            x, lo = 2 * t + c, (CHUNK if t == 0 and c == 0 else 0)
                            nc.tensor.matmul(PS[:, 4 + a, c * P + lo:(c + 1) * P], aq[ee][rows, t, c],
                                             ak[rows, (x - 1) * CHUNK + lo:(x + 1) * CHUNK], start=True, stop=True)
                    for c in range(2):
                        last = nc.tensor.matmul(PS[:, 5, 256 + 2 * c:258 + 2 * c], aq2[:, t % 2, c],
                                                pair[:, 0:P:HD], start=True, stop=True)
                    last.then_inc(a_pe, 1)
                it = item(h, e, s, 3)
                if it:
                    hh, _, t, n = it
                    pe.wait_ge(a_cp, n + 1)
                    pe.wait_ge(va_in[0], 48 * hh + 48)
                    if t == 0:
                        pe.wait_ge(a_vz, 1)
                    if t >= 4:
                        pe.wait_ge(va_in[1], 32 * hh + 32)
                    if not (isinstance(n, int) and n == 0):
                        pe.wait_ge(a_oc, n)
                    for a in range(2):
                        for c in range(2):
                            last = nc.tensor.matmul(PS[a * HD:(a + 1) * HD, 7, c * P:(c + 1) * P], av[:, c, t],
                                                    apt[:, 2 * a + c], start=True, stop=True)
                    last.then_inc(a_pv, 1)
                it = item(h, e, s, 2)
                if it:
                    _, _, t, n = it
                    pe.wait_ge(a_pr, n + 1)
                    if not (isinstance(n, int) and n == 0):
                        pe.wait_ge(a_cp, n)
                    for g in range(4):
                        last = nc.tensor.transpose(PS[:, 6, g * P:(g + 1) * P], ae[:, t % 2, g], ident[:, :])
                    last.then_inc(a_tr, 1)

            def beside(h, e):
                return lambda s: att_pe(h, e, s)

            units(GB0 - 1, 0, 1)
            for u in (2, 3):
                unit(GB0 - 1, u, beside=beside(-1, 1))
            with pe.Fori(0, KVH - 1) as h:
                for e in range(2):
                    for u in range(NU):
                        unit(2 * h + (GB0 + e), u, beside=beside(h, e))
            for e in range(2):
                for u in range(NU):
                    unit(OB0 - 2 + e, u, beside=beside(KVH - 1, e))

            for u in range(NU):
                unit(OB0, u, ready=(r_lo, KT + UK * (u + 1)))
            with pe.Fori(OB0 + 1, END) as nb:
                units(nb, 0)
                transposes(nb - 1, nb)
                units(nb, 1, 2, 3)
            transposes(END - 1, END)


_INS = ['x', 'a_norm', 'a_w_in', 'a_w_alpha_up', 'a_b_alpha', 'a_out_norm', 'a_w_out', 'kv_norm', 'w_kv', 'k_norm',
        'b_norm', 'b_w_in', 'b_q_norm', 'b_sinks', 'b_w_out']


def kernel(**inputs):
    import numpy as _np
    import concourse.bacc as _bacc
    from concourse import mybir as _mybir
    from concourse.bass_utils import run_bass_kernel_spmd as _run

    nc = _bacc.Bacc("TRN2", target_bir_lowering=False, num_devices=1)
    arrays, args = {}, []
    for name in _INS:
        a = _np.ascontiguousarray(inputs[name])
        arrays[f"in_{name}_dram"] = a
        args.append(nc.dram_tensor(f"in_{name}_dram", a.shape, _mybir.dt.from_np(a.dtype), kind="ExternalInput").ap())
    shape = _np.asarray(inputs['x']).shape
    args.append(nc.dram_tensor("out_0_dram", shape, _mybir.dt.float32, kind="ExternalOutput").ap())
    trunk_kernel(nc, *args)
    r = _run(nc, [arrays], core_ids=[0])
    return r.results[0]["out_0_dram"]
```
